# Optimizing a Trainium2 kernel written in Bass

```python
import math
import jax
import jax.numpy as jnp
from jax import lax
import numpy as np
import jax, jax.numpy as jnp

D_MODEL = 1024
BATCH = 1
SEQ = 1024
DEPTH = 2

CTX_LEN = 256
GRID_W = 64
HEAD_DIM = 64
ROPE_BASE = 10000.0
EPS = 1e-6
NEG_INF = -1e30
ATTN_SCALE = HEAD_DIM ** -0.5
Q_BLOCK = 128
N_EVEN = (DEPTH + 1) // 2
N_ODD = DEPTH // 2

A_HEADS = 8
A_KV_HEADS = 2
A_GROUP = A_HEADS // A_KV_HEADS
WINDOW = 128
A_WIDTH = A_HEADS * HEAD_DIM
B_HEADS = 4
B_VDIM = 2 * HEAD_DIM
B_WIDTH = B_HEADS * B_VDIM
EVEN_SPLITS = (A_WIDTH, A_KV_HEADS * HEAD_DIM, A_KV_HEADS * HEAD_DIM, A_WIDTH,
               B_HEADS * 2 * HEAD_DIM, B_HEADS * 2 * HEAD_DIM, B_WIDTH, B_WIDTH)
EVEN_IN = sum(EVEN_SPLITS)

G_HEADS = 4
G_DK = (D_MODEL // 2) // G_HEADS
G_DV = D_MODEL // G_HEADS
G_RANK = 16
G_TAU = 16.0
G_CHUNK = 64
ODD_SPLITS = (G_HEADS * G_DK, G_HEADS * G_DK, G_HEADS * G_DV, G_HEADS * G_DV, G_RANK, G_RANK)
ODD_IN = sum(ODD_SPLITS)


def rms_norm(x, g):
    xf = x.astype(jnp.float32)
    y = xf * lax.rsqrt(jnp.mean(xf * xf, axis=-1, keepdims=True) + EPS)
    return (y * g.astype(jnp.float32)).astype(x.dtype)

def split_cols(p, sizes):
    out, start = [], 0
    for s in sizes:
        out.append(p[..., start:start + s])
        start += s
    return out

def adaln_params(cond, w, b):
    m = jax.nn.silu(cond) @ w + b
    return jnp.split(m, 3, axis=-1)

def grid_positions(n_rows):
    rows = jnp.repeat(jnp.arange(n_rows, dtype=jnp.int32), GRID_W)
    cols = jnp.tile(jnp.arange(GRID_W, dtype=jnp.int32), n_rows)
    return rows, cols

def rope_1d(x, pos):
    m = x.shape[-1] // 2
    inv = ROPE_BASE ** (-jnp.arange(m, dtype=jnp.float32) / m)
    ang = pos.astype(jnp.float32)[:, None] * inv[None, :]
    cos = jnp.cos(ang)[:, None, :]
    sin = jnp.sin(ang)[:, None, :]
    x1 = x[..., :m].astype(jnp.float32)
    x2 = x[..., m:].astype(jnp.float32)
    return jnp.concatenate([x1 * cos - x2 * sin, x2 * cos + x1 * sin], axis=-1)

def rope_axial(x, rows, cols):
    h = x.shape[-1] // 2
    return jnp.concatenate([rope_1d(x[..., :h], rows), rope_1d(x[..., h:], cols)], axis=-1).astype(x.dtype)

def sink_attention(qg, k, v, sink, valid):
    s = jnp.einsum('bqhgd,bkhd->bhgqk', qg, k).astype(jnp.float32) * ATTN_SCALE
    if valid is not None:
        s = jnp.where(valid, s, NEG_INF)
    sink_col = jnp.broadcast_to(sink.astype(jnp.float32).reshape(1, A_KV_HEADS, A_GROUP, 1, 1),
                                s.shape[:-1] + (1,))
    p = jax.nn.softmax(jnp.concatenate([s, sink_col], axis=-1), axis=-1)[..., :-1]
    return jnp.einsum('bhgqk,bkhd->bqhgd', p, v.astype(jnp.float32))

def window_sink_attention(q, k, v, kc, vc, sink):
    Bn, T = q.shape[:2]
    nb = T // Q_BLOCK
    band = Q_BLOCK + 2 * WINDOW
    qg = q.reshape(Bn, T, A_KV_HEADS, A_GROUP, HEAD_DIM)
    pad = ((0, 0), (WINDOW, WINDOW), (0, 0), (0, 0))
    kp = jnp.pad(k, pad)
    vp = jnp.pad(v, pad)
    ctx_valid = jnp.ones((Q_BLOCK, kc.shape[1]), dtype=bool)

    def block(i):
        start = i * Q_BLOCK
        qb = lax.dynamic_slice_in_dim(qg, start, Q_BLOCK, axis=1)
        kb = lax.dynamic_slice_in_dim(kp, start, band, axis=1)
        vb = lax.dynamic_slice_in_dim(vp, start, band, axis=1)
        qpos = start + jnp.arange(Q_BLOCK)
        kpos = start - WINDOW + jnp.arange(band)
        valid = ((kpos[None, :] >= 0) & (kpos[None, :] < T)
                 & (jnp.abs(qpos[:, None] - kpos[None, :]) <= WINDOW))
        valid = jnp.concatenate([valid, ctx_valid], axis=1)
        return sink_attention(qb, jnp.concatenate([kb, kc], axis=1),
                              jnp.concatenate([vb, vc], axis=1), sink, valid)

    out = lax.map(block, jnp.arange(nb))
    return jnp.moveaxis(out, 0, 1).reshape(Bn, T, A_KV_HEADS, A_GROUP, HEAD_DIM)

def diff_attention(q1, q2, k1, k2, v, lam):
    s1 = jnp.einsum('bqhd,bkhd->bhqk', q1, k1).astype(jnp.float32) * ATTN_SCALE
    s2 = jnp.einsum('bqhd,bkhd->bhqk', q2, k2).astype(jnp.float32) * ATTN_SCALE
    w = jax.nn.softmax(s1, axis=-1) - lam * jax.nn.softmax(s2, axis=-1)
    return jnp.einsum('bhqk,bkhe->bqhe', w, v.astype(jnp.float32))

def blocked_diff_attention(q1, q2, k1, k2, v, lam):
    Bn, T = q1.shape[:2]
    nb = T // Q_BLOCK

    def block(i):
        start = i * Q_BLOCK
        return diff_attention(lax.dynamic_slice_in_dim(q1, start, Q_BLOCK, axis=1),
                              lax.dynamic_slice_in_dim(q2, start, Q_BLOCK, axis=1),
                              k1, k2, v, lam)

    out = lax.map(block, jnp.arange(nb))
    return jnp.moveaxis(out, 0, 1).reshape(Bn, T, B_HEADS, B_VDIM)

def even_mixer(hx, hc, rows, cols, w_in, a_qn, a_kn, a_sink, b_qn, b_kn,
               lq1, lk1, lq2, lk2, b_subln, lambda_init, need_ctx):
    dt = hx.dtype

    def project(h):
        Bn, T = h.shape[:2]
        qa, ka, va, ga, qb, kb, vb, gb = split_cols(h @ w_in, EVEN_SPLITS)
        qa = rms_norm(qa.reshape(Bn, T, A_HEADS, HEAD_DIM), a_qn)
        ka = rms_norm(ka.reshape(Bn, T, A_KV_HEADS, HEAD_DIM), a_kn)
        va = va.reshape(Bn, T, A_KV_HEADS, HEAD_DIM)
        qb = rms_norm(qb.reshape(Bn, T, 2 * B_HEADS, HEAD_DIM), b_qn)
        kb = rms_norm(kb.reshape(Bn, T, 2 * B_HEADS, HEAD_DIM), b_kn)
        vb = vb.reshape(Bn, T, B_HEADS, B_VDIM)
        return qa, ka, va, ga, qb, kb, vb, gb

    def split_pair(t):
        Bn, T = t.shape[:2]
        t = t.reshape(Bn, T, B_HEADS, 2, HEAD_DIM)
        return t[..., 0, :], t[..., 1, :]

    def merge(oa, ga, ob, gb):
        Bn, T = oa.shape[:2]
        ob = rms_norm(ob, b_subln) * (1.0 - lambda_init)
        oa = oa.reshape(Bn, T, A_WIDTH).astype(dt) * jax.nn.silu(ga)
        ob = ob.reshape(Bn, T, B_WIDTH).astype(dt) * jax.nn.silu(gb)
        return jnp.concatenate([oa, ob], axis=-1)

    qa_x, ka_x, va_x, ga_x, qb_x, kb_x, vb_x, gb_x = project(hx)
    qa_c, ka_c, va_c, ga_c, qb_c, kb_c, vb_c, gb_c = project(hc)
    qa_x = rope_axial(qa_x, rows, cols)
    ka_x = rope_axial(ka_x, rows, cols)
    qb_x = rope_axial(qb_x, rows, cols)
    kb_x = rope_axial(kb_x, rows, cols)

    lam = (jnp.exp(jnp.sum(lq1.astype(jnp.float32) * lk1.astype(jnp.float32)))
           - jnp.exp(jnp.sum(lq2.astype(jnp.float32) * lk2.astype(jnp.float32))) + lambda_init)

    q1x, q2x = split_pair(qb_x)
    k1x, k2x = split_pair(kb_x)
    k1c, k2c = split_pair(kb_c)

    oa_x = window_sink_attention(qa_x, ka_x, va_x, ka_c, va_c, a_sink)
    ob_x = blocked_diff_attention(q1x, q2x,
                                  jnp.concatenate([k1x, k1c], axis=1),
                                  jnp.concatenate([k2x, k2c], axis=1),
                                  jnp.concatenate([vb_x, vb_c], axis=1), lam)
    ox = merge(oa_x, ga_x, ob_x, gb_x)
    if not need_ctx:
        return ox, None
    Bn, L = hc.shape[:2]
    oa_c = sink_attention(qa_c.reshape(Bn, L, A_KV_HEADS, A_GROUP, HEAD_DIM), ka_c, va_c, a_sink, None)
    q1c, q2c = split_pair(qb_c)
    ob_c = diff_attention(q1c, q2c, k1c, k2c, vb_c, lam)
    oc = merge(oa_c, ga_c, ob_c, gb_c)
    return ox, oc

def gla_chunked(q, k, v, log_a, s0, with_output):
    Bn, H, T, dk = q.shape
    dv = v.shape[-1]
    n = T // G_CHUNK
    f32 = jnp.float32

    def ch(t):
        return t.astype(f32).reshape(Bn, H, n, G_CHUNK, t.shape[-1])

    q, k, v, la = ch(q), ch(k), ch(v), ch(log_a)
    b = jnp.cumsum(la, axis=3)
    b_last = b[:, :, :, -1:, :]
    d_state = jnp.einsum('bhncd,bhnce->bhnde', k * jnp.exp(b_last - b), v)
    decay = jnp.exp(b_last[:, :, :, 0, :])

    def step(S, inp):
        dec, ds = inp
        return dec[..., None] * S + ds, S

    s_fin, s_prev = lax.scan(step, s0.astype(f32),
                             (jnp.moveaxis(decay, 2, 0), jnp.moveaxis(d_state, 2, 0)))
    if not with_output:
        return None, s_fin
    s_prev = jnp.moveaxis(s_prev, 0, 2)
    qd = q * jnp.exp(b)
    kd = k * jnp.exp(-b)
    tri = jnp.tril(jnp.ones((G_CHUNK, G_CHUNK), dtype=bool))
    att = jnp.where(tri, jnp.einsum('bhncd,bhnsd->bhncs', qd, kd), 0.0)
    o = (jnp.einsum('bhncs,bhnse->bhnce', att, v)
         + jnp.einsum('bhncd,bhnde->bhnce', qd, s_prev))
    return o.reshape(Bn, H, T, dv), s_fin

def gla_mixer(hx, hc, w_in, wa_f, ba_f, wa_b, ba_b, out_norm, need_ctx):
    dt = hx.dtype

    def project(h):
        Bn, T = h.shape[:2]
        q, k, v, g, rf, rb = split_cols(h @ w_in, ODD_SPLITS)

        def heads(t, d):
            return t.reshape(Bn, T, G_HEADS, d).transpose(0, 2, 1, 3)

        la_f = jax.nn.log_sigmoid((rf @ wa_f + ba_f).astype(jnp.float32)) / G_TAU
        la_b = jax.nn.log_sigmoid((rb @ wa_b + ba_b).astype(jnp.float32)) / G_TAU
        return (heads(q, G_DK) * (G_DK ** -0.5), heads(k, G_DK), heads(v, G_DV), g,
                heads(la_f, G_DK), heads(la_b, G_DK))

    def flip(t):
        return jnp.flip(t, axis=2)

    def finish(o, g):
        Bn, H, T, dv = o.shape
        o = rms_norm(o.transpose(0, 2, 1, 3), out_norm).reshape(Bn, T, H * dv)
        return o.astype(dt) * jax.nn.silu(g)

    qx, kx, vx, gx, lfx, lbx = project(hx)
    qc, kc, vc, gc, lfc, lbc = project(hc)
    Bn = hx.shape[0]
    s0 = jnp.zeros((Bn, G_HEADS, G_DK, G_DV), jnp.float32)
    oc_f, sc_f = gla_chunked(qc, kc, vc, lfc, s0, need_ctx)
    oc_b, sc_b = gla_chunked(flip(qc), flip(kc), flip(vc), flip(lbc), s0, need_ctx)
    ox_f, _ = gla_chunked(qx, kx, vx, lfx, sc_f, True)
    ox_b, _ = gla_chunked(flip(qx), flip(kx), flip(vx), flip(lbx), sc_b, True)
    ox = finish(ox_f + flip(ox_b), gx)
    if not need_ctx:
        return ox, None
    oc = finish(oc_f + flip(oc_b), gc)
    return ox, oc

def first_inputs(seed: int = 0) -> dict:
    key = jax.random.key(seed)
    ks = jax.random.split(key, 32)
    f32 = jnp.float32

    def nrm(k, shape, scale):
        return jax.random.normal(k, shape, f32) * scale

    def gain(k, shape):
        return 1.0 + 0.1 * jax.random.normal(k, shape, f32)

    D = D_MODEL
    return {
        'x': nrm(ks[0], (BATCH, SEQ, D), 1.0),
        'c': nrm(ks[1], (BATCH, D), 1.0),
        'ctx': nrm(ks[2], (BATCH, CTX_LEN, D), 1.0),
        'c_ctx': nrm(ks[3], (D,), 1.0),
        'adaln_w': nrm(ks[4], (DEPTH, D, 3 * D), 0.5 * D ** -0.5),
        'adaln_b': nrm(ks[5], (DEPTH, 3 * D), 0.02),
        'norm_g': gain(ks[6], (DEPTH, D)),
        'w_out': nrm(ks[7], (DEPTH, D, D), D ** -0.5),
        'ab_w_in': nrm(ks[8], (N_EVEN, D, EVEN_IN), D ** -0.5),
        'a_q_norm': gain(ks[9], (N_EVEN, HEAD_DIM)),
        'a_k_norm': gain(ks[10], (N_EVEN, HEAD_DIM)),
        'a_sink': nrm(ks[11], (N_EVEN, A_HEADS), 0.5),
        'b_q_norm': gain(ks[12], (N_EVEN, HEAD_DIM)),
        'b_k_norm': gain(ks[13], (N_EVEN, HEAD_DIM)),
        'b_lambda_q1': nrm(ks[14], (N_EVEN, HEAD_DIM), 0.1),
        'b_lambda_k1': nrm(ks[15], (N_EVEN, HEAD_DIM), 0.1),
        'b_lambda_q2': nrm(ks[16], (N_EVEN, HEAD_DIM), 0.1),
        'b_lambda_k2': nrm(ks[17], (N_EVEN, HEAD_DIM), 0.1),
        'b_subln': gain(ks[18], (N_EVEN, B_VDIM)),
        'gla_w_in': nrm(ks[19], (N_ODD, D, ODD_IN), D ** -0.5),
        'gla_wa_f': nrm(ks[20], (N_ODD, G_RANK, G_HEADS * G_DK), G_RANK ** -0.5),
        'gla_ba_f': nrm(ks[21], (N_ODD, G_HEADS * G_DK), 0.1),
        'gla_wa_b': nrm(ks[22], (N_ODD, G_RANK, G_HEADS * G_DK), G_RANK ** -0.5),
        'gla_ba_b': nrm(ks[23], (N_ODD, G_HEADS * G_DK), 0.1),
        'gla_out_norm': gain(ks[24], (N_ODD, G_DV)),
    }

def first_block(x, c, ctx, c_ctx, adaln_w, adaln_b, norm_g, w_out, ab_w_in, a_q_norm, a_k_norm,
              a_sink, b_q_norm, b_k_norm, b_lambda_q1, b_lambda_k1, b_lambda_q2, b_lambda_k2,
              b_subln, gla_w_in, gla_wa_f, gla_ba_f, gla_wa_b, gla_ba_b, gla_out_norm):
    ROWS = x.shape[1] // GRID_W
    rows, cols = grid_positions(ROWS)
    for layer in range(DEPTH):
        need_ctx = layer < DEPTH - 1
        shx, scx, gtx = adaln_params(c, adaln_w[layer], adaln_b[layer])
        shc, scc, gtc = adaln_params(c_ctx, adaln_w[layer], adaln_b[layer])
        hx = rms_norm(x, norm_g[layer]) * (1.0 + scx[:, None, :]) + shx[:, None, :]
        hc = rms_norm(ctx, norm_g[layer]) * (1.0 + scc) + shc
        j = layer // 2
        if layer % 2 == 0:
            lambda_init = 0.8 - 0.6 * math.exp(-0.3 * layer)
            ox, oc = even_mixer(hx, hc, rows, cols, ab_w_in[j], a_q_norm[j], a_k_norm[j], a_sink[j],
                                b_q_norm[j], b_k_norm[j], b_lambda_q1[j], b_lambda_k1[j],
                                b_lambda_q2[j], b_lambda_k2[j], b_subln[j], lambda_init, need_ctx)
        else:
            ox, oc = gla_mixer(hx, hc, gla_w_in[j], gla_wa_f[j], gla_ba_f[j], gla_wa_b[j], gla_ba_b[j],
                               gla_out_norm[j], need_ctx)
        x = x + gtx[:, None, :] * (ox @ w_out[layer])
        if need_ctx:
            ctx = ctx + gtc * (oc @ w_out[layer])
    return x


DEPTH_2 = 1

CHUNK = 64
N_META = 16

POOL_GROUPS = 4
POOL_WINDOWS = (2, 4, 8, 16)
POOL_WIDTH = D_MODEL // 4
POOL_GDIM = POOL_WIDTH // POOL_GROUPS
CONV_WIDTH = D_MODEL // 4
CONV_KSIZE = 31
FOX_HEADS = 8
FOX_HEAD_DIM = 64
FOX_WIDTH = FOX_HEADS * FOX_HEAD_DIM
N_BRANCH = 3
IN_SPLITS = (POOL_WIDTH, CONV_WIDTH, CONV_WIDTH, FOX_WIDTH, FOX_WIDTH, FOX_WIDTH, FOX_HEADS, N_BRANCH * D_MODEL)
N_IN = sum(IN_SPLITS)
N_GROUPS = 4
EXPERTS_PER_GROUP = 4
N_EXPERTS = N_GROUPS * EXPERTS_PER_GROUP
TOP_K = 2
EXPERT_HIDDEN = D_MODEL // 4


def rms_norm_2(x, g):
    xf = x.astype(jnp.float32)
    y = xf * lax.rsqrt(jnp.mean(xf * xf, axis=-1, keepdims=True) + EPS)
    return (y * g.astype(jnp.float32)).astype(x.dtype)

def layer_norm(x, g, b):
    xf = x.astype(jnp.float32)
    mu = jnp.mean(xf, axis=-1, keepdims=True)
    var = jnp.mean(jnp.square(xf - mu), axis=-1, keepdims=True)
    y = (xf - mu) * lax.rsqrt(var + EPS)
    return (y * g.astype(jnp.float32) + b.astype(jnp.float32)).astype(x.dtype)

def pool_mixer(a, pool_w, pool_b, pool_scale):
    B_, L, _ = a.shape
    af = a.astype(jnp.float32).reshape(B_, L, POOL_GROUPS, POOL_GDIM)
    cs = jnp.concatenate([jnp.zeros_like(af[:, :1]), jnp.cumsum(af, axis=1)], axis=1)
    t = jnp.arange(L, dtype=jnp.int32)[:, None]
    win = jnp.array(POOL_WINDOWS, dtype=jnp.int32)[None, :]
    lo = jnp.maximum(t + 1 - win, 0)
    cnt = (t + 1 - lo).astype(jnp.float32)
    grp = jnp.arange(POOL_GROUPS, dtype=jnp.int32)[None, :]
    mean = (cs[:, 1:] - cs[:, lo, grp]) / cnt[None, :, :, None]
    diff = mean - af
    y = jnp.einsum('blgc,gcd->blgd', diff, pool_w.astype(jnp.float32)) + pool_b.astype(jnp.float32)
    y = y.reshape(B_, L, POOL_WIDTH) * pool_scale.astype(jnp.float32)
    return y.astype(a.dtype)

def conv_module(bv, bg, conv_w, conv_b, ln_g, ln_b):
    glu = bv * jax.nn.sigmoid(bg)
    y = lax.conv_general_dilated(
        glu, conv_w.astype(glu.dtype)[:, None, :], window_strides=(1,),
        padding=[(CONV_KSIZE - 1, 0)], dimension_numbers=('NWC', 'WIO', 'NWC'),
        feature_group_count=CONV_WIDTH)
    y = y + conv_b.astype(y.dtype)
    y = layer_norm(y, ln_g, ln_b)
    return jax.nn.silu(y)

def forgetting_attention(q, k, v, logf):
    B_, L, H, dh = q.shape
    n_blk = -(-L // Q_BLOCK)
    Lp = n_blk * Q_BLOCK
    pad = Lp - L
    qh = jnp.pad(q.transpose(0, 2, 1, 3), ((0, 0), (0, 0), (0, pad), (0, 0)))
    kh = jnp.pad(k.transpose(0, 2, 1, 3), ((0, 0), (0, 0), (0, pad), (0, 0)))
    vh = jnp.pad(v.transpose(0, 2, 1, 3), ((0, 0), (0, 0), (0, pad), (0, 0)))
    F = jnp.cumsum(jnp.pad(logf.transpose(0, 2, 1), ((0, 0), (0, 0), (0, pad))), axis=-1)
    qb = qh.reshape(B_, H, n_blk, Q_BLOCK, dh).transpose(2, 0, 1, 3, 4)
    Fq = F.reshape(B_, H, n_blk, Q_BLOCK).transpose(2, 0, 1, 3)
    qpos = jnp.arange(Lp, dtype=jnp.int32).reshape(n_blk, Q_BLOCK)
    kpos = jnp.arange(Lp, dtype=jnp.int32)
    scale = FOX_HEAD_DIM ** -0.5

    def block(args):
        qi, Fi, pi = args
        s = jnp.einsum('bhqd,bhkd->bhqk', qi, kh, preferred_element_type=jnp.float32) * scale
        s = s + Fi[..., None] - F[:, :, None, :]
        s = jnp.where(kpos[None, :] <= pi[:, None], s, -jnp.inf)
        p = jax.nn.softmax(s, axis=-1)
        return jnp.einsum('bhqk,bhkd->bhqd', p.astype(vh.dtype), vh)

    o = lax.map(block, (qb, Fq, qpos))
    o = o.transpose(1, 0, 3, 2, 4).reshape(B_, Lp, H * dh)
    return o[:, :L]

def mixer_layer(u, w_in, b_forget, pool_w, pool_b, pool_scale, conv_w, conv_b, conv_ln_g, conv_ln_b,
                w_out_a, w_out_b, w_out_c, w_o):
    B_, L, D = u.shape
    p = u @ w_in
    a, bv, bg, q, k, v, fg, gates = jnp.split(p, [int(i) for i in np.cumsum(IN_SPLITS)[:-1]], axis=-1)
    ya = pool_mixer(a, pool_w, pool_b, pool_scale) @ w_out_a
    yb = conv_module(bv, bg, conv_w, conv_b, conv_ln_g, conv_ln_b) @ w_out_b
    logf = jax.nn.log_sigmoid((fg + b_forget).astype(jnp.float32))
    heads = lambda z: z.reshape(B_, L, FOX_HEADS, FOX_HEAD_DIM)
    yc = forgetting_attention(heads(q), heads(k), heads(v), logf) @ w_out_c
    g = jax.nn.sigmoid(gates.reshape(B_, L, N_BRANCH, D))
    merged = g[:, :, 0] * ya + g[:, :, 1] * yb + g[:, :, 2] * yc
    return merged @ w_o

def hier_moe(h, router_g, router_g_b, router_e, router_e_b, exp_w1, exp_w3, exp_w2):
    B_, L, D = h.shape
    t = h.reshape(B_ * L, D)
    T = t.shape[0]
    glog = (t @ router_g).astype(jnp.float32) + router_g_b.astype(jnp.float32)
    gprob = jax.nn.softmax(glog, axis=-1)
    _, gsel = lax.top_k(glog, 1)
    gw = jnp.take_along_axis(gprob, gsel, axis=-1)
    elog = ((t @ router_e).astype(jnp.float32) + router_e_b.astype(jnp.float32)).reshape(T, N_GROUPS, EXPERTS_PER_GROUP)
    elog_sel = jnp.take_along_axis(elog, gsel[:, :, None], axis=1)[:, 0]
    eprob = jax.nn.softmax(elog_sel, axis=-1)
    top_p, top_i = lax.top_k(eprob, TOP_K)
    top_p = top_p / jnp.sum(top_p, axis=-1, keepdims=True)
    w_grp = jnp.sum(jax.nn.one_hot(top_i, EXPERTS_PER_GROUP, dtype=jnp.float32) * top_p[..., None], axis=1)
    comb = (jax.nn.one_hot(gsel[:, 0], N_GROUPS, dtype=jnp.float32)[:, :, None] * w_grp[:, None, :] * gw[:, :, None])
    comb = comb.reshape(T, N_EXPERTS).astype(t.dtype)
    y = jnp.zeros_like(t)
    for e in range(N_EXPERTS):
        he = jax.nn.silu(t @ exp_w1[e]) * (t @ exp_w3[e])
        y = y + comb[:, e:e + 1] * (he @ exp_w2[e])
    return y.reshape(B_, L, D)

def second_inputs(seed: int = 0) -> dict:
    key = jax.random.key(seed)
    ks = jax.random.split(key, 32)
    f32 = jnp.float32
    nrm = lambda k, shape, s: (jax.random.normal(k, shape, f32) * s).astype(f32)
    D = D_MODEL
    return {
        "x": nrm(ks[0], (BATCH, SEQ, D), 1.0),
        "meta": nrm(ks[1], (N_META, D), 1.0),
        "norm1_g": 1.0 + nrm(ks[2], (DEPTH_2, D), 0.02),
        "w_in": nrm(ks[3], (DEPTH_2, D, N_IN), D ** -0.5),
        "b_forget": jax.random.uniform(ks[4], (DEPTH_2, FOX_HEADS), f32, 1.0, 6.0),
        "pool_w": nrm(ks[5], (DEPTH_2, POOL_GROUPS, POOL_GDIM, POOL_GDIM), POOL_GDIM ** -0.5),
        "pool_b": nrm(ks[6], (DEPTH_2, POOL_GROUPS, POOL_GDIM), 0.01),
        "pool_scale": 1.0 + nrm(ks[7], (DEPTH_2, POOL_WIDTH), 0.1),
        "conv_w": nrm(ks[8], (DEPTH_2, CONV_KSIZE, CONV_WIDTH), CONV_KSIZE ** -0.5),
        "conv_b": nrm(ks[9], (DEPTH_2, CONV_WIDTH), 0.01),
        "conv_ln_g": 1.0 + nrm(ks[10], (DEPTH_2, CONV_WIDTH), 0.02),
        "conv_ln_b": nrm(ks[11], (DEPTH_2, CONV_WIDTH), 0.01),
        "w_out_a": nrm(ks[12], (DEPTH_2, POOL_WIDTH, D), POOL_WIDTH ** -0.5),
        "w_out_b": nrm(ks[13], (DEPTH_2, CONV_WIDTH, D), CONV_WIDTH ** -0.5),
        "w_out_c": nrm(ks[14], (DEPTH_2, FOX_WIDTH, D), FOX_WIDTH ** -0.5),
        "w_o": nrm(ks[15], (DEPTH_2, D, D), D ** -0.5),
        "norm2_g": 1.0 + nrm(ks[16], (DEPTH_2, D), 0.02),
        "router_g": nrm(ks[17], (DEPTH_2, D, N_GROUPS), D ** -0.5),
        "router_g_b": nrm(ks[18], (DEPTH_2, N_GROUPS), 0.01),
        "router_e": nrm(ks[19], (DEPTH_2, D, N_EXPERTS), D ** -0.5),
        "router_e_b": nrm(ks[20], (DEPTH_2, N_EXPERTS), 0.01),
        "exp_w1": nrm(ks[21], (DEPTH_2, N_EXPERTS, D, EXPERT_HIDDEN), D ** -0.5),
        "exp_w3": nrm(ks[22], (DEPTH_2, N_EXPERTS, D, EXPERT_HIDDEN), D ** -0.5),
        "exp_w2": nrm(ks[23], (DEPTH_2, N_EXPERTS, EXPERT_HIDDEN, D), EXPERT_HIDDEN ** -0.5),
        "final_g": 1.0 + nrm(ks[24], (D,), 0.02),
    }

def second_block(x, meta, norm1_g, w_in, b_forget, pool_w, pool_b, pool_scale, conv_w, conv_b, conv_ln_g,
              conv_ln_b, w_out_a, w_out_b, w_out_c, w_o, norm2_g, router_g, router_g_b, router_e,
              router_e_b, exp_w1, exp_w3, exp_w2, final_g):
    B_ = x.shape[0]
    m = jnp.broadcast_to(meta.astype(x.dtype)[None], (B_, N_META, D_MODEL))
    h = jnp.concatenate([m, x], axis=1)
    for l in range(DEPTH_2):
        u = rms_norm_2(h, norm1_g[l])
        h = h + mixer_layer(u, w_in[l], b_forget[l], pool_w[l], pool_b[l], pool_scale[l], conv_w[l],
                            conv_b[l], conv_ln_g[l], conv_ln_b[l], w_out_a[l], w_out_b[l], w_out_c[l], w_o[l])
        v = rms_norm_2(h, norm2_g[l])
        h = h + hier_moe(v, router_g[l], router_g_b[l], router_e[l], router_e_b[l], exp_w1[l], exp_w3[l], exp_w2[l])
    return rms_norm_2(h[:, N_META:], final_g)


def setup_inputs(seed=0):
    out = dict(first_inputs(seed))
    for name, value in second_inputs(seed + 1).items():
        if name != "x":
            out[name + "_2"] = value
    return out


def reference(
    x, c, ctx, c_ctx, adaln_w, adaln_b, norm_g, w_out, ab_w_in, a_q_norm, a_k_norm, a_sink,
    b_q_norm, b_k_norm, b_lambda_q1, b_lambda_k1, b_lambda_q2, b_lambda_k2, b_subln, gla_w_in,
    gla_wa_f, gla_ba_f, gla_wa_b, gla_ba_b, gla_out_norm, meta_2, norm1_g_2, w_in_2, b_forget_2,
    pool_w_2, pool_b_2, pool_scale_2, conv_w_2, conv_b_2, conv_ln_g_2, conv_ln_b_2, w_out_a_2,
    w_out_b_2, w_out_c_2, w_o_2, norm2_g_2, router_g_2, router_g_b_2, router_e_2, router_e_b_2,
    exp_w1_2, exp_w3_2, exp_w2_2, final_g_2,
):
    x = first_block(
        x, c, ctx, c_ctx, adaln_w, adaln_b, norm_g, w_out, ab_w_in, a_q_norm, a_k_norm, a_sink,
        b_q_norm, b_k_norm, b_lambda_q1, b_lambda_k1, b_lambda_q2, b_lambda_k2, b_subln,
        gla_w_in, gla_wa_f, gla_ba_f, gla_wa_b, gla_ba_b, gla_out_norm,
    )
    return second_block(
        x, meta_2, norm1_g_2, w_in_2, b_forget_2, pool_w_2, pool_b_2, pool_scale_2, conv_w_2,
        conv_b_2, conv_ln_g_2, conv_ln_b_2, w_out_a_2, w_out_b_2, w_out_c_2, w_o_2, norm2_g_2,
        router_g_2, router_g_b_2, router_e_2, router_e_b_2, exp_w1_2, exp_w3_2, exp_w2_2,
        final_g_2,
    )


_drawn_inputs = setup_inputs


def setup_inputs(seed=0):
    import zlib

    import numpy as np

    out = dict(_drawn_inputs(seed))
    spreads = {}
    factors = {'a_q_norm': 8.0,
     'a_k_norm': 8.0,
     'a_sink': 8.0,
     'b_q_norm': 4.919,
     'b_k_norm': 5.105,
     'b_lambda_q1': 44.842,
     'b_lambda_k1': 4.551,
     'b_lambda_q2': 3.817,
     'b_lambda_k2': 2.972,
     'b_subln': 3.238,
     'gla_ba_f': 3.615,
     'gla_ba_b': 3.732,
     'norm1_g_2': 3.06,
     'pool_b_2': 23.271,
     'conv_b_2': 17.583,
     'conv_ln_g_2': 17.068,
     'conv_ln_b_2': 29.606,
     'router_g_b_2': 17.62,
     'router_e_b_2': 41.978,
     'final_g_2': 8.013,
     'norm2_g_2': 6.32}
    for name, (base, spread) in spreads.items():
        noise = np.random.default_rng([zlib.crc32(name.encode()), seed]).standard_normal(out[name].shape)
        drawn = base * np.exp(spread * noise) if base else spread * noise
        out[name] = jnp.asarray(drawn.astype(out[name].dtype))
    for name, factor in factors.items():
        out[name] = (out[name] * factor).astype(out[name].dtype)
    return out
```

```python
from contextlib import ExitStack

import numpy as np
import concourse.bass as bass
from concourse import mybir

F32 = mybir.dt.float32
F32R = mybir.dt.float32r
BF16 = mybir.dt.bfloat16
ALU = mybir.AluOpType
ACT = mybir.ActivationFunctionType
AX = mybir.AxisListType.X

P = 128
D = 1024
KD = D // P
T = 1024
CTX = 256
META = 16
L2 = META + T
X0 = META
C0 = META + T
NT1 = T + CTX
EPS = 1e-6
NEG = -1e30
HD = 64
SCALE = HD ** -0.5
LAMBDA_INIT = 0.8 - 0.6 * float(np.exp(-0.3 * 0))
GC = 64
GH, GDK, GDV = 4, 128, 256
NE, EH = 16, 256
TILES1 = [(0, 512), (512, 512), (1024, 256)]
TILES2 = [(0, 352), (352, 352), (704, 336)]


class Shared:
    def __init__(self, nc, sb, tables):
        self.X = sb("residual", [P, KD, META + NT1])
        self.par, self.con = sb("params", [P, PARAM_N]), sb("consts", [P, CONST_N])
        self.mask, self.nsink = sb("mask", [P, 5 * P], BF16), sb("neg_sink", [P, 8])
        self.lam, self.neglam = sb("lambda", [P, 8]), sb("neg_lambda", [P, 1])
        self.mod, self.gain = sb("mod", [P, 2, 48]), sb("mod_gain", [P, 2, 16])
        self.subln, self.eps = sb("subln", [P, 1]), sb("eps", [P, 1])
        self.tables = tables
        self.y_stored = nc.alloc_semaphore("y_stored")


def shape_constants():
    p = np.arange(P)
    parts = {}
    parts["ident"] = np.eye(P)
    parts["ones"] = np.ones((P, P))
    parts["headones"] = (p[:, None] // HD == p[None, :] // HD)
    rot = np.zeros((P, P))
    for d in range(P):
        if d % 32 < 16:
            rot[d + 16, d] = -1.0
        else:
            rot[d - 16, d] = 1.0
    parts["rot"] = rot
    m = 16
    inv = (np.float32(10000.0) ** (-np.arange(m, dtype=np.float32) / np.float32(m))).astype(np.float32)
    tok = np.arange(T)
    rows, cols = tok // 64, tok % 64
    ang = np.zeros((P, T), np.float32)
    for d in range(P):
        pos = rows if d % HD < 32 else cols
        ang[d] = pos.astype(np.float32) * inv[d % 16]
    parts["cos"], parts["sin"] = np.cos(ang), np.sin(ang)
    reset = np.ones((P, NT1)); reset[:, ::GC] = 0
    parts["reset"] = reset
    s, c = p[:, None], p[None, :]
    parts["causal"] = (s // GC == c // GC) & (s <= c)
    parts["anti"] = (s // GC == c // GC) & (s >= c)
    inv_cnt = np.zeros((P, 2, META))
    for j in range(2):
        for q in range(P):
            w = 2 ** (2 * j + q // 64 + 1)
            inv_cnt[q, j] = 1.0 / np.minimum(np.arange(META) + 1, w)
    parts["invcnt"] = inv_cnt.reshape(P, -1)
    return parts


def mask_constants():
    q, x = np.arange(P)[:, None], np.arange(3 * P)[None, :]
    late = np.where(x - P <= q, 0.0, NEG)
    early = np.where(np.arange(P)[None, :] >= q, 0.0, NEG)
    return np.concatenate([np.eye(P), early, late], 1)


CONST_WIDTHS = [("ident", P), ("ones", P), ("headones", P), ("rot", P), ("causal", P), ("anti", P), ("invcnt", 2 * META)]
PARAM_WIDTHS = [
    ("cond", 2 * KD), ("adaln_b", 2 * 3 * KD), ("norm_g", 2 * KD), ("a_qn", 1), ("a_kn", 1), ("sink", 8),
    ("b_qn", 1), ("b_kn", 1), ("lq1", HD), ("lk1", HD), ("lq2", HD), ("lk2", HD), ("subln", 1), ("ba", 2 * GH),
    ("out_norm", 2), ("norm1", KD), ("bforget", 1), ("pool_b", 2), ("pool_scale", 2), ("conv_w", 62),
    ("conv_b", 2), ("conv_g", 2), ("conv_lb", 2), ("norm2", KD), ("rbias", 20), ("final_g", KD)]


def offsets(widths):
    at, n = {}, 0
    for name, w in widths:
        at[name] = (n, w)
        n += w
    return at, n


CONST_AT, CONST_N = offsets(CONST_WIDTHS)
PARAM_AT, PARAM_N = offsets(PARAM_WIDTHS)


def col(tile, at, name, j=None, w=1):
    o, width = at[name]
    if j is None:
        return tile[:, o:o + width]
    return tile[:, o + j:o + j + w]


class Chain:
    def __init__(self, eng, sem):
        self.eng, self.sem, self.n = eng, sem, 0

    def __call__(self, ins):
        self.n += 1
        ins.then_inc(self.sem, 1)
        self.eng.wait_ge(self.sem, self.n)


def phase(nc, ctx):
    mine = []

    def sb(name, shape, dt=F32):
        return ctx.enter_context(nc.sbuf_tensor(f"{name}_{nc_tag(nc)}", shape, dt))

    def ps(name, shape, dt=F32):
        return ctx.enter_context(nc.psum_tensor(f"{name}_{nc_tag(nc)}", shape, dt))

    def sem(name):
        if not name.startswith("gp_"):
            mine.append(ctx.enter_context(nc.semaphore(f"{name}_{nc_tag(nc)}")))
            return mine[-1]
        return nc.alloc_semaphore(f"{name}_{nc_tag(nc)}")

    used = sorted(s.num for s in TAGS["used"])
    while used:
        n = 1
        while n < len(used) and used[n] == used[0] + n:
            n += 1
        nc.gpsimd.sem_clear(range(used[0], used[0] + n))
        used = used[n:]
    TAGS["used"] = mine
    return sb, ps, sem


TAGS = {"n": 0, "used": []}


def nc_tag(nc):
    TAGS["n"] += 1
    return TAGS["n"]


def setup_phase(nc, E, dram):
    with ExitStack() as ctx:
        sb, ps, sem = phase(nc, ctx)
        ring = sb("adaln_w", [P, 3, 3 * D])
        sc = sb("silu_cond", [P, 16])
        sg = sb("sigma_cond", [P, 16])
        lam = sb("lam_work", [P, 4 * HD])
        acc = [ps(f"mod{l}", [P, 48]) for l in range(2)]
        loaded, x_in = sem("small_loaded"), sem("gp_x_loaded")
        w_in = [sem(f"w_loaded{i}") for i in range(3)]
        cond_ready, tile_used, steps, asteps = (sem(n) for n in ("cond_ready", "w_used", "dve_steps", "act_steps"))
        lam_sum, lam_exp = sem("lam_sum"), sem("lam_exp")
        block = ctx.enter_context(nc.Block())
        NTILE = 2 * KD

        @block.sync
        def _(eng):
            eng.dma_start(E.par[:], dram["params"]).then_inc(loaded, 16)
            eng.dma_start(E.con[:], dram["consts"]).then_inc(loaded, 16)
            eng.dma_start(E.mask32[:], dram["masks"]).then_inc(loaded, 16)
            for i in range(NTILE):
                if i >= 3:
                    eng.wait_ge(tile_used, i - 2)
                eng.dma_start(ring[:, i % 3, :], dram["adaln_w"][i // KD, i % KD]).then_inc(w_in[i % 3], 16)
            eng.wait_ge(x_in, 32)

        @block.gpsimd
        def _(eng):
            eng.dma_start(E.X[:, :, X0:X0 + NT1], dram["x0"]).then_inc(x_in, 16)
            eng.dma_start(E.X[:, :, 0:META], dram["meta"]).then_inc(x_in, 16)

        @block.scalar
        def _(eng):
            eng.wait_ge(loaded, 48)
            eng.activation(sg[:], col(E.par, PARAM_AT, "cond"), ACT.Exp, scale=-1.0).then_inc(asteps, 1)
            eng.wait_ge(lam_sum, 1)
            eng.activation(E.lam[:, 0:2], E.lam[:, 2:4], ACT.Exp).then_inc(lam_exp, 1)

        @block.vector
        def _(eng):
            chain = Chain(eng, steps)
            eng.wait_ge(loaded, 48)
            eng.wait_ge(asteps, 1)
            chain(eng.tensor_scalar(sg[:], sg[:], 1.0, None, ALU.add))
            chain(eng.reciprocal(sg[:], sg[:]))
            eng.tensor_tensor(sc[:], col(E.par, PARAM_AT, "cond"), sg[:], ALU.mult).then_inc(cond_ready, 1)
            chain(eng.memset(E.eps[:], EPS))
            chain(eng.tensor_copy(E.mask[:], E.mask32[:]))
            chain(eng.tensor_scalar(E.nsink[:], col(E.par, PARAM_AT, "sink"), -1.0, None, ALU.mult))
            for j, (a, b) in enumerate((("lq1", "lk1"), ("lq2", "lk2"))):
                chain(eng.tensor_tensor(lam[:, j * HD:(j + 1) * HD], col(E.par, PARAM_AT, a),
                                        col(E.par, PARAM_AT, b), ALU.mult))
            red = eng.tensor_reduce(E.lam[:, 2:4], lam[:, 0:2 * HD].rearrange("p (j d) -> p j d", j=2), AX, ALU.add)
            red.then_inc(lam_sum, 1)
            eng.wait_ge(lam_exp, 1)
            chain(eng.tensor_tensor(E.lam[:, 4:5], E.lam[:, 1:2], E.lam[:, 0:1], ALU.subtract))
            chain(eng.tensor_scalar(E.neglam[:], E.lam[:, 4:5], -LAMBDA_INIT, None, ALU.add))
            for l in range(2):
                eng.wait_ge(tile_used, KD * (l + 1))
                bias = col(E.par, PARAM_AT, "adaln_b", 24 * l, 24).unsqueeze(2).to_broadcast([P, 24, 2])
                chain(eng.tensor_tensor(E.mod[:, l, :].rearrange("p (f c) -> p f c", c=2),
                                        acc[l][:].rearrange("p (f c) -> p f c", c=2), bias, ALU.add))
                gain = col(E.par, PARAM_AT, "norm_g", 8 * l, 8).unsqueeze(2).to_broadcast([P, 8, 2])
                chain(eng.tensor_scalar(E.gain[:, l, :], E.mod[:, l, 16:32], 1.0, None, ALU.add))
                chain(eng.tensor_tensor(E.gain[:, l, :].rearrange("p (f c) -> p f c", c=2),
                                        E.gain[:, l, :].rearrange("p (f c) -> p f c", c=2), gain, ALU.mult))

        @block.tensor
        def _(eng):
            eng.wait_ge(cond_ready, 1)
            for i in range(NTILE):
                l, k = i // KD, i % KD
                eng.wait_ge(w_in[i % 3], 16 * (i // 3 + 1))
                for f in range(24):
                    mm = eng.matmul(acc[l][:, 2 * f:2 * f + 2], ring[:, i % 3, f * P:(f + 1) * P],
                                    sc[:, 2 * k:2 * k + 2], start=(k == 0 and f == 0), stop=(k == KD - 1),
                                    skip_group_check=True)
                mm.then_inc(tile_used, 1)


def norm_phase(nc, E, x_of, tiles, gain_of, shift_of, hi, lo, out=None, out_dram=None):
    with ExitStack() as ctx:
        sb, ps, sem = phase(nc, ctx)
        sq = sb("sq", [P, 4, 512])
        rstd = sb("rstd", [P, 2, 512])
        u = sb("u", [P, 4, 512])
        ss = [ps(f"ss{i}", [P, 512]) for i in range(2)]
        squared, rs_ready, u_ready, hi_ready, lo_done, sq_used = (
            sem("squared"), sem("rstd_ready"), sem("u_ready"), sem("hi_ready"), sem("lo_done"), sem("sq_used"))
        ms_ready = sem("mean_square_ready")
        block = ctx.enter_context(nc.Block())
        NTL = len(tiles)


        @block.scalar
        def _(eng):
            def squares(t):
                off, n = tiles[t]
                for k in range(KD):
                    i = t * KD + k
                    if i >= 4:
                        eng.wait_ge(sq_used, i - 3)
                    eng.activation(sq[:, i % 4, 0:n], x_of(k, off, n), ACT.Square).then_inc(squared, 1)
            squares(0)
            for t, (off, n) in enumerate(tiles):
                if t + 1 < NTL:
                    squares(t + 1)
                eng.wait_ge(sq_used, KD * (t + 1))
                if t >= 2:
                    eng.wait_ge(u_ready, KD * (t - 1))
                eng.activation(rstd[:, t % 2, 0:n], ss[t % 2][:, 0:n], ACT.Ln, scale=1.0 / D,
                               bias=E.eps[:]).then_inc(ms_ready, 1)
                eng.wait_ge(ms_ready, t + 1)
                eng.activation(rstd[:, t % 2, 0:n], rstd[:, t % 2, 0:n], ACT.Exp, scale=-0.5).then_inc(rs_ready, 1)
                if out is None:
                    for k in range(KD):
                        i = t * KD + k
                        eng.wait_ge(u_ready, i + 1)
                        s = shift_of(k, t)
                        if s is None:
                            eng.activation(hi[:, k, off:off + n], u[:, i % 4, 0:n], ACT.Copy).then_inc(hi_ready, 1)
                        else:
                            eng.activation(hi[:, k, off:off + n], u[:, i % 4, 0:n], ACT.Identity,
                                           bias=s).then_inc(hi_ready, 1)

        @block.tensor
        def _(eng):
            for t, (off, n) in enumerate(tiles):
                if t >= 2:
                    eng.wait_ge(ms_ready, t - 1)
                for k in range(KD):
                    i = t * KD + k
                    eng.wait_ge(squared, i + 1)
                    eng.matmul(ss[t % 2][:, 0:n], col(E.con, CONST_AT, "ones"), sq[:, i % 4, 0:n],
                               start=(k == 0), stop=(k == KD - 1)).then_inc(sq_used, 1)

        @block.vector
        def _(eng):
            for t, (off, n) in enumerate(tiles):
                eng.wait_ge(rs_ready, t + 1)

                def split(k):
                    i = t * KD + k
                    eng.wait_ge(hi_ready, i + 1)
                    h = hi[:, k, off:off + n].bitcast(F32)
                    s = shift_of(k, t)
                    if s is None:
                        ins = eng.tensor_tensor(lo[:, k, off:off + n], u[:, i % 4, 0:n], h, ALU.subtract)
                    else:
                        ins = eng.scalar_tensor_tensor(lo[:, k, off:off + n], u[:, i % 4, 0:n], s, h,
                                                       ALU.add, ALU.subtract)
                    ins.then_inc(lo_done, 1)

                for k in range(KD):
                    i = t * KD + k
                    if out is not None:
                        eng.scalar_tensor_tensor(out[:, k, off:off + n], x_of(k, off, n), gain_of(k, t),
                                                 rstd[:, t % 2, 0:n], ALU.mult, ALU.mult).then_inc(u_ready, 1)
                        continue
                    if i >= 4:
                        eng.wait_ge(lo_done, i - 3)
                    eng.scalar_tensor_tensor(u[:, i % 4, 0:n], x_of(k, off, n), gain_of(k, t),
                                             rstd[:, t % 2, 0:n], ALU.mult, ALU.mult).then_inc(u_ready, 1)
                    if k >= 1:
                        split(k - 1)
                if out is None:
                    split(KD - 1)

        if out is not None:
            @block.sync
            def _(eng):
                for t, (off, n) in enumerate(tiles):
                    eng.wait_ge(u_ready, KD * (t + 1))
                    eng.dma_start(out_dram[:, :, off:off + n], out[:, :, off:off + n]).then_inc(E.y_stored, 16)
                eng.wait_ge(E.y_stored, 16 * NTL)


class JobArgs:
    def __init__(self, func=None, out=None, gain=None, f=None, gate_of=None, first=False, last=False, gates=None,
                 hi=None, lo=None, slot=None, reuse=None, needs=None):
        self.func, self.out, self.gain, self.f, self.gate_of = func, out, gain, f, gate_of
        self.first, self.last, self.gates, self.hi, self.lo = first, last, gates, hi, lo
        self.slot, self.reuse, self.needs = slot, reuse, needs


class Job:
    def __init__(self, w, k0, k1, rhs, tiles, kind, **kw):
        self.w, self.k0, self.k1, self.rhs, self.tiles, self.kind = w, k0, k1, rhs, tiles, kind
        self.a = JobArgs(**kw)


def gemm_phase(nc, E, wdram, jobs, comb=None):
    with ExitStack() as ctx:
        sb, ps, sem = phase(nc, ctx)
        NJ = len(jobs)
        NW = max(j.w for j in jobs) + 1
        last_job = {j.w: i for i, j in enumerate(jobs)}
        kinds = {j.kind for j in jobs}
        NTmax = 1280 if "rope" in kinds or any(j.tiles[-1][0] + j.tiles[-1][1] > L2 for j in jobs) else L2
        NSTG = 2 if "gate" in kinds else 3
        stage = sb("w_stage", [P, NSTG, KD * P])
        whi = sb("w_hi", [P, 2, KD * P], F32R)
        wlo = sb("w_lo", [P, 2, KD * P], F32R)
        acc = [ps(f"acc{i}", [P, 3, 512]) for i in range(2)]
        w_in = [sem(f"w_loaded{i}") for i in range(NSTG)]
        w_hi, w_lo, mm = sem("w_hi_ready"), sem("w_lo_ready"), sem("products")
        free = [sem(f"acc_free{i}") for i in range(2)]
        steps = sem("dve_steps")
        out_stored = [sem(f"out_stored{i}") for i in range(2)]
        tiles_before = [sum(len(j.tiles) for j in jobs[:i]) for i in range(NJ + 1)]
        free_before = {}
        cnt = [0, 0]
        for i, j in enumerate(jobs):
            free_before[i] = cnt[i % 2]
            cnt[i % 2] += len(j.tiles)
        storing = [i for i, j in enumerate(jobs) if j.kind in ("store", "rope")]
        turn = {i: n for n, i in enumerate(storing)}
        if storing:
            outb = sb("out_stage", [P, 2, NTmax])
        if "rope" in kinds:
            xg = sb("rope_x", [P, 1280])
            sq = sb("rope_sq", [P, 1280])
            tab = sb("rope_tab", [P, 2, T])
            t1 = sb("rope_t1", [P, 512])
            t2 = sb("rope_t2", [P, 512])
            rs = sb("rope_rs", [P, 512])
            aux = [ps("rope_ss", [P, 512]), ps("rope_rot", [P, 512])]
            tab_in, xg_ready, aux_done, rope_done, ms_ready, rs_ready = (
                sem(n) for n in ("tab_loaded", "xg_ready", "aux_done", "rope_done", "mean_square_ready", "rstd_ready"))
        ropes = [i for i, j in enumerate(jobs) if j.kind == "rope"]
        ropes_tiles = {i: sum(len(jobs[q].tiles) for q in ropes if q < i) for i in ropes}
        if "gate" in kinds:
            gt = sb("gates", [P, 3, 352])
            gtmp = sb("gated", [P, 352])
            gate_in = [sem(f"gp_gate_loaded{i}") for i in range(3)]
            gated, m_hi, m_lo = sem("gated"), sem("merged_hi"), sem("merged_lo")

            def halves(x):
                return x.rearrange("p (a b) -> p a b", a=2)

            def merged(t, n):
                return E.X[:, 2 * t:2 * t + 2, C0:C0 + n // 2]
        if "up" in kinds:
            s1 = sb("silu_up", [P, L2])
            h2 = sb("hidden", [P, 352])
            cb = sb("comb", [P, 2, L2])
            hhi, hlo = comb["hhi"], comb["hlo"]
            cb_in = [sem(f"gp_comb_loaded{i}") for i in range(2)]
            s1_ready, he_ready, he_hi, he_lo = sem("silu_ready"), sem("he_ready"), sem("he_hi"), sem("he_lo")
        block = ctx.enter_context(nc.Block())
        order = {}
        for kd in ("up", "he", "down", "gate"):
            n = 0
            for i, j in enumerate(jobs):
                if j.kind == kd:
                    for t in range(len(j.tiles)):
                        order[i, t] = n
                        n += 1

        @block.sync
        def _(eng):
            if "rope" in kinds:
                eng.dma_start(tab[:], E.tables).then_inc(tab_in, 16)
            for w in range(NW):
                if w >= NSTG:
                    eng.wait_ge(w_lo, w - NSTG + 1)
                eng.dma_start(stage[:, w % NSTG, :], wdram[w]).then_inc(w_in[w % NSTG], 16)

        @block.gpsimd
        def _(eng):
            if "gate" in kinds:
                for i, j in enumerate(jobs):
                    if j.kind == "gate":
                        for t, (off, w) in enumerate(j.tiles):
                            if i >= 1:
                                eng.wait_ge(free[(i - 1) % 2], free_before[i - 1] + t + 1)
                            eng.dma_start(gt[:, t, 0:w], j.a.gates[:, off:off + w]).then_inc(gate_in[t], 16)
            if "up" in kinds:
                for e in range(NE):
                    if e >= 2:
                        eng.wait_ge(he_ready, 6 * (e - 1))
                    eng.dma_start(cb[:, e % 2, :], comb["dram"][e:e + 1, :].to_broadcast([P, L2])).then_inc(cb_in[e % 2], 16)

        @block.scalar
        def _(eng):
            def round_w(w):
                eng.wait_ge(w_in[w % NSTG], 16 * (w // NSTG + 1))
                eng.activation(whi[:, w % 2, :], stage[:, w % NSTG, :], ACT.Copy).then_inc(w_hi, 1)
            def store(i):
                n, j = turn[i], jobs[i]
                width = j.tiles[-1][0] + j.tiles[-1][1]
                if j.kind == "store":
                    eng.wait_ge(free[i % 2], free_before[i] + len(j.tiles))
                else:
                    eng.wait_ge(rope_done, ropes_tiles[i] + len(j.tiles))
                eng.dma_start(j.a.out[:, 0:width], outb[:, n % 2, 0:width]).then_inc(out_stored[n % 2], 16)

            def roots(i):
                for t, (off, n) in enumerate(jobs[i].tiles):
                    r = ropes_tiles[i] + t
                    eng.wait_ge(aux_done, r + 1)
                    if r >= 1:
                        eng.wait_ge(rope_done, r)
                    eng.activation(rs[:, 0:n], aux[0][:, 0:n], ACT.Ln, scale=1.0 / HD, bias=E.eps[:]).then_inc(ms_ready, 1)
                    eng.wait_ge(ms_ready, r + 1)
                    eng.activation(rs[:, 0:n], rs[:, 0:n], ACT.Exp, scale=-0.5).then_inc(rs_ready, 1)

            for w in range(min(2, NW)):
                round_w(w)
            for i, j in enumerate(jobs):
                if i >= 1 and jobs[i - 1].kind == "rope":
                    roots(i - 1)
                    store(i - 1)
                if last_job[j.w] == i and j.w + 2 < NW:
                    eng.wait_ge(mm, tiles_before[i + 1])
                    round_w(j.w + 2)
                a = acc[i % 2]
                for t, (off, n) in enumerate(j.tiles):
                    src = a[:, t, 0:n]
                    if j.kind == "store":
                        if t == 0 and turn[i] >= 2:
                            eng.wait_ge(out_stored[turn[i] % 2], 16 * (turn[i] // 2))
                        eng.wait_ge(mm, tiles_before[i] + t + 1)
                        eng.activation(outb[:, turn[i] % 2, off:off + n], src, j.a.func).then_inc(free[i % 2], 1)
                    elif j.kind == "rope":
                        if t == 0 and i != ropes[0]:
                            eng.wait_ge(rope_done, ropes_tiles[i])
                        eng.wait_ge(mm, tiles_before[i] + t + 1)
                        eng.activation(sq[:, off:off + n], src, ACT.Square).then_inc(xg_ready, 1)
                        eng.activation(xg[:, off:off + n], src, ACT.Copy, scale=j.a.gain).then_inc(free[i % 2], 1)
                    elif j.kind == "up":
                        q = order[i, t]
                        if q >= 3:
                            eng.wait_ge(he_ready, q - 2)
                        eng.wait_ge(mm, tiles_before[i] + t + 1)
                        eng.activation(s1[:, off:off + n], src, ACT.Silu).then_inc(free[i % 2], 1)
                    elif j.kind == "he":
                        q = order[i, t]
                        if j.a.reuse is not None:
                            eng.wait_ge(mm, tiles_before[j.a.reuse + 1])
                        eng.wait_ge(he_ready, q + 1)
                        eng.activation(hhi[:, j.a.slot, off:off + n], h2[:, 0:n], ACT.Copy).then_inc(he_hi, 1)
                    elif j.kind == "gate" and j.a.last:
                        eng.wait_ge(gated, 6 * j.a.f + 3 + t + 1)
                        eng.activation(halves(j.a.hi[:, j.a.f, off:off + n]), merged(t, n), ACT.Copy).then_inc(m_hi, 1)
                if j.kind == "store":
                    store(i)
            if jobs[-1].kind == "rope":
                roots(NJ - 1)
                store(NJ - 1)
            for b in range(2):
                if len(storing) > b:
                    eng.wait_ge(out_stored[b], 16 * ((len(storing) - b + 1) // 2))

        @block.vector
        def _(eng):
            chain = Chain(eng, steps)

            def split_w(w):
                eng.wait_ge(w_hi, w + 1)
                eng.tensor_tensor(wlo[:, w % 2, :], stage[:, w % NSTG, :], whi[:, w % 2, :].bitcast(F32),
                                  ALU.subtract).then_inc(w_lo, 1)
            for w in range(min(2, NW)):
                split_w(w)
            if "rope" in kinds:
                eng.wait_ge(tab_in, 16)
            n_hi, n_gated = [0], [0]
            for i, j in enumerate(jobs):
                if last_job[j.w] == i and j.w + 2 < NW:
                    split_w(j.w + 2)
                a = acc[i % 2]
                for t, (off, n) in enumerate(j.tiles):
                    src = a[:, t, 0:n]
                    if j.kind == "resid":
                        eng.wait_ge(mm, tiles_before[i] + t + 1)
                        xs = E.X[:, j.a.f, X0 + off:X0 + off + n]
                        eng.scalar_tensor_tensor(xs, src, j.a.gate_of(t), xs, ALU.mult, ALU.add).then_inc(free[i % 2], 1)
                    elif j.kind in ("add", "down"):
                        eng.wait_ge(mm, tiles_before[i] + t + 1)
                        xs = E.X[:, j.a.f, off:off + n]
                        q = order.get((i, t), 0)
                        eng.tensor_tensor(xs, src, xs, ALU.add).then_inc(free[i % 2], 1)
                    elif j.kind == "rope":
                        r = ropes_tiles[i] + t
                        if t == 0 and turn[i] >= 2:
                            eng.wait_ge(out_stored[turn[i] % 2], 16 * (turn[i] // 2))
                        eng.wait_ge(aux_done, r + 1)
                        out = outb[:, turn[i] % 2, off:off + n]
                        if off < T:
                            eng.tensor_tensor(t2[:, 0:n], aux[1][:, 0:n], tab[:, 1, off:off + n], ALU.mult)
                            chain(eng.tensor_tensor(t1[:, 0:n], xg[:, off:off + n], tab[:, 0, off:off + n], ALU.mult))
                            chain(eng.tensor_tensor(t1[:, 0:n], t1[:, 0:n], t2[:, 0:n], ALU.add))
                        eng.wait_ge(rs_ready, r + 1)
                        if off < T:
                            ins = eng.tensor_tensor(out, t1[:, 0:n], rs[:, 0:n], ALU.mult)
                        else:
                            ins = eng.tensor_tensor(out, xg[:, off:off + n], rs[:, 0:n], ALU.mult)
                        ins.then_inc(rope_done, 1)
                    elif j.kind == "he":
                        q = order[i, t]
                        e = q // 6
                        eng.wait_ge(mm, tiles_before[i] + t + 1)
                        eng.wait_ge(free[1 - i % 2], free_before[i - 1] + t + 1)
                        if q % 6 == 0:
                            eng.wait_ge(cb_in[e % 2], 16 * (e // 2 + 1))
                        if q >= 1:
                            eng.wait_ge(he_lo, q)
                        ins = eng.tensor_tensor(h2[:, 0:n], src, s1[:, off:off + n], ALU.mult)
                        ins.then_inc(free[i % 2], 1)
                        eng.wait_ge(free[i % 2], free_before[i] + t + 1)
                        eng.tensor_tensor(h2[:, 0:n], h2[:, 0:n], cb[:, e % 2, off:off + n], ALU.mult).then_inc(he_ready, 1)
                        eng.wait_ge(he_hi, q + 1)
                        eng.tensor_tensor(hlo[:, j.a.slot, off:off + n], h2[:, 0:n],
                                          hhi[:, j.a.slot, off:off + n].bitcast(F32), ALU.subtract).then_inc(he_lo, 1)
                    elif j.kind == "gate":
                        q = order[i, t]
                        g = q // 3
                        eng.wait_ge(mm, tiles_before[i] + t + 1)
                        eng.wait_ge(gate_in[t], 16 * (g + 1))
                        m, gate, x = merged(t, n), halves(gt[:, t, 0:n]), halves(src)
                        if j.a.first:
                            if q >= 9:
                                eng.wait_ge(m_lo, q // 9 * 3 - 3 + t + 1)
                            eng.tensor_tensor(m, x, gate, ALU.mult).then_inc(free[i % 2], 1)
                            eng.wait_ge(free[i % 2], free_before[i] + t + 1)
                        else:
                            if n_gated[0]:
                                eng.wait_ge(gated, n_gated[0])
                            n_gated[0] += 1
                            eng.tensor_tensor(halves(gtmp[:, 0:n]), x, gate, ALU.mult).then_inc(free[i % 2], 1)
                            eng.wait_ge(free[i % 2], free_before[i] + t + 1)
                            eng.tensor_tensor(m, m, halves(gtmp[:, 0:n]), ALU.add).then_inc(gated, 1)
                        if j.a.last:
                            n_hi[0] += 1
                            eng.wait_ge(m_hi, n_hi[0])
                            eng.tensor_tensor(halves(j.a.lo[:, j.a.f, off:off + n]), m,
                                              halves(j.a.hi[:, j.a.f, off:off + n]).bitcast(F32),
                                              ALU.subtract).then_inc(m_lo, 1)

        @block.tensor
        def _(eng):
            pending = []

            def rope_aux(i, t):
                j = jobs[i]
                off, n = j.tiles[t]
                r = ropes_tiles[i] + t
                eng.wait_ge(free[i % 2], free_before[i] + t + 1)
                if r >= 1:
                    eng.wait_ge(rope_done, r)
                if off < T:
                    eng.matmul(aux[1][:, 0:n], col(E.con, CONST_AT, "rot"), xg[:, off:off + n],
                               start=True, stop=True)
                eng.matmul(aux[0][:, 0:n], col(E.con, CONST_AT, "headones"), sq[:, off:off + n],
                           start=True, stop=True).then_inc(aux_done, 1)

            for i, j in enumerate(jobs):
                a = acc[i % 2]
                eng.wait_ge(w_lo, j.w + 1)
                if i >= 2:
                    eng.wait_ge(free[i % 2], free_before[i])
                if j.kind == "down":
                    eng.wait_ge(he_lo, j.a.needs)
                hi, lo, c0 = j.rhs
                nk = j.k1 - j.k0
                for k in range(nk):
                    kb = (j.k0 + k) * P
                    for lhs, rhs in ((whi, hi), (whi, lo), (wlo, hi)):
                        first, last = k == 0 and lhs is whi and rhs is hi, k == nk - 1 and lhs is wlo
                        for t, (off, n) in enumerate(j.tiles):
                            mmi = eng.matmul(a[:, t, 0:n], lhs[:, j.w % 2, kb:kb + P],
                                             rhs[:, c0 + k, off:off + n], start=first, stop=last)
                            if last:
                                mmi.then_inc(mm, 1)
                    if k % 2 == 1 and pending:
                        rope_aux(*pending.pop(0))
                while pending:
                    rope_aux(*pending.pop(0))
                if j.kind == "rope":
                    pending = [(i, t) for t in range(len(j.tiles))]
            while pending:
                rope_aux(*pending.pop(0))


def split_phase(nc, src_dram, n_chunks, width, hi, lo):
    with ExitStack() as ctx:
        sb, ps, sem = phase(nc, ctx)
        stage = sb("stage", [P, 3, width])
        loaded = [sem(f"loaded{i}") for i in range(3)]
        rounded, split = sem("rounded"), sem("split")
        block = ctx.enter_context(nc.Block())

        @block.sync
        def _(eng):
            for c in range(n_chunks):
                if c >= 3:
                    eng.wait_ge(split, c - 2)
                eng.dma_start(stage[:, c % 3, :], src_dram(c)).then_inc(loaded[c % 3], 16)

        @block.scalar
        def _(eng):
            for c in range(n_chunks):
                eng.wait_ge(loaded[c % 3], 16 * (c // 3 + 1))
                eng.activation(hi[:, c, 0:width], stage[:, c % 3, :], ACT.Copy).then_inc(rounded, 1)

        @block.vector
        def _(eng):
            for c in range(n_chunks):
                eng.wait_ge(rounded, c + 1)
                eng.tensor_tensor(lo[:, c, 0:width], stage[:, c % 3, :], hi[:, c, 0:width].bitcast(F32),
                                  ALU.subtract).then_inc(split, 1)


class Unit:
    def __init__(self, side, q0, blocks, masks=()):
        self.side, self.q0, self.blocks, self.masks = side, q0, blocks, dict(masks)
        self.at, n = [], 0
        for _, w in blocks:
            self.at.append(n)
            n += w
        self.width = n
        self.segs = []
        for at, (tok, w) in zip(self.at, blocks):
            last = self.segs[-1] if self.segs else None
            if last and last[1] + last[2] == tok and last[0] // 512 == (at + w - 1) // 512:
                self.segs[-1] = (last[0], last[1], last[2] + w)
            else:
                self.segs.append((at, tok, w))


class Chunk:
    def __init__(self, q, k, v, gate, out, units, sinks=None, frow=None, vcols=None, kv_same=False):
        self.q, self.k, self.v, self.gate, self.out, self.units = q, k, v, gate, out, units
        self.sinks, self.frow, self.vcols, self.kv_same = sinks, frow, vcols, kv_same


def attention_phase(nc, E, NT, chunks, mode):
    diff, fox, sink = mode == "diff", mode == "fox", mode == "sink"
    with ExitStack() as ctx:
        sb, ps, sem = phase(nc, ctx)
        WMAX = max(u.width for c in chunks for u in c.units)
        NB = -(-NT // P)
        NC = len(chunks)
        qraw, kraw, vraw = sb("q_raw", [P, 2, NT]), sb("k_raw", [P, 2, NT]), sb("v_raw", [P, NT])
        qs, kh, kl = (sb(n, [P, 2, 2, NT], F32R) for n in ("q_stack", "k_hi", "k_lo"))
        if fox:
            q2 = sb("q_rows", [P, 2, 2, NT], F32R)
        LR = 68 if fox else 64
        v = sb("v", [P, NB, P])
        if not fox:
            gate = sb("gate", [P, 2, NT])
        oT = sb("o_t", [P, 2, NT])
        pr = sb("probs", [P, 2, WMAX])
        if diff:
            wd = sb("diff_w", [P, WMAX])
        pT = sb("probs_t", [P, 2, WMAX if WMAX % P == 0 else (WMAX // P + 1) * P])
        on = sb("o_n", [P, 4, P])
        osq = sb("o_sq", [P, P])
        st = sb("stats", [P, 2, 4])
        un = sb("unit_stats", [P, 4, 4])
        SBK = -(-WMAX // 512)
        NTB = 4 - SBK
        S = [ps(f"scores{i}", [P, SBK * 512]) for i in range(2)]
        TB = [ps(f"transposed{i}", [P, 512]) for i in range(NTB)]
        OB = [ps(f"outputs{i}", [P, 512]) for i in range(NTB)]
        (raw_in, v_in, hi_ready, lo_ready, scored, maxed, exped, sinked, w_ready, t_done, pv_done,
         on_ready, out_ready, rows_in, steps) = (
            sem(n) for n in ("qk_loaded", "v_loaded", "hi_ready", "lo_ready", "scored", "max_ready", "exp_ready",
                             "sink_ready", "diff_ready", "transposed", "pv_done", "o_n_ready",
                             "out_ready", "gp_rows_loaded", "dve_steps"))
        o_read = sem("o_read")
        copied = [sem(f"transposed_copied{i}") for i in range(NTB)]
        ss_ready, ms_ready, root_ready = sem("o_square_ready"), sem("o_mean_ready"), sem("o_root_ready")
        gate_in = [sem(f"gate_loaded{i}") for i in range(2)]
        stored = [sem(f"gp_stored{i}") for i in range(2)]
        block = ctx.enter_context(nc.Block())

        units = [(c, u) for c, ch in enumerate(chunks) for u in ch.units]
        NU = len(units)
        per = 2 if diff else 1
        per_out = 1 if diff else 2
        dv = P if diff else HD
        first_unit = [sum(len(ch.units) for ch in chunks[:c]) for c in range(NC + 1)]
        outs_before = [n // per_out for n in first_unit]
        NO = NU // per_out
        LAG = 2

        def outputs_after(i):
            if (i + 1) % per_out:
                return []
            m = (i + 1) // per_out - 1
            return ([m - LAG] if m >= LAG else []) + (list(range(NO - LAG, NO)) if m == NO - 1 else [])

        NG = -(-NB // 4)
        groups = [[list(range(g, min(g + 4, len(u.blocks)))) for g in range(0, len(u.blocks), 4)] for _, u in units]
        group_no, v_group_no, o_group_no, n = {}, {}, {}, 0
        for i, (c, u) in enumerate(units):
            if i == first_unit[c]:
                v_group_no[c] = n
                n += NG
            for g in range(len(groups[i])):
                group_no[i, g] = n
                n += 1
            for m in outputs_after(i):
                o_group_no[m] = n
                n += 1

        def by_vector(g):
            return not diff and g % 2 == 1

        @block.sync
        def _(eng):
            for c, ch in enumerate(chunks):
                if c >= 1:
                    eng.wait_ge(lo_ready, 4 * c)
                for a in range(2):
                    for half in range(2):
                        rows = slice(64 * half, 64 * half + 64)
                        eng.dma_start(qraw[rows, a, :], ch.q[a]).then_inc(raw_in, 16)
                        eng.dma_start(kraw[rows, a, :], ch.k[a]).then_inc(raw_in, 16)
                if c >= 1:
                    eng.wait_ge(t_done, v_group_no[c - 1] + NG)
                eng.dma_start(vraw[:], ch.v).then_inc(v_in, 16)
                if not fox:
                    if c >= 2:
                        eng.wait_ge(out_ready, outs_before[c - 1])
                    eng.dma_start(gate[:, c % 2, :], ch.gate).then_inc(gate_in[c % 2], 16)
                eng.wait_ge(raw_in, 128 * (c + 1))
                eng.wait_ge(v_in, 16 * (c + 1))

        @block.gpsimd
        def _(eng):
            def rows(c):
                if c >= 2:
                    eng.wait_ge(scored, first_unit[c - 1])
                for a in range(2):
                    f, one, nf = chunks[c].frow[a]
                    eng.dma_start(q2[64:66, c % 2, a, :], f).then_inc(rows_in, 16)
                    eng.dma_start(q2[66:68, c % 2, a, :], one).then_inc(rows_in, 16)
                    eng.dma_start(kl[64:66, c % 2, a, :], one).then_inc(rows_in, 16)
                    eng.dma_start(kl[66:68, c % 2, a, :], nf).then_inc(rows_in, 16)
                eng.wait_ge(rows_in, 128 * (c + 1))
            if fox:
                rows(0)
            for c, ch in enumerate(chunks):
                if fox and c + 1 < NC:
                    rows(c + 1)
                eng.wait_ge(out_ready, outs_before[c + 1])
                eng.dma_start(ch.out, oT[:, c % 2, :]).then_inc(stored[c % 2], 16)
            for b in range(2):
                if NC > b:
                    eng.wait_ge(stored[b], 16 * ((NC - b + 1) // 2))

        def softmaxes(i):
            return [(2 * i + a, a) for a in range(2)] if diff else [(i, units[i][1].side)]

        def copy_group(eng, copy, i, g):
            u = units[i][1]
            eng.wait_ge(t_done, group_no[i, g] + 1)
            full = [b for b in groups[i][g] if u.blocks[b][1] == P]
            b0 = groups[i][g][0]
            T1 = TB[group_no[i, g] % NTB]
            ins = None
            if full:
                ins = copy(pT[:, i % 2, b0 * P:(b0 + len(full)) * P], T1[:, 0:len(full) * P])
            for b in groups[i][g][len(full):]:
                w, at = u.blocks[b][1], (b - b0) * P
                ins = copy(pT[0:w, i % 2, b * P:b * P + P], T1[0:w, at:at + P])
            ins.then_inc(copied[group_no[i, g] % NTB], 1)

        @block.scalar
        def _(eng):
            def copy(out, in_):
                return eng.activation(out, in_, ACT.Copy)

            def round_qk(c):
                eng.wait_ge(raw_in, 128 * (c + 1))
                if c >= 2:
                    eng.wait_ge(scored, per * first_unit[c - 1])
                for a in range(2):
                    if fox:
                        copy(q2[0:64, c % 2, a, :], qraw[0:64, a, :])
                    copy(qs[:, c % 2, a, :], qraw[:, a, :]).then_inc(hi_ready, 1)
                    copy(kh[:, c % 2, a, :], kraw[:, a, :]).then_inc(hi_ready, 1)

            def exps(i):
                c, u = units[i]
                for q, a in softmaxes(i):
                    eng.wait_ge(maxed, q + 1)
                    if diff and i >= 1:
                        eng.wait_ge(w_ready, i)
                    if not diff and i >= 2:
                        eng.wait_ge(t_done, group_no[i - 2, len(groups[i - 2]) - 1] + 1)
                    eng.activation(pr[:, q % 2, 0:u.width], S[q % 2][:, 0:u.width], ACT.Exp,
                                   bias=st[:, q % 2, 1:2], scale=SCALE,
                                   accum_out=st[:, q % 2, 2:3]).then_inc(exped, 1)
                    if sink:
                        eng.activation(st[:, q % 2, 3:4], col(E.par, PARAM_AT, "sink", chunks[c].sinks[a]),
                                       ACT.Exp, bias=st[:, q % 2, 1:2]).then_inc(sinked, 1)

            round_qk(0)
            exps(0)
            for i in range(NU):
                c = units[i][0]
                if i == first_unit[c] and c + 1 < NC:
                    round_qk(c + 1)
                for g in range(len(groups[i])):
                    if not by_vector(g):
                        copy_group(eng, copy, i, g)
                if i + 1 < NU:
                    exps(i + 1)
                if diff:
                    r = un[:, i % 4, 3:4]
                    eng.wait_ge(ss_ready, i + 1)
                    eng.activation(r, r, ACT.Ln, scale=1.0 / P, bias=E.eps[:]).then_inc(ms_ready, 1)
                    eng.wait_ge(ms_ready, i + 1)
                    eng.activation(r, r, ACT.Exp, scale=-0.5).then_inc(root_ready, 1)

        @block.vector
        def _(eng):
            chain = Chain(eng, steps)

            def split_qk(c):
                for a in range(2):
                    eng.wait_ge(hi_ready, 4 * c + 2 * a + 1)
                    up = qs[64:128, c % 2, a, :]
                    eng.tensor_tensor(up, qraw[64:128, a, :], up.bitcast(F32), ALU.subtract).then_inc(lo_ready, 1)
                    eng.wait_ge(hi_ready, 4 * c + 2 * a + 2)
                    eng.tensor_tensor(kl[0:64, c % 2, a, :], kraw[0:64, a, :],
                                      kh[0:64, c % 2, a, :].bitcast(F32), ALU.subtract).then_inc(lo_ready, 1)

            def maxes(i):
                u = units[i][1]
                for q, a in softmaxes(i):
                    eng.wait_ge(scored, q + 1)
                    if q >= 2:
                        eng.wait_ge(exped, q - 1)
                        if sink:
                            eng.wait_ge(sinked, q - 1)
                    chain(eng.tensor_reduce(st[:, q % 2, 0:1], S[q % 2][:, 0:u.width], AX, ALU.max))
                    if sink:
                        h = chunks[units[i][0]].sinks[a]
                        ins = eng.tensor_scalar(st[:, q % 2, 1:2], st[:, q % 2, 0:1], -SCALE,
                                                E.nsink[:, h:h + 1], ALU.mult, ALU.min)
                    else:
                        ins = eng.tensor_scalar(st[:, q % 2, 1:2], st[:, q % 2, 0:1], -SCALE, None, ALU.mult)
                    ins.then_inc(maxed, 1)

            def weights(i):
                u, r = units[i][1], un[:, i % 4, :]
                eng.wait_ge(exped, per * (i + 1))
                if diff:
                    chain(eng.reciprocal(r[:, 0:1], st[:, 1, 2:3]))
                    chain(eng.scalar_tensor_tensor(r[:, 1:2], st[:, 0, 2:3], E.neglam[:], r[:, 0:1], ALU.mult, ALU.mult))
                    if i >= 1:
                        eng.wait_ge(t_done, group_no[i - 1, len(groups[i - 1]) - 1] + 1)
                    chain(eng.reciprocal(r[:, 2:3], st[:, 0, 2:3]))
                    eng.scalar_tensor_tensor(wd[:, 0:u.width], pr[:, 1, 0:u.width], r[:, 1:2], pr[:, 0, 0:u.width],
                                             ALU.mult, ALU.add).then_inc(w_ready, 1)
                elif sink:
                    eng.wait_ge(sinked, i + 1)
                    chain(eng.tensor_tensor(r[:, 1:2], st[:, i % 2, 2:3], st[:, i % 2, 3:4], ALU.add))
                    chain(eng.reciprocal(r[:, 2:3], r[:, 1:2]))
                else:
                    chain(eng.reciprocal(r[:, 2:3], st[:, i % 2, 2:3]))

            def output(m):
                i = per_out * m
                eng.wait_ge(pv_done, i + per_out)
                if m >= 4:
                    eng.wait_ge(t_done, o_group_no[m - 4] + 1)
                for n in range(per_out):
                    at = HD * units[i + n][1].side
                    dst = on[:, m % 4, at:at + dv]
                    ins = eng.tensor_scalar(dst, OB[m % NTB][:, at:at + dv], un[:, (i + n) % 4, 2:3], None, ALU.mult)
                ins.then_inc(o_read, 1)
                if not diff:
                    return
                eng.wait_ge(o_read, m + 1)
                eng.scalar_tensor_tensor(osq[:], dst, 1.0, dst, ALU.mult, ALU.mult,
                                         accum_out=un[:, i % 4, 3:4]).then_inc(ss_ready, 1)

            def normalise(i):
                eng.wait_ge(root_ready, i + 1)
                dst = on[:, i % 4, :]
                eng.tensor_scalar(dst, dst, un[:, i % 4, 3:4], None, ALU.mult).then_inc(on_ready, 1)

            def finish(m):
                c, u = units[m * per_out]
                g = o_group_no[m]
                eng.wait_ge(t_done, g + 1)
                if m == outs_before[c]:
                    if c >= 2:
                        eng.wait_ge(stored[c % 2], 16 * (c // 2))
                    if not fox:
                        eng.wait_ge(gate_in[c % 2], 16 * (c // 2 + 1))
                src = TB[g % NTB][:, 0:P]
                dst = oT[:, c % 2, u.q0:u.q0 + P]
                if fox:
                    ins = eng.tensor_copy(dst, src)
                elif sink:
                    ins = eng.tensor_tensor(dst, src, gate[:, c % 2, u.q0:u.q0 + P], ALU.mult)
                else:
                    ins = eng.scalar_tensor_tensor(dst, src, E.subln[:], gate[:, c % 2, u.q0:u.q0 + P],
                                                   ALU.mult, ALU.mult)
                ins.then_inc(copied[g % NTB], 1)
                eng.wait_ge(copied[g % NTB], g // NTB + 1)
                eng.engine_nop().then_inc(out_ready, 1)

            def values(c):
                for g in range(NG):
                    eng.wait_ge(t_done, v_group_no[c] + g + 1)
                    T1 = TB[(v_group_no[c] + g) % NTB]
                    nb = min(4, NB - 4 * g)
                    rest = NT - 4 * g * P
                    full = min(nb, rest // P)
                    ins = None
                    if full:
                        ins = eng.tensor_copy(v[:, 4 * g:4 * g + full, :],
                                              T1[:, 0:full * P].rearrange("p (b f) -> p b f", f=P))
                    if full < nb:
                        w = rest - full * P
                        ins = eng.tensor_copy(v[0:w, 4 * g + full, :], T1[0:w, full * P:(full + 1) * P])
                    ins.then_inc(copied[(v_group_no[c] + g) % NTB], 1)

            if diff:
                chain(eng.tensor_scalar(E.subln[:], col(E.par, PARAM_AT, "subln"), 1.0 - LAMBDA_INIT, None, ALU.mult))
            split_qk(0)
            maxes(0)
            for i in range(NU):
                c = units[i][0]
                weights(i)
                if i == first_unit[c]:
                    if c + 1 < NC:
                        split_qk(c + 1)
                if i + 1 < NU:
                    maxes(i + 1)
                if i == first_unit[c]:
                    values(c)
                for g in range(len(groups[i])):
                    if by_vector(g):
                        copy_group(eng, eng.tensor_copy, i, g)
                if (i + 1) % per_out == 0:
                    output(i // per_out)
                if diff and i >= 1:
                    normalise(i - 1)
                if diff and i == NU - 1:
                    normalise(i)
                for m in outputs_after(i):
                    finish(m)

        @block.tensor
        def _(eng):
            def scores(i):
                c, u = units[i]
                if i == first_unit[c]:
                    eng.wait_ge(lo_ready, 4 * (c + 1))
                    eng.wait_ge(hi_ready, 4 * (c + 1))
                    if fox:
                        eng.wait_ge(rows_in, 128 * (c + 1))
                for q, a in softmaxes(i):
                    if q >= 2:
                        eng.wait_ge(exped, q - 1)
                    s, sl = S[q % 2], c % 2
                    second = q2 if fox else qs
                    qcols = slice(u.q0, u.q0 + P)
                    masks = {u.at[b]: m for b, m in u.masks.items()}
                    for at, tok, w in u.segs:
                        inside = [(p0, m) for p0, m in masks.items() if at <= p0 < at + w]
                        eng.matmul(s[:, at:at + w], qs[:, sl, a, qcols], kh[:, sl, a, tok:tok + w],
                                   start=True, stop=False)
                        for p0, (m0, mw) in inside:
                            eng.matmul(s[:, p0:p0 + mw], E.mask[:, 0:P], E.mask[:, m0:m0 + mw], start=False,
                                       stop=False, skip_group_check=True)
                        mmi = eng.matmul(s[:, at:at + w], second[0:LR, sl, a, qcols], kl[0:LR, sl, a, tok:tok + w],
                                         start=False, stop=True)
                    mmi.then_inc(scored, 1)

            def transpose_group(number, parts):
                if number >= NTB:
                    eng.wait_ge(copied[number % NTB], number // NTB)
                for dst, src in parts:
                    ins = eng.transpose(dst, src, col(E.con, CONST_AT, "ident"))
                ins.then_inc(t_done, 1)

            def values(c):
                eng.wait_ge(v_in, 16 * (c + 1))
                for g in range(NG):
                    parts = []
                    T1 = TB[(v_group_no[c] + g) % NTB]
                    for b in range(4 * g, min(4 * g + 4, NB)):
                        w = min(P, NT - b * P)
                        parts.append((T1[0:w, (b - 4 * g) * P:(b - 4 * g + 1) * P], vraw[:, b * P:b * P + w]))
                    transpose_group(v_group_no[c] + g, parts)

            def weights_t(i, g):
                u = units[i][1]
                src = wd[:, :] if diff else pr[:, i % 2, :]
                if g == 0:
                    if diff:
                        eng.wait_ge(w_ready, i + 1)
                    else:
                        eng.wait_ge(exped, i + 1)
                b0 = groups[i][g][0]
                T1 = TB[group_no[i, g] % NTB]
                transpose_group(group_no[i, g], [
                    (T1[0:u.blocks[b][1], (b - b0) * P:(b - b0 + 1) * P], src[:, u.at[b]:u.at[b] + u.blocks[b][1]])
                    for b in groups[i][g]])

            def pv(i, g):
                c, u = units[i]
                m = i // per_out
                o0 = HD * u.side
                n = group_no[i, g]
                vc = 0 if diff else chunks[c].vcols[u.side]
                if g == 0 and i == first_unit[c]:
                    for vg in range(v_group_no[c], v_group_no[c] + NG):
                        eng.wait_ge(copied[vg % NTB], vg // NTB + 1)
                eng.wait_ge(copied[n % NTB], n // NTB + 1)
                if g == 0 and m >= NTB:
                    eng.wait_ge(o_read, m - NTB + 1)
                nb = len(u.blocks)
                for b in groups[i][g]:
                    tok, w = u.blocks[b]
                    ins = eng.matmul(OB[m % NTB][:, o0:o0 + dv], pT[0:w, i % 2, b * P:(b + 1) * P],
                                     v[0:w, tok // P, vc:vc + dv], start=b == 0, stop=b == nb - 1)
                if g == len(groups[i]) - 1:
                    ins.then_inc(pv_done, 1)

            def output_t(m):
                eng.wait_ge(on_ready if diff else o_read, m + 1)
                transpose_group(o_group_no[m], [(TB[o_group_no[m] % NTB][:, 0:P], on[:, m % 4, :])])

            scores(0)
            for i in range(NU):
                c = units[i][0]
                if i + 1 < NU:
                    scores(i + 1)
                if i == first_unit[c]:
                    values(c)
                weights_t(i, 0)
                for g in range(len(groups[i])):
                    if g + 1 < len(groups[i]):
                        weights_t(i, g + 1)
                    pv(i, g)
                for m in outputs_after(i):
                    output_t(m)


def gla_phase(nc, E, dram):
    with ExitStack() as ctx:
        sb, ps, sem = phase(nc, ctx)
        NP_, NCH, NXC, NCC = T // P, NT1 // GC, T // GC, CTX // GC
        NBK = NT1 // P
        NS = NCH - 1
        ISC = 1.0 / 16.0
        reset = sb("reset", [P, NT1])
        r = sb("rank", [48, NT1])
        wa = sb("wa", [48, GH * GDK])
        q, k, vraw, gate = sb("q", [P, T]), sb("k", [P, NT1]), sb("v_raw", [P, 2, NT1]), sb("gate", [P, 2, T])
        v = sb("v", [P, NBK, GDV])
        M, A, CUM = sb("log_decay", [P, NT1]), sb("expo", [P, NT1]), sb("cum", [P, NT1])
        bl, dec = sb("chunk_total", [P, 2, NCH]), sb("chunk_decay", [P, 2, NCH])
        QD, KD = sb("q_decayed", [P, 2, T]), sb("k_decayed", [P, 2, T])
        K2, K2T = sb("k_to_end", [P, NT1]), sb("k_to_end_t", [P, 2, NBK, GDK])
        ST = sb("states", [P, 2, NXC, GDV])
        RUN = sb("ctx_state", [P, 2, GDV])
        AT = sb("att", [P, 2, 2, P])
        ATS = sb("att_sum", [P, 2, P])
        OX = sb("o", [P, 2, T])
        sq, rs = sb("o_sq", [P, 2, 512]), sb("rstd", [P, 2, 512])
        Z = ps("z", [P, 3, 512])
        TR = ps("tr", [P, 512])
        AB, OPB = [ps(f"state_att{i}", [P, 512]) for i in range(2)], [ps(f"o_p{i}", [P, 512]) for i in range(2)]
        (base_in, qk_in, v_in, gate_in, z_done, z_copied, ln_done, cum_done, e_done, kq_done, t_done,
         t_copied, ds_done, state_done, att_done, att_ready, o_done, o_copied, sq_done, ss_done, rs_done,
         out_done, stored, steps, asteps, ms_ready) = (sem(n) for n in (
             "base_loaded", "qk_loaded", "v_loaded", "gate_loaded", "z_done", "z_copied", "ln_done",
             "cum_done", "exps_done", "kq_done", "t_done", "t_copied", "ds_done", "state_done", "att_done",
             "att_ready", "o_done", "o_copied", "sq_done", "ss_done", "rs_done", "out_done", "gp_stored", "dve_steps",
             "act_steps", "mean_square_ready"))
        block = ctx.enter_context(nc.Block())
        NVG, NKG = 5, 3
        TG = NVG + 2 * NKG

        @block.sync
        def _(eng):
            eng.dma_start(reset[:], dram["reset"]).then_inc(base_in, 16)
            eng.dma_start(r[0:16, :], dram["rank"][0:16, :]).then_inc(base_in, 16)
            eng.dma_start(r[32:48, :], dram["rank"][16:32, :]).then_inc(base_in, 16)
            eng.dma_start(wa[0:16, :], dram["wa_f"]).then_inc(base_in, 16)
            eng.dma_start(wa[32:48, :], dram["wa_b"]).then_inc(base_in, 16)
            for h in range(GH):
                if h >= 1:
                    eng.wait_ge(kq_done, 2 * h)
                eng.dma_start(q[:], dram["q"](h)).then_inc(qk_in, 16)
                eng.dma_start(k[:], dram["k"](h)).then_inc(qk_in, 16)
                if h >= 1:
                    eng.wait_ge(t_done, TG * (h - 1) + NVG)
                eng.dma_start(vraw[:], dram["v"](h)).then_inc(v_in, 16)
                if h >= 1:
                    eng.wait_ge(out_done, 4 * h)
                eng.dma_start(gate[:], dram["gate"](h)).then_inc(gate_in, 16)
                eng.wait_ge(qk_in, 32 * (h + 1))

        @block.gpsimd
        def _(eng):
            for h in range(GH):
                eng.wait_ge(out_done, 4 * (h + 1))
                eng.dma_start(dram["out"](h), OX[:]).then_inc(stored, 16)
            eng.wait_ge(stored, 16 * GH)

        @block.scalar
        def _(eng):
            chain = Chain(eng, asteps)

            def zs(g):
                h, d = divmod(g, 2)
                eng.wait_ge(z_done, g + 1)
                if g >= 1:
                    eng.wait_ge(kq_done, g)
                eng.activation(M[:], Z[:].rearrange("p b n -> p (b n)")[:, 0:NT1], ACT.Identity,
                               bias=col(E.par, PARAM_AT, "ba", 4 * d + h)).then_inc(z_copied, 1)
                eng.wait_ge(z_copied, g + 1)
                chain(eng.activation(A[:], M[:], ACT.Abs))
                chain(eng.activation(A[:], A[:], ACT.Exp, scale=-1.0))
                eng.activation(A[:], A[:], ACT.Ln, bias=1.0).then_inc(ln_done, 1)
                eng.wait_ge(cum_done, g + 1)
                eng.activation(A[:, 0:T], CUM[:, 0:T], ACT.Exp, scale=ISC)
                chain(eng.activation(M[:], M[:], ACT.Exp, scale=ISC))
                if h >= 1:
                    eng.wait_ge(state_done, NS * (2 * (h - 1) + d + 1))
                eng.activation(dec[:, d, :], bl[:, d, :], ACT.Exp, scale=ISC)
                eng.activation(CUM[:, 0:T], CUM[:, 0:T], ACT.Exp, scale=-ISC).then_inc(e_done, 1)

            def outs(h):
                for p in range(NP_):
                    n = h * NP_ + p
                    eng.wait_ge(o_done, n + 1)
                    if p == 0 and h >= 1:
                        eng.wait_ge(stored, 16 * h)
                    eng.activation(OX[:, :, p * P:(p + 1) * P],
                                   OPB[n % 2][:, 0:256].rearrange("p (e c) -> p e c", e=2),
                                   ACT.Copy).then_inc(o_copied, 1)
                for t in range(2):
                    for e in range(2):
                        n = 4 * h + 2 * t + e
                        if n >= 2:
                            eng.wait_ge(ss_done, n - 1)
                        eng.wait_ge(o_copied, NP_ * (h + 1))
                        eng.activation(sq[:, e, :], OX[:, e, 512 * t:512 * t + 512], ACT.Square).then_inc(sq_done, 1)
                for t in range(2):
                    n = 2 * h + t
                    eng.wait_ge(ss_done, 4 * h + 2 * t + 2)
                    eng.activation(rs[:, t, :], Z[:, t, :], ACT.Ln, scale=1.0 / GDV, bias=E.eps[:]).then_inc(ms_ready, 1)
                    eng.wait_ge(ms_ready, n + 1)
                    eng.activation(rs[:, t, :], rs[:, t, :], ACT.Exp, scale=-0.5).then_inc(rs_done, 1)

            eng.wait_ge(base_in, 80)
            zs(0)
            zs(1)
            for h in range(GH):
                outs(h)
                if h + 1 < GH:
                    zs(2 * h + 2)
                    zs(2 * h + 3)

        @block.vector
        def _(eng):
            chain = Chain(eng, steps)
            chain(eng.memset(AT[:], 0.0))
            eng.wait_ge(base_in, 80)

            def decays(g):
                h, d = divmod(g, 2)
                eng.wait_ge(ln_done, g + 1)
                chain(eng.scalar_tensor_tensor(M[:], M[:], 0.0, A[:], ALU.min, ALU.subtract))
                if d == 0:
                    chain(eng.tensor_tensor_scan(CUM[:], reset[:], M[:], 0.0, ALU.mult, ALU.add))
                    tot = CUM[:, GC - 1:NT1:GC]
                else:
                    chain(eng.tensor_tensor_scan(CUM[:, ::-1], reset[:], M[:, ::-1], 0.0, ALU.mult, ALU.add))
                    tot = CUM[:, 0:NT1:GC]
                chain(eng.tensor_copy(bl[:, d, :], tot))
                eng.tensor_tensor(M[:].rearrange("p (c t) -> p c t", t=GC),
                                  bl[:, d, :].unsqueeze(2).to_broadcast([P, NCH, GC]),
                                  CUM[:].rearrange("p (c t) -> p c t", t=GC), ALU.subtract).then_inc(cum_done, 1)
                eng.wait_ge(e_done, g + 1)
                if d == 0:
                    eng.wait_ge(qk_in, 32 * (h + 1))
                    if h >= 1:
                        eng.wait_ge(o_done, NP_ * h)
                eng.scalar_tensor_tensor(QD[:, d, :], q[:], GDK ** -0.5, A[:, 0:T], ALU.mult, ALU.mult)
                eng.tensor_tensor(KD[:, d, :], k[:, 0:T], CUM[:, 0:T], ALU.mult)
                if g >= 1:
                    eng.wait_ge(t_done, TG * ((g - 1) // 2) + NVG + NKG * ((g - 1) % 2 + 1))
                eng.tensor_tensor(K2[:], k[:], M[:], ALU.mult).then_inc(kq_done, 1)

            def copies(h, g0, n, dst):
                for g in range(n):
                    eng.wait_ge(t_done, TG * h + g0 + g + 1)
                    dst(g).then_inc(t_copied, 1)

            def values(h):
                def dst(g):
                    return eng.tensor_copy(v[:, 2 * g:2 * g + 2, :].rearrange("p b f -> p (b f)"), TR[:])
                copies(h, 0, NVG, dst)

            def keys(h, d):
                def dst(g):
                    nb = min(4, NBK - 4 * g)
                    return eng.tensor_copy(K2T[:, d, 4 * g:4 * g + nb, :].rearrange("p b f -> p (b f)"), TR[:, 0:nb * P])
                copies(h, NVG + NKG * d, NKG, dst)

            def states(h, d):
                for n, c in enumerate(chunk_order(d, NXC, NCC)[:NS]):
                    i = NS * (2 * h + d) + n
                    eng.wait_ge(ds_done, i + 1)
                    dsp = AB[i % 2][:, 0:256]
                    if n < NCC:
                        dst = RUN[:, n % 2, :] if n < NCC - 1 else ST[:, d, 0, :]
                        src = RUN[:, (n - 1) % 2, :]
                    else:
                        dst, src = ST[:, d, n - NCC + 1, :], ST[:, d, n - NCC, :]
                    if n == 0:
                        ins = eng.tensor_copy(dst, dsp)
                    else:
                        ins = eng.scalar_tensor_tensor(dst, src, dec[:, d, c:c + 1], dsp, ALU.mult, ALU.add)
                    ins.then_inc(state_done, 1)
                    eng.wait_ge(state_done, i + 1)

            def attend(h):
                for p in range(NP_):
                    n = h * NP_ + p
                    for d, m in enumerate(("causal", "anti")):
                        eng.wait_ge(att_done, 2 * n + 2)
                        at = AB[n % 2][:, 128 * d:128 * d + 128]
                        ins = eng.copy_predicated(AT[:, n % 2, d, :], col(E.con, CONST_AT, m).bitcast(mybir.dt.int32), at)
                        chain(ins)
                    if n >= 2:
                        eng.wait_ge(o_done, n - 1)
                    eng.tensor_tensor(ATS[:, n % 2, :], AT[:, n % 2, 0, :], AT[:, n % 2, 1, :], ALU.add).then_inc(att_ready, 1)

            def finish(h):
                for t in range(2):
                    eng.wait_ge(ss_done, 4 * h + 2 * t + 2)
                    eng.wait_ge(rs_done, 2 * h + t + 1)
                    if t == 0:
                        eng.wait_ge(gate_in, 16 * (h + 1))
                        eng.wait_ge(sq_done, 4 * (h + 1))
                    for e in range(2):
                        o = OX[:, e, 512 * t:512 * t + 512]
                        chain(eng.scalar_tensor_tensor(o, o, col(E.par, PARAM_AT, "out_norm", e), rs[:, t, :], ALU.mult, ALU.mult))
                        eng.tensor_tensor(o, o, gate[:, e, 512 * t:512 * t + 512], ALU.mult).then_inc(out_done, 1)

            for h in range(GH):
                values(h)
                for d in range(2):
                    decays(2 * h + d)
                    keys(h, d)
                for d in range(2):
                    states(h, d)
                attend(h)
                finish(h)

        @block.tensor
        def _(eng):
            ident = col(E.con, CONST_AT, "ident")

            def group(number, parts):
                if number >= 1:
                    eng.wait_ge(t_copied, number)
                for dst, src in parts:
                    ins = eng.transpose(dst, src, ident)
                ins.then_inc(t_done, 1)

            def z(g):
                h, d = divmod(g, 2)
                if g >= 1:
                    eng.wait_ge(z_copied, g)
                for t, (off, n) in enumerate(TILES1):
                    ins = eng.matmul(Z[:, t, 0:n], wa[32 * d:32 * d + 16, h * P:(h + 1) * P],
                                     r[32 * d:32 * d + 16, off:off + n], start=True, stop=True)
                ins.then_inc(z_done, 1)

            eng.wait_ge(base_in, 80)
            for h in range(GH):
                eng.wait_ge(v_in, 16 * (h + 1))
                for g in range(NVG):
                    group(TG * h + g, [(TR[:, (2 * b + e) * P:(2 * b + e + 1) * P],
                                        vraw[:, e, (2 * g + b) * P:(2 * g + b + 1) * P])
                                       for b in range(2) for e in range(2)])
                for d in range(2):
                    if h >= 1 and d == 0:
                        eng.wait_ge(out_done, 4 * h)
                    z(2 * h + d)
                    eng.wait_ge(kq_done, 2 * h + d + 1)
                    for g in range(NKG):
                        group(TG * h + NVG + NKG * d + g,
                              [(TR[:, (b - 4 * g) * P:(b - 4 * g + 1) * P], K2[:, b * P:(b + 1) * P])
                               for b in range(4 * g, min(4 * g + 4, NBK))])
                for d in range(2):
                    eng.wait_ge(t_copied, TG * h + NVG + NKG * (d + 1))
                    for n, c in enumerate(chunk_order(d, NXC, NCC)[:NS]):
                        i = NS * (2 * h + d) + n
                        if i >= 2:
                            eng.wait_ge(state_done, i - 1)
                        rows = slice(GC * (c % 2), GC * (c % 2) + GC)
                        eng.matmul(AB[i % 2][:, 0:256], K2T[rows, d, c // 2, :],
                                   v[rows, c // 2, :], start=True, stop=True).then_inc(ds_done, 1)

                def att(p):
                    n = h * NP_ + p
                    if n >= 2:
                        eng.wait_ge(att_ready, n - 1)
                    for d in range(2):
                        eng.matmul(AB[n % 2][:, 128 * d:128 * d + 128], KD[:, d, p * P:(p + 1) * P], QD[:, d, p * P:(p + 1) * P],
                                   start=True, stop=True).then_inc(att_done, 1)
                eng.wait_ge(state_done, NS * 2 * (h + 1))
                att(0)
                for p in range(NP_):
                    n = h * NP_ + p
                    if p + 1 < NP_:
                        att(p + 1)
                    eng.wait_ge(att_ready, n + 1)
                    if n >= 2:
                        eng.wait_ge(o_copied, n - 1)
                    for e in range(2):
                        o = OPB[n % 2][:, P * e:P * e + P]
                        es = slice(P * e, P * e + P)
                        eng.matmul(o, v[:, p, es], ATS[:, n % 2, :], start=True, stop=False, skip_group_check=True)
                        for j in range(2):
                            c = 2 * p + j
                            for d in range(2):
                                pos = c if d == 0 else NXC - 1 - c
                                ins = eng.matmul(o[:, GC * j:GC * j + GC], ST[:, d, pos, es],
                                                 QD[:, d, GC * c:GC * c + GC], start=False, stop=(j == 1 and d == 1),
                                                 skip_group_check=True)
                    ins.then_inc(o_done, 1)
                for t in range(2):
                    for e in range(2):
                        n = 4 * h + 2 * t + e
                        eng.wait_ge(sq_done, n + 1)
                        eng.matmul(Z[:, t, :], col(E.con, CONST_AT, "ones"), sq[:, e, :], start=(e == 0),
                                   stop=(e == 1)).then_inc(ss_done, 1)


def chunk_order(d, nx, nctx):
    if d == 0:
        return [nx + c for c in range(nctx)] + list(range(nx))
    return [nx + c for c in reversed(range(nctx))] + list(reversed(range(nx)))


def decay_phase(nc, E, fg_dram, rows_dram):
    H = 8
    with ExitStack() as ctx:
        sb, ps, sem = phase(nc, ctx)
        z, a, m = sb("fg", [H, L2]), sb("fg_a", [H, L2]), sb("fg_m", [H, L2])
        one = sb("one", [H, L2])
        o = sb("rows", [H, 6, L2], F32R)
        loaded, steps, act_done, f_done, out_done = (sem(n) for n in ("loaded", "dve_steps", "act_done", "f_done", "gp_stored"))
        block = ctx.enter_context(nc.Block())

        @block.sync
        def _(eng):
            eng.dma_start(z[:], fg_dram).then_inc(loaded, 16)

        @block.gpsimd
        def _(eng):
            eng.wait_ge(f_done, 1)
            eng.dma_start(rows_dram, o[:]).then_inc(out_done, 16)
            eng.wait_ge(out_done, 16)

        @block.scalar
        def _(eng):
            b = col(E.par, PARAM_AT, "bforget")[0:H, :]
            eng.wait_ge(loaded, 16)
            eng.activation(a[:], z[:], ACT.Abs, bias=b).then_inc(act_done, 1)
            eng.wait_ge(act_done, 1)
            eng.activation(a[:], a[:], ACT.Exp, scale=-1.0).then_inc(act_done, 1)
            eng.wait_ge(act_done, 2)
            eng.activation(a[:], a[:], ACT.Ln, bias=1.0).then_inc(act_done, 1)

        @block.vector
        def _(eng):
            chain = Chain(eng, steps)
            eng.wait_ge(loaded, 16)
            eng.memset(one[:], 1.0)
            chain(eng.tensor_scalar(m[:], z[:], col(E.par, PARAM_AT, "bforget")[0:H, :], 0.0, ALU.add, ALU.min))
            eng.wait_ge(act_done, 3)
            chain(eng.tensor_tensor(m[:], m[:], a[:], ALU.subtract))
            chain(eng.tensor_scalar(m[:], m[:], 1.0 / SCALE, None, ALU.mult))
            chain(eng.tensor_tensor_scan(a[:], one[:], m[:], 0.0, ALU.mult, ALU.add))
            chain(eng.tensor_copy(o[:, 0, :], a[:]))
            chain(eng.tensor_tensor(o[:, 1, :], a[:], o[:, 0, :].bitcast(F32), ALU.subtract))
            for j in range(2):
                chain(eng.tensor_copy(o[:, 2 + j, :], one[:]))
                chain(eng.tensor_scalar(o[:, 4 + j, :], o[:, j, :].bitcast(F32), -1.0, None, ALU.mult))
            eng.engine_nop().then_inc(f_done, 1)


def branch_phase(nc, E, dram, hi, lo):
    KS, PADW = 31, 30
    with ExitStack() as ctx:
        sb, ps, sem = phase(nc, ctx)
        a = sb("pool_in", [P, META + L2])
        win = sb("pool_sums", [P, 4, META + L2])
        diff = sb("pool_diff", [P, L2])
        pw = sb("pool_w", [P, 2, P])
        bv, bg = sb("conv_v", [P, L2]), sb("conv_g", [P, L2])
        glu = sb("glu", [P, PADW + L2])
        y = sb("conv_y", [P, 2, L2])
        u = sb("branch", [P, L2])
        stat, t0 = sb("ln_mean", [P, L2]), sb("ln_sq", [P, 2, L2])
        acc = ps("pool_acc", [P, 3, 512])
        acc2 = ps("ln_acc", [P, 3, 512])
        (pin, cin, win_ready, pe_done, u_ready, hi_done, a_used, y_ready, glu_used, c_ready, sq_ready, mean_done,
         var_done, steps, silu_done) = (sem(n) for n in (
             "pool_loaded", "conv_loaded", "diff_ready", "pool_done", "branch_ready", "branch_hi", "pool_used",
             "y_ready", "glu_used", "centered", "sq_ready", "mean_done", "var_done", "dve_steps", "silu_done"))
        ms_ready, root_ready = sem("mean_square_ready"), sem("root_ready")
        block = ctx.enter_context(nc.Block())

        @block.sync
        def _(eng):
            eng.dma_start(pw[:], dram["pool_w"]).then_inc(pin, 16)
            eng.dma_start(a[:, META:], dram["p2"][0]).then_inc(pin, 16)
            eng.dma_start(bv[:], dram["p2"][2]).then_inc(cin, 16)
            eng.dma_start(bg[:], dram["p2"][4]).then_inc(cin, 16)
            eng.wait_ge(win_ready, 1)
            eng.dma_start(a[:, META:], dram["p2"][1]).then_inc(a_used, 16)
            eng.wait_ge(glu_used, 1)
            eng.dma_start(bv[:], dram["p2"][3]).then_inc(c_ready, 16)
            eng.dma_start(bg[:], dram["p2"][5]).then_inc(c_ready, 16)

        @block.scalar
        def _(eng):
            for j in range(2):
                eng.wait_ge(u_ready, j + 1)
                eng.activation(hi[:, j, :], u[:], ACT.Copy).then_inc(hi_done, 1)
            eng.wait_ge(var_done, 1)
            for t, (off, n) in enumerate(TILES2):
                ln = eng.activation(stat[:, off:off + n], acc2[:, t, 0:n], ACT.Ln, scale=1.0 / 256, bias=E.eps[:])
            ln.then_inc(ms_ready, 1)
            eng.wait_ge(ms_ready, 1)
            eng.activation(stat[:], stat[:], ACT.Exp, scale=-0.5).then_inc(root_ready, 1)
            for j in range(2):
                eng.wait_ge(u_ready, j + 3)
                eng.activation(u[:], t0[:, j, :], ACT.Silu).then_inc(silu_done, 1)
                eng.wait_ge(silu_done, j + 1)
                eng.activation(hi[:, 2 + j, :], u[:], ACT.Copy).then_inc(hi_done, 1)

        @block.tensor
        def _(eng):
            eng.wait_ge(pin, 32)
            for j in range(2):
                eng.wait_ge(win_ready, j + 1)
                if j:
                    eng.wait_ge(u_ready, 1)
                for t, (off, n) in enumerate(TILES2):
                    mm = eng.matmul(acc[:, t, 0:n], pw[:, j, :], diff[:, off:off + n], start=True, stop=True)
                mm.then_inc(pe_done, 1)
            ones = col(E.con, CONST_AT, "ones")
            eng.wait_ge(y_ready, 2)
            for t, (off, n) in enumerate(TILES2):
                for j in range(2):
                    mm = eng.matmul(acc2[:, t, 0:n], ones, y[:, j, off:off + n], start=(j == 0), stop=(j == 1))
            mm.then_inc(mean_done, 1)
            eng.wait_ge(sq_ready, 1)
            for t, (off, n) in enumerate(TILES2):
                for j in range(2):
                    mm = eng.matmul(acc2[:, t, 0:n], ones, t0[:, j, off:off + n], start=(j == 0), stop=(j == 1))
            mm.then_inc(var_done, 1)

        @block.vector
        def _(eng):
            chain = Chain(eng, steps)
            eng.memset(a[:, 0:META], 0.0)
            chain(eng.memset(glu[:, 0:PADW], 0.0))
            chain(eng.memset(win[:, :, 0:META], 0.0))
            inv = col(E.con, CONST_AT, "invcnt")
            for j in range(2):
                if j == 0:
                    eng.wait_ge(pin, 32)
                else:
                    eng.wait_ge(a_used, 16)
                src = a
                prev = a[:, :]
                for g in range(2 * j + 2):
                    sh = 1 << g
                    chain(eng.tensor_tensor(win[:, g, META:], prev[:, META:], prev[:, META - sh:META + L2 - sh], ALU.add))
                    prev = win[:, g, :]
                if j:
                    eng.wait_ge(pe_done, 1)
                for half in range(2):
                    g = 2 * j + half
                    rows = slice(64 * half, 64 * half + 64)
                    chain(eng.scalar_tensor_tensor(diff[rows, :], win[rows, g, META:], 1.0 / 2 ** (g + 1),
                                                   a[rows, META:], ALU.mult, ALU.subtract))
                    chain(eng.tensor_tensor(diff[rows, 0:META], win[rows, g, META:2 * META],
                                            inv[rows, META * j:META * j + META], ALU.mult))
                    chain(eng.tensor_tensor(diff[rows, 0:META], diff[rows, 0:META], a[rows, META:2 * META], ALU.subtract))
                eng.engine_nop().then_inc(win_ready, 1)
                eng.wait_ge(pe_done, j + 1)
                for t, (off, n) in enumerate(TILES2):
                    chain(eng.tensor_scalar(u[:, off:off + n], acc[:, t, 0:n], col(E.par, PARAM_AT, "pool_b", j),
                                            col(E.par, PARAM_AT, "pool_scale", j), ALU.add, ALU.mult))
                eng.engine_nop().then_inc(u_ready, 1)
                eng.wait_ge(hi_done, j + 1)
                chain(eng.tensor_tensor(lo[:, j, :], u[:], hi[:, j, :].bitcast(F32), ALU.subtract))
            for j in range(2):
                if j == 0:
                    eng.wait_ge(cin, 32)
                else:
                    eng.wait_ge(c_ready, 32)
                chain(eng.tensor_tensor(glu[:, PADW:], bv[:], bg[:], ALU.mult))
                eng.engine_nop().then_inc(glu_used, 1)
                chain(eng.tensor_scalar(y[:, j, :], glu[:, 0:L2], col(E.par, PARAM_AT, "conv_w", KS * j),
                                        col(E.par, PARAM_AT, "conv_b", j), ALU.mult, ALU.add))
                for i in range(1, KS):
                    chain(eng.scalar_tensor_tensor(y[:, j, :], glu[:, i:i + L2], col(E.par, PARAM_AT, "conv_w", KS * j + i),
                                                   y[:, j, :], ALU.mult, ALU.add))
                eng.engine_nop().then_inc(y_ready, 1)
            eng.wait_ge(mean_done, 1)
            for t, (off, n) in enumerate(TILES2):
                chain(eng.tensor_scalar(stat[:, off:off + n], acc2[:, t, 0:n], 1.0 / 256, None, ALU.mult))
            for j in range(2):
                chain(eng.tensor_tensor(y[:, j, :], y[:, j, :], stat[:], ALU.subtract))
                chain(eng.tensor_tensor(t0[:, j, :], y[:, j, :], y[:, j, :], ALU.mult))
            eng.engine_nop().then_inc(sq_ready, 1)
            eng.wait_ge(root_ready, 1)
            for j in range(2):
                chain(eng.scalar_tensor_tensor(t0[:, j, :], y[:, j, :], col(E.par, PARAM_AT, "conv_g", j), stat[:],
                                               ALU.mult, ALU.mult))
                chain(eng.tensor_scalar(t0[:, j, :], t0[:, j, :], col(E.par, PARAM_AT, "conv_lb", j), None, ALU.add))
                eng.engine_nop().then_inc(u_ready, 1)
                eng.wait_ge(hi_done, 3 + j)
                chain(eng.tensor_tensor(lo[:, 2 + j, :], u[:], hi[:, 2 + j, :].bitcast(F32), ALU.subtract))


def router_phase(nc, E, dram, hi, lo):
    NG, EPG = 4, 4
    starts = [P * i for i in range(L2 // P)] + [L2 - P]
    NTL = len(starts)
    with ExitStack() as ctx:
        sb, ps, sem = phase(nc, ctx)
        w = sb("router_w", [P, KD, 20])
        wh, wl = sb("router_hi", [P, KD, 20], F32R), sb("router_lo", [P, KD, 20], F32R)
        lg = sb("logits", [P, NTL, 20])
        s1, s2, t4, ex = (sb(n, [P, NTL, 4]) for n in ("sel1", "sel2", "tmp4", "ex"))
        gs = sb("gsel", [P, NTL, 4])
        m, rem, sm, gw, v1, v2 = (sb(n, [P, NTL]) for n in ("m", "rem", "sm", "gw", "v1", "v2"))
        cm = sb("comb", [P, NTL, 16])
        ct = sb("comb_t", [16, L2])
        pl = ps("logits_p", [P, NTL, 20])
        pt = ps("comb_p", [16, 3, 512])
        loaded, whi_d, wlo_d, mm, step, x_in, x_out, comb_d, t_d, ct_d, out_d = (sem(n) for n in (
            "loaded", "w_hi", "w_lo", "logits_done", "dve_steps", "exp_in", "exp_out", "comb_ready", "t_done",
            "ct_ready", "stored"))
        block = ctx.enter_context(nc.Block())

        @block.sync
        def _(eng):
            eng.dma_start(w[:], dram["router_w"]).then_inc(loaded, 16)
            eng.wait_ge(ct_d, 1)
            eng.dma_start(dram["comb"], ct[:]).then_inc(out_d, 16)
            eng.wait_ge(out_d, 16)

        @block.tensor
        def _(eng):
            eng.wait_ge(wlo_d, 1)
            for t, off in enumerate(starts):
                n = 0
                for k in range(KD):
                    for x, y in ((hi, wh), (hi, wl), (lo, wh)):
                        ins = eng.matmul(pl[:, t, :], x[:, k, off:off + P], y[:, k, :], start=(n == 0), stop=(n == 3 * KD - 1))
                        n += 1
            ins.then_inc(mm, 1)
            eng.wait_ge(comb_d, 1)
            for t in range(NTL):
                ins = eng.transpose(pt[:, t // 4, (t % 4) * P:(t % 4 + 1) * P], cm[:, t, :], col(E.con, CONST_AT, "ident"))
            ins.then_inc(t_d, 1)

        @block.scalar
        def _(eng):
            eng.wait_ge(x_in, 1)
            eng.activation(ex[:], t4[:], ACT.Exp).then_inc(x_out, 1)
            eng.wait_ge(x_in, 2)
            eng.activation(ex[:], t4[:], ACT.Exp).then_inc(x_out, 1)

        @block.vector
        def _(eng):
            chain = Chain(eng, step)

            def b4(x):
                return x[:].unsqueeze(2).to_broadcast([P, NTL, 4])

            def first_max(sel, val, src):
                chain(eng.tensor_reduce(val[:], src, AX, ALU.max))
                chain(eng.tensor_tensor(sel[:], src, b4(val), ALU.is_ge))
                chain(eng.memset(rem[:], 1.0))
                for j in range(4):
                    chain(eng.tensor_tensor(sel[:, :, j], sel[:, :, j], rem[:], ALU.mult))
                    chain(eng.tensor_tensor(rem[:], rem[:], sel[:, :, j], ALU.subtract))

            eng.wait_ge(loaded, 16)
            chain(eng.tensor_copy(wh[:], w[:]))
            eng.tensor_tensor(wl[:], w[:], wh[:].bitcast(F32), ALU.subtract).then_inc(wlo_d, 1)
            eng.wait_ge(mm, 1)
            bias = col(E.par, PARAM_AT, "rbias").unsqueeze(1).to_broadcast([P, NTL, 20])
            chain(eng.tensor_tensor(lg[:], pl[:], bias, ALU.add))
            g = lg[:, :, 0:4]
            first_max(gs, m, g)
            chain(eng.tensor_tensor(t4[:], g, b4(m), ALU.subtract))
            eng.engine_nop().then_inc(x_in, 1)
            eng.wait_ge(x_out, 1)
            chain(eng.tensor_reduce(gw[:], ex[:], AX, ALU.add))
            chain(eng.reciprocal(gw[:], gw[:]))
            for j in range(NG):
                e = lg[:, :, 4 + 4 * j:8 + 4 * j]
                one = gs[:, :, j].unsqueeze(2).to_broadcast([P, NTL, 4])
                if j == 0:
                    chain(eng.tensor_tensor(s2[:], e, one, ALU.mult))
                else:
                    chain(eng.tensor_tensor(t4[:], e, one, ALU.mult))
                    chain(eng.tensor_tensor(s2[:], s2[:], t4[:], ALU.add))
            chain(eng.tensor_reduce(m[:], s2[:], AX, ALU.max))
            chain(eng.tensor_tensor(t4[:], s2[:], b4(m), ALU.subtract))
            eng.engine_nop().then_inc(x_in, 1)
            eng.wait_ge(x_out, 2)
            chain(eng.tensor_reduce(sm[:], ex[:], AX, ALU.add))
            chain(eng.reciprocal(sm[:], sm[:]))
            chain(eng.tensor_tensor(ex[:], ex[:], b4(sm), ALU.mult))
            first_max(s1, v1, ex[:])
            chain(eng.scalar_tensor_tensor(t4[:], s1[:], -2.0, ex[:], ALU.mult, ALU.add))
            first_max(s2, v2, t4[:])
            chain(eng.tensor_tensor(sm[:], v1[:], v2[:], ALU.add))
            chain(eng.reciprocal(sm[:], sm[:]))
            chain(eng.tensor_tensor(sm[:], sm[:], gw[:], ALU.mult))
            chain(eng.tensor_tensor(s1[:], s1[:], b4(v1), ALU.mult))
            chain(eng.tensor_tensor(s2[:], s2[:], b4(v2), ALU.mult))
            chain(eng.tensor_tensor(s1[:], s1[:], s2[:], ALU.add))
            chain(eng.tensor_tensor(s1[:], s1[:], b4(sm), ALU.mult))
            for j in range(NG):
                one = gs[:, :, j].unsqueeze(2).to_broadcast([P, NTL, 4])
                chain(eng.tensor_tensor(cm[:, :, 4 * j:4 * j + 4], s1[:], one, ALU.mult))
            eng.engine_nop().then_inc(comb_d, 1)
            eng.wait_ge(t_d, 1)
            chain(eng.tensor_copy(ct[:, 0:1024], pt[:, 0:2, :].rearrange("p b n -> p (b n)")))
            tail = L2 - 1024
            chain(eng.tensor_copy(ct[:, 1024:L2], pt[:, 2, P - tail:P]))
            eng.engine_nop().then_inc(ct_d, 1)


def build(nc, d, stop=None):
    TAGS.update(n=0, used=[])
    with ExitStack() as ctx:
        def sb(name, shape, dt=F32):
            return ctx.enter_context(nc.sbuf_tensor(name, shape, dt))

        E = Shared(nc, sb, d["tables"])
        with ExitStack() as c2:
            E.mask32 = c2.enter_context(nc.sbuf_tensor("mask32", [P, 5 * P], F32))
            setup_phase(nc, E, d)

        def split_tiles(c, width):
            return [c.enter_context(nc.sbuf_tensor(f"act_{n}_{nc_tag(nc)}", [P, KD, width], F32R)) for n in ("hi", "lo")]

        def scratch(name, shape, dt=F32):
            return nc.dram_tensor(name, shape, dt, kind="Internal").ap()

        XT = TILES1[:2]
        P1 = scratch("proj1", (26, P, NT1))
        O1 = scratch("mixed1", (8, P, NT1))
        P2 = scratch("proj2", (25, P, NT1))
        O2 = scratch("mixed2", (8, P, T))
        P3 = scratch("proj3", (19, P, L2))
        G3 = scratch("gates3", (24, P, L2))
        O3 = scratch("fox3", (4, P, L2))
        FR = scratch("decay_rows", (8, 6, L2), F32R)
        CB = scratch("comb", (16, L2))

        def modulated(layer, hi, lo):
            norm_phase(nc, E, lambda k, off, n: E.X[:, k, X0 + off:X0 + off + n], TILES1,
                       lambda k, t: E.gain[:, layer, 2 * k + (t == 2):2 * k + (t == 2) + 1],
                       lambda k, t: E.mod[:, layer, 2 * k + (t == 2):2 * k + (t == 2) + 1], hi, lo)

        def out_proj(layer, o, tiles):
            with ExitStack() as c:
                hi, lo = split_tiles(c, NT1)
                width = tiles[-1][0] + tiles[-1][1]
                split_phase(nc, lambda ch: o[ch], KD, width, hi, lo)
                gemm_phase(nc, E, d["w_out"][layer], [
                    Job(f, 0, KD, (hi, lo, 0), tiles, "resid", f=f,
                        gate_of=lambda t, f=f: E.mod[:, layer, 32 + 2 * f + (t == 2):32 + 2 * f + (t == 2) + 1])
                    for f in range(KD)])

        par = lambda name, j=None: col(E.par, PARAM_AT, name, j)
        with ExitStack() as c:
            hi, lo = split_tiles(c, NT1)
            modulated(0, hi, lo)
            kind = {}
            for f in range(26):
                if f < 4: kind[f] = ("rope", dict(gain=par("a_qn")))
                elif f == 4: kind[f] = ("rope", dict(gain=par("a_kn")))
                elif 10 <= f < 14: kind[f] = ("rope", dict(gain=par("b_qn")))
                elif 14 <= f < 18: kind[f] = ("rope", dict(gain=par("b_kn")))
                elif f == 5 or 18 <= f < 22: kind[f] = ("store", dict(func=ACT.Copy))
                else: kind[f] = ("store", dict(func=ACT.Silu))
            gemm_phase(nc, E, d["ab_w_in"], [Job(f, 0, KD, (hi, lo, 0), TILES1, kind[f][0], out=P1[f], **kind[f][1])
                                          for f in range(26)])
        if stop == "proj1":
            return P1

        def qblocks(i, band):
            ctxb = [(T, P), (T + P, P)]
            if i >= 8:
                return ctxb, {}
            if not band:
                return [(P * b, P) for b in range(10)], {}
            bl = [b for b in (i - 1, i, i + 1) if 0 <= b < 8]
            masks = {n: ((P, P) if b < i else (3 * P, P)) for n, b in enumerate(bl) if b != i}
            return [(P * b, P) for b in bl] + ctxb, masks

        chunks = []
        for c in range(4):
            g = c // 2
            chunks.append(Chunk([P1[c][64 * a:64 * a + 64] for a in range(2)], [P1[4][64 * g:64 * g + 64]] * 2, P1[5],
                                P1[6 + c], O1[c], [Unit(a, P * i, *qblocks(i, True)) for i in range(10) for a in range(2)],
                                sinks=[2 * c, 2 * c + 1], vcols=[64 * g] * 2))
        attention_phase(nc, E, NT1, chunks, "sink")
        if stop == "attnA":
            return O1
        chunks = [Chunk([P1[10 + c][64 * a:64 * a + 64] for a in range(2)], [P1[14 + c][64 * a:64 * a + 64] for a in range(2)],
                        P1[18 + c], P1[22 + c], O1[4 + c], [Unit(0, P * i, *qblocks(i, False)) for i in range(10)])
                  for c in range(4)]
        attention_phase(nc, E, NT1, chunks, "diff")
        if stop == "attnB":
            return O1
        out_proj(0, O1, TILES1)
        if stop == "x1":
            return E.X

        with ExitStack() as c:
            hi, lo = split_tiles(c, NT1)
            modulated(1, hi, lo)
            jobs = []
            for f in range(25):
                jobs.append(Job(f, 0, KD, (hi, lo, 0), XT if f < 4 or 16 <= f < 24 else TILES1, "store",
                                func=ACT.Silu if 16 <= f < 24 else ACT.Copy, out=P2[f]))
            gemm_phase(nc, E, d["gla_w_in"], jobs)
        if stop == "proj2":
            return P2
        gla_phase(nc, E, dict(
            reset=d["reset"], rank=P2[24], wa_f=d["wa_f"], wa_b=d["wa_b"], q=lambda h: P2[h][:, 0:T], k=lambda h: P2[4 + h],
            v=lambda h: P2[8 + 2 * h:10 + 2 * h].rearrange("e p n -> p e n"),
            gate=lambda h: P2[16 + 2 * h:18 + 2 * h, :, 0:T].rearrange("e p n -> p e n"),
            out=lambda h: O2[2 * h:2 * h + 2].rearrange("e p n -> p e n")))
        if stop == "gla":
            return O2
        out_proj(1, O2, XT)
        if stop == "x2":
            return E.X

        with ExitStack() as c:
            hi, lo = split_tiles(c, L2)
            norm_phase(nc, E, lambda k, off, n: E.X[:, k, off:off + n], TILES2, lambda k, t: par("norm1", k),
                       lambda k, t: None, hi, lo)
            jobs = []
            for f in range(43):
                out = P3[f] if f < 19 else G3[f - 19]
                func = ACT.Sigmoid if f in (4, 5) or f >= 19 else ACT.Copy
                jobs.append(Job(f, 0, KD, (hi, lo, 0), TILES2, "store", func=func, out=out))
            gemm_phase(nc, E, d["w_in"], jobs)
        if stop == "proj3":
            return P3
        decay_phase(nc, E, P3[18][0:8], FR)
        units = []
        for i in range(9):
            q0 = P * i if i < 8 else L2 - P
            blocks = [(P * b, P) for b in range(min(i + 1, 8))] + ([(T, META)] if i == 8 else [])
            masks = {i: (3 * P, P)} if i < 8 else {7: (3 * P - 16, P), 8: (3 * P + 112, META)}
            units += [Unit(a, q0, blocks, masks) for a in range(2)]
        chunks = [Chunk([P3[6 + c][64 * a:64 * a + 64] for a in range(2)], [P3[10 + c][64 * a:64 * a + 64] for a in range(2)],
                        P3[14 + c], None, O3[c], units, vcols=[0, 64],
                        frow=[[FR[2 * c + a, 2 * j:2 * j + 2] for j in range(3)] for a in range(2)]) for c in range(4)]
        attention_phase(nc, E, L2, chunks, "fox")
        if stop == "fox":
            return O3
        with ExitStack() as c:
            hi, lo = split_tiles(c, L2)
            branch_phase(nc, E, dict(pool_w=d["pool_w"], p2=P3), hi, lo)
            split_phase(nc, lambda ch: O3[ch], 4, L2, hi[:, 4:8, :], lo[:, 4:8, :])
            mhi, mlo = split_tiles(c, L2)
            jobs = []
            for f in range(KD):
                for b, (k0, k1) in enumerate(((0, 2), (2, 4), (4, 8))):
                    jobs.append(Job(f, k0, k1, (hi, lo, k0), TILES2, "gate", f=f, first=b == 0, last=b == 2,
                                    gates=G3[8 * b + f], hi=mhi, lo=mlo))
            gemm_phase(nc, E, d["w_abc"], jobs)
            gemm_phase(nc, E, d["w_o"], [Job(f, 0, KD, (mhi, mlo, 0), TILES2, "add", f=f) for f in range(KD)])
        if stop == "x3":
            return E.X
        with ExitStack() as c:
            hi, lo = split_tiles(c, L2)
            norm_phase(nc, E, lambda k, off, n: E.X[:, k, off:off + n], TILES2, lambda k, t: par("norm2", k),
                       lambda k, t: None, hi, lo)
            router_phase(nc, E, dict(router_w=d["router_w"], comb=CB), hi, lo)
            if stop == "router":
                return CB
            hhi, hlo = (c.enter_context(nc.sbuf_tensor(f"hidden_{n}", [P, 4, L2], F32R)) for n in ("hi", "lo"))
            jobs, last_down = [], {}

            def up(e, ch):
                slot = 2 * (e % 2) + ch
                jobs.append(Job(4 * e + 2 * ch, 0, KD, (hi, lo, 0), TILES2, "up"))
                jobs.append(Job(4 * e + 2 * ch + 1, 0, KD, (hi, lo, 0), TILES2, "he", slot=slot, reuse=last_down.get(e - 2)))

            def down(e):
                for f in range(KD):
                    jobs.append(Job(("down", e, f // 4), 2 * (f % 4), 2 * (f % 4) + 2, (hhi, hlo, 2 * (e % 2)), TILES2,
                                    "down", f=f, needs=6 * (e + 1)))
                last_down[e] = len(jobs) - 1

            for e in range(NE + 1):
                if e < NE:
                    up(e, 0)
                    up(e, 1)
                if e >= 1:
                    down(e - 1)
            tiles, number = [], {}
            for j in jobs:
                if j.w not in number:
                    number[j.w] = len(tiles)
                    tiles.append(d["exp_down"][j.w[1], j.w[2]] if isinstance(j.w, tuple) else d["exp_up"][j.w])
                j.w = number[j.w]
            gemm_phase(nc, E, tiles, jobs, comb=dict(hhi=hhi, hlo=hlo, dram=CB))
        if stop == "x4":
            return E.X
        with ExitStack() as c:
            out = c.enter_context(nc.sbuf_tensor("y", [P, KD, T], F32))
            norm_phase(nc, E, lambda k, off, n: E.X[:, k, META + off:META + off + n], TILES1[:2],
                       lambda k, t: par("final_g", k), lambda k, t: None, None, None, out=out, out_dram=d["y"])


def tiles_of(w):
    k, n = w.shape
    pad = -n % P
    if pad:
        w = np.concatenate([w, np.zeros((k, pad), w.dtype)], 1)
    return np.ascontiguousarray(w.reshape(k // P, P, (n + pad) // P, P).transpose(2, 1, 0, 3)).reshape(-1, P, k)


def by_chunk(vec):
    return vec.reshape(-1, P).T


def rows_of(vec):
    return np.broadcast_to(vec.reshape(1, -1), (P, vec.size))


def layout(i):
    f = {k: np.asarray(v) for k, v in i.items()}
    par = {
        "cond": np.stack([by_chunk(f["c"][0]), by_chunk(f["c_ctx"])], 2).reshape(P, 16),
        "adaln_b": np.concatenate([by_chunk(f["adaln_b"][l]) for l in range(2)], 1),
        "norm_g": np.concatenate([by_chunk(f["norm_g"][l]) for l in range(2)], 1),
        "a_qn": np.tile(f["a_q_norm"][0], 2)[:, None], "a_kn": np.tile(f["a_k_norm"][0], 2)[:, None],
        "sink": rows_of(f["a_sink"][0]),
        "b_qn": np.tile(f["b_q_norm"][0], 2)[:, None], "b_kn": np.tile(f["b_k_norm"][0], 2)[:, None],
        "lq1": rows_of(f["b_lambda_q1"][0]), "lk1": rows_of(f["b_lambda_k1"][0]),
        "lq2": rows_of(f["b_lambda_q2"][0]), "lk2": rows_of(f["b_lambda_k2"][0]),
        "subln": f["b_subln"][0][:, None],
        "ba": np.concatenate([by_chunk(f["gla_ba_f"][0]), by_chunk(f["gla_ba_b"][0])], 1),
        "out_norm": by_chunk(f["gla_out_norm"][0]),
        "norm1": by_chunk(f["norm1_g_2"][0]),
        "bforget": np.concatenate([f["b_forget_2"][0], np.zeros(P - 8, np.float32)])[:, None],
        "pool_b": by_chunk(f["pool_b_2"][0].reshape(-1)), "pool_scale": by_chunk(f["pool_scale_2"][0]),
        "conv_w": f["conv_w_2"][0].T.reshape(2, P, 31).transpose(1, 0, 2).reshape(P, 62),
        "conv_b": by_chunk(f["conv_b_2"][0]), "conv_g": by_chunk(f["conv_ln_g_2"][0]),
        "conv_lb": by_chunk(f["conv_ln_b_2"][0]),
        "norm2": by_chunk(f["norm2_g_2"][0]),
        "rbias": rows_of(np.concatenate([f["router_g_b_2"][0], f["router_e_b_2"][0]])),
        "final_g": by_chunk(f["final_g_2"]),
    }
    con = shape_constants()
    pw = np.zeros((P, 2, P), np.float32)
    for g in range(4):
        r = slice(64 * (g % 2), 64 * (g % 2) + 64)
        pw[r, g // 2, r] = f["pool_w_2"][0, g]
    w_in = f["w_in_2"][0]
    c0 = 3 * 256 + 3 * 512
    x = np.concatenate([f["x"][0], f["ctx"][0]], 0).T.reshape(KD, P, NT1).transpose(1, 0, 2)
    down = f["exp_w2_2"][0].reshape(NE, 2, P, 2, 4, P)
    arrays = dict(
        params=np.concatenate([par[n] for n, _ in PARAM_WIDTHS], 1),
        consts=np.concatenate([con[n] for n, _ in CONST_WIDTHS], 1).astype(np.float32),
        masks=mask_constants().astype(np.float32),
        tables=np.stack([con["cos"], con["sin"]], 1).astype(np.float32),
        reset=con["reset"].astype(np.float32),
        x0=x, meta=f["meta_2"].T.reshape(KD, P, META).transpose(1, 0, 2),
        adaln_w=f["adaln_w"].reshape(2, KD, P, 3 * D),
        ab_w_in=tiles_of(f["ab_w_in"][0]),
        w_out=np.stack([tiles_of(f["w_out"][l]) for l in range(2)]),
        gla_w_in=tiles_of(f["gla_w_in"][0]),
        wa_f=f["gla_wa_f"][0], wa_b=f["gla_wa_b"][0],
        w_in=np.concatenate([tiles_of(w_in[:, :c0 + 8]), tiles_of(w_in[:, c0 + 8:])], 0),
        pool_w=pw,
        w_abc=tiles_of(np.concatenate([f["w_out_a_2"][0], f["w_out_b_2"][0], f["w_out_c_2"][0]], 0)),
        w_o=tiles_of(f["w_o_2"][0]),
        router_w=np.concatenate([f["router_g_2"][0], f["router_e_2"][0]], 1).reshape(KD, P, 20).transpose(1, 0, 2),
        exp_up=np.stack([tiles_of(f["exp_w1_2"][0, e]) if j == 0 else tiles_of(f["exp_w3_2"][0, e])
                         for e in range(NE) for j in range(2)], 0).reshape(NE, 2, 2, P, D)
                 .transpose(0, 2, 1, 3, 4).reshape(4 * NE, P, D),
        exp_down=down.transpose(0, 3, 2, 4, 1, 5).reshape(NE, 2, P, 8 * P),
    )
    return {k: np.ascontiguousarray(v) for k, v in arrays.items()}


def kernel(**inputs):
    import numpy as _np
    import concourse.bacc as _bacc
    from concourse import mybir as _mybir
    from concourse.bass_utils import run_bass_kernel_spmd as _run

    arrays = layout(inputs)
    nc = _bacc.Bacc("TRN2", target_bir_lowering=False, num_devices=1)
    d = {n: nc.dram_tensor(f"in_{n}", a.shape, F32, kind="ExternalInput").ap() for n, a in arrays.items()}
    d["y"] = nc.dram_tensor("y_dram", (P, KD, T), F32, kind="ExternalOutput").ap()
    build(nc, d)
    r = _run(nc, [{f"in_{n}": a for n, a in arrays.items()}], core_ids=[0])
    y = r.results[0]["y_dram"]
    return _np.ascontiguousarray(y.transpose(2, 1, 0)).reshape(1, T, D)
```

```python
from contextlib import ExitStack

import numpy as np
import concourse.bass as bass
from concourse import mybir

F32 = mybir.dt.float32
F32R = mybir.dt.float32r
BF16 = mybir.dt.bfloat16
ALU = mybir.AluOpType
ACT = mybir.ActivationFunctionType
AX = mybir.AxisListType.X

P = 128
D = 1024
KD = D // P
T = 1024
CTX = 256
META = 16
L2 = META + T
X0 = META
C0 = META + T
NT1 = T + CTX
EPS = 1e-6
NEG = -1e30
HD = 64
SCALE = HD ** -0.5
LAMBDA_INIT = 0.8 - 0.6 * float(np.exp(-0.3 * 0))
CONV_K = 31
GC = 64
GH, GDK, GDV = 4, 128, 256
NE, EH = 16, 256
TILES1 = [(0, 512), (512, 512), (1024, 256)]
TILES2 = [(0, 352), (352, 352), (704, 336)]


class Shared:
    def __init__(self, nc, sb, tables):
        self.X = sb("residual", [P, KD, META + NT1])
        self.par, self.con = sb("params", [P, PARAM_N]), sb("consts", [P, CONST_N])
        self.mask, self.nsink = sb("mask", [P, 5 * P], BF16), sb("neg_sink", [P, 8])
        self.sc = sb("silu_cond", [P, 2 * KD])
        self.lam, self.neglam = sb("lambda", [P, 8]), sb("neg_lambda", [P, 1])
        self.mod, self.gain = sb("mod", [P, 2, 48]), sb("mod_gain", [P, 2, 16])
        self.subln, self.eps = sb("subln", [P, 1]), sb("eps", [P, 1])
        self.tables = tables
        self.y_stored = nc.alloc_semaphore("y_stored")


def shape_constants():
    p = np.arange(P)
    parts = {}
    parts["ident"] = np.eye(P)
    parts["ones"] = np.ones((P, P))
    parts["headones"] = (p[:, None] // HD == p[None, :] // HD)
    rot = np.zeros((P, P))
    for d in range(P):
        if d % 32 < 16:
            rot[d + 16, d] = -1.0
        else:
            rot[d - 16, d] = 1.0
    parts["rot"] = rot
    m = 16
    inv = (np.float32(10000.0) ** (-np.arange(m, dtype=np.float32) / np.float32(m))).astype(np.float32)
    tok = np.arange(T)
    rows, cols = tok // 64, tok % 64
    ang = np.zeros((P, T), np.float32)
    for d in range(P):
        pos = rows if d % HD < 32 else cols
        ang[d] = pos.astype(np.float32) * inv[d % 16]
    parts["cos"], parts["sin"] = np.cos(ang), np.sin(ang)
    reset = np.ones((P, NT1)); reset[:, ::GC] = 0
    parts["reset"] = reset
    s, c = p[:, None], p[None, :]
    parts["causal"] = (s // GC == c // GC) & (s <= c)
    parts["anti"] = (s // GC == c // GC) & (s >= c)
    inv_cnt = np.zeros((P, 2, META))
    for j in range(2):
        for q in range(P):
            w = 2 ** (2 * j + q // 64 + 1)
            inv_cnt[q, j] = 1.0 / np.minimum(np.arange(META) + 1, w)
    parts["invcnt"] = inv_cnt.reshape(P, -1)
    return parts


def mask_constants():
    q, x = np.arange(P)[:, None], np.arange(3 * P)[None, :]
    late = np.where(x - P <= q, 0.0, NEG)
    early = np.where(np.arange(P)[None, :] >= q, 0.0, NEG)
    return np.concatenate([np.eye(P), early, late], 1)


CONST_WIDTHS = [("ident", P), ("ones", P), ("headones", P), ("rot", P), ("causal", P), ("anti", P), ("invcnt", 2 * META)]
PARAM_WIDTHS = [
    ("cond", 2 * KD), ("adaln_b", 2 * 3 * KD), ("norm_g", 2 * KD), ("a_qn", 1), ("a_kn", 1), ("sink", 8),
    ("b_qn", 1), ("b_kn", 1), ("lq1", HD), ("lk1", HD), ("lq2", HD), ("lk2", HD), ("subln", 1), ("ba", 2 * GH),
    ("out_norm", 2), ("norm1", KD), ("bforget", 1), ("pool_b", 2), ("pool_scale", 2), ("conv_w", 62),
    ("conv_b", 2), ("conv_g", 2), ("conv_lb", 2), ("norm2", KD), ("rbias", 20), ("final_g", KD)]


def offsets(widths):
    at, n = {}, 0
    for name, w in widths:
        at[name] = (n, w)
        n += w
    return at, n


CONST_AT, CONST_N = offsets(CONST_WIDTHS)
PARAM_AT, PARAM_N = offsets(PARAM_WIDTHS)


def col(tile, at, name, j=None, w=1):
    o, width = at[name]
    if j is None:
        return tile[:, o:o + width]
    return tile[:, o + j:o + j + w]


class Chain:
    def __init__(self, eng, sem):
        self.eng, self.sem, self.n = eng, sem, 0

    def __call__(self, ins):
        self.n += 1
        ins.then_inc(self.sem, 1)
        self.eng.wait_ge(self.sem, self.n)


def phase(nc, ctx):
    mine = []

    def sb(name, shape, dt=F32):
        return ctx.enter_context(nc.sbuf_tensor(f"{name}_{nc_tag(nc)}", shape, dt))

    def ps(name, shape, dt=F32):
        return ctx.enter_context(nc.psum_tensor(f"{name}_{nc_tag(nc)}", shape, dt))

    def sem(name):
        if not name.startswith("gp_"):
            mine.append(ctx.enter_context(nc.semaphore(f"{name}_{nc_tag(nc)}")))
            return mine[-1]
        return nc.alloc_semaphore(f"{name}_{nc_tag(nc)}")

    used = sorted(s.num for s in TAGS["used"])
    while used:
        n = 1
        while n < len(used) and used[n] == used[0] + n:
            n += 1
        nc.gpsimd.sem_clear(range(used[0], used[0] + n))
        used = used[n:]
    TAGS["used"] = mine
    return sb, ps, sem


TAGS = {"n": 0, "used": []}


def load_exp_ln(nc):
    nc.scalar.preload_act_table_set("natural_log_exp_and_others")


def nc_tag(nc):
    TAGS["n"] += 1
    return TAGS["n"]


def modulation(eng, chain, E, layer, acc):
    bias = col(E.par, PARAM_AT, "adaln_b", 24 * layer, 24).unsqueeze(2).to_broadcast([P, 24, 2])
    chain(eng.tensor_tensor(E.mod[:, layer, :].rearrange("p (f c) -> p f c", c=2),
                            acc[:].rearrange("p (f c) -> p f c", c=2), bias, ALU.add))
    gain = col(E.par, PARAM_AT, "norm_g", 8 * layer, 8).unsqueeze(2).to_broadcast([P, 8, 2])
    chain(eng.tensor_scalar(E.gain[:, layer, :], E.mod[:, layer, 16:32], 1.0, None, ALU.add))
    chain(eng.tensor_tensor(E.gain[:, layer, :].rearrange("p (f c) -> p f c", c=2),
                            E.gain[:, layer, :].rearrange("p (f c) -> p f c", c=2), gain, ALU.mult))


def setup_phase(nc, E, dram):
    with ExitStack() as ctx:
        sb, ps, sem = phase(nc, ctx)
        tiles = sb("adaln_w", [P, KD, 3 * D])
        sg = sb("sigma_cond", [P, 16])
        lam = sb("lam_work", [P, 4 * HD])
        acc = ps("mod", [P, 48])
        rows_p, rows = ps("mod_rows_p", [2, 6, 512]), sb("mod_rows", [2, 3 * D])
        rows_done, rows_ready, mod_done = sem("mod_rows_done"), sem("mod_rows_ready"), sem("mod_done")
        loaded, x_in = sem("small_loaded"), sem("gp_x_loaded")
        w_in = [sem(f"w_loaded{i}") for i in range(KD)]
        cond_ready, steps, asteps = (sem(n) for n in ("cond_ready", "dve_steps", "act_steps"))
        lam_sum, lam_exp = sem("lam_sum"), sem("lam_exp")
        load_exp_ln(nc)
        block = ctx.enter_context(nc.Block())

        @block.sync
        def _(eng):
            eng.dma_start(E.par[:], dram["params"]).then_inc(loaded, 16)
            eng.dma_start(E.con[:], dram["consts"]).then_inc(loaded, 16)
            eng.dma_start(E.mask32[:], dram["masks"]).then_inc(loaded, 16)
            eng.wait_ge(loaded, 48)
            for i in range(0, KD, 2):
                eng.dma_start(tiles[:, i, :], dram["adaln_w0"][i]).then_inc(w_in[i], 16)
            eng.wait_ge(x_in, 32)

        @block.gpsimd
        def _(eng):
            eng.wait_ge(w_in[1], 16)
            eng.dma_start(E.X[:, :, X0:X0 + NT1], dram["x0"]).then_inc(x_in, 16)
            eng.dma_start(E.X[:, :, 0:META], dram["meta"]).then_inc(x_in, 16)

        @block.scalar
        def _(eng):
            eng.wait_ge(loaded, 48)
            for i in range(1, KD, 2):
                eng.dma_start(tiles[:, i, :], dram["adaln_w0"][i]).then_inc(w_in[i], 16)
            eng.activation(sg[:], col(E.par, PARAM_AT, "cond"), ACT.Exp, scale=-1.0).then_inc(asteps, 1)
            eng.wait_ge(lam_sum, 1)
            eng.activation(E.lam[:, 0:2], E.lam[:, 2:4], ACT.Exp).then_inc(lam_exp, 1)
            eng.wait_ge(rows_done, 1)
            eng.activation(rows[:, 0:3 * 512], rows_p[:, 0:3, :].rearrange("p b n -> p (b n)"), ACT.Copy).then_inc(rows_ready, 1)

        @block.vector
        def _(eng):
            chain = Chain(eng, steps)
            eng.wait_ge(loaded, 48)
            eng.wait_ge(asteps, 1)
            chain(eng.tensor_scalar(sg[:], sg[:], 1.0, None, ALU.add))
            chain(eng.reciprocal(sg[:], sg[:]))
            eng.tensor_tensor(E.sc[:], col(E.par, PARAM_AT, "cond"), sg[:], ALU.mult).then_inc(cond_ready, 1)
            chain(eng.memset(E.eps[:], EPS))
            chain(eng.tensor_copy(E.mask[:], E.mask32[:]))
            chain(eng.tensor_scalar(E.nsink[:], col(E.par, PARAM_AT, "sink"), -1.0, None, ALU.mult))
            for j, (a, b) in enumerate((("lq1", "lk1"), ("lq2", "lk2"))):
                chain(eng.tensor_tensor(lam[:, j * HD:(j + 1) * HD], col(E.par, PARAM_AT, a),
                                        col(E.par, PARAM_AT, b), ALU.mult))
            red = eng.tensor_reduce(E.lam[:, 2:4], lam[:, 0:2 * HD].rearrange("p (j d) -> p j d", j=2), AX, ALU.add)
            red.then_inc(lam_sum, 1)
            eng.wait_ge(lam_exp, 1)
            chain(eng.tensor_tensor(E.lam[:, 4:5], E.lam[:, 1:2], E.lam[:, 0:1], ALU.subtract))
            chain(eng.tensor_scalar(E.neglam[:], E.lam[:, 4:5], -LAMBDA_INIT, None, ALU.add))
            eng.wait_ge(rows_done, 1)
            eng.tensor_copy(rows[:, 3 * 512:], rows_p[:, 3:6, :].rearrange("p b n -> p (b n)")).then_inc(rows_ready, 1)
            eng.wait_ge(mod_done, 1)
            modulation(eng, chain, E, 0, acc)

        @block.tensor
        def _(eng):
            eng.wait_ge(cond_ready, 1)
            for i in range(KD):
                eng.wait_ge(w_in[i], 16)
                for g in range(6):
                    mm = eng.matmul(rows_p[:, g, :], E.sc[:, 2 * i:2 * i + 2], tiles[:, i, 512 * g:512 * g + 512],
                                    start=(i == 0), stop=(i == KD - 1))
            mm.then_inc(rows_done, 1)
            eng.wait_ge(rows_ready, 2)
            for f in range(3 * KD):
                mm = eng.transpose(acc[:, 2 * f:2 * f + 2], rows[:, f * P:(f + 1) * P],
                                   col(E.con, CONST_AT, "ident")[0:2, 0:2])
            mm.then_inc(mod_done, 1)


def norm_phase(nc, E, x_of, tiles, gain_of, shift_of, hi, lo, out=None, out_dram=None, wts=None):
    with ExitStack() as ctx:
        sb, ps, sem = phase(nc, ctx)
        sq = sb("sq", [P, 4, 512])
        rstd = sb("rstd", [P, 3, 512])
        u = sb("u", [P, 4, 512])
        ss = [ps(f"ss{i}", [P, 512]) for i in range(len(tiles))]
        squared, rs_ready, u_ready, hi_ready, lo_done, sq_used = (
            sem("squared"), sem("rstd_ready"), sem("u_ready"), sem("hi_ready"), sem("lo_done"), sem("sq_used"))
        ms_ready = sem("mean_square_ready")
        if wts:
            wts.sems(sem)
        load_exp_ln(nc)
        block = ctx.enter_context(nc.Block())
        NTL = len(tiles)

        if wts:
            @block.sync
            def _(eng):
                wts.first_loads(eng)

        @block.scalar
        def _(eng):
            def squares(t, k):
                off, n = tiles[t]
                i = t * KD + k
                if i >= 4:
                    eng.wait_ge(sq_used, i - 3)
                eng.activation(sq[:, i % 4, 0:n], x_of(k, off, n), ACT.Square).then_inc(squared, 1)

            def root(t):
                n = tiles[t][1]
                eng.wait_ge(sq_used, KD * (t + 1))
                eng.activation(rstd[:, t, 0:n], ss[t][:, 0:n], ACT.Ln, scale=1.0 / D, bias=E.eps[:]).then_inc(ms_ready, 1)
                eng.wait_ge(ms_ready, t + 1)
                eng.activation(rstd[:, t, 0:n], rstd[:, t, 0:n], ACT.Exp, scale=-0.5).then_inc(rs_ready, 1)

            for t in range(2):
                for k in range(KD):
                    squares(t, k)
            root(0)
            root(1)
            for t, (off, n) in enumerate(tiles):
                for k in range(KD):
                    if out is None:
                        i = t * KD + k
                        eng.wait_ge(u_ready, i + 1)
                        s = shift_of(k, t)
                        if s is None:
                            eng.activation(hi[:, k, off:off + n], u[:, i % 4, 0:n], ACT.Copy).then_inc(hi_ready, 1)
                        else:
                            eng.activation(hi[:, k, off:off + n], u[:, i % 4, 0:n], ACT.Identity,
                                           bias=s).then_inc(hi_ready, 1)
                    if t + 2 < NTL:
                        squares(t + 2, k)
                if t + 2 < NTL:
                    root(t + 2)
                if wts and t == 1:
                    wts.first_hi(eng)

        @block.tensor
        def _(eng):
            for t, (off, n) in enumerate(tiles):
                for k in range(KD):
                    i = t * KD + k
                    eng.wait_ge(squared, i + 1)
                    eng.matmul(ss[t][:, 0:n], col(E.con, CONST_AT, "ones"), sq[:, i % 4, 0:n],
                               start=(k == 0), stop=(k == KD - 1)).then_inc(sq_used, 1)

        @block.vector
        def _(eng):
            for t, (off, n) in enumerate(tiles):
                eng.wait_ge(rs_ready, t + 1)

                def split(k):
                    i = t * KD + k
                    eng.wait_ge(hi_ready, i + 1)
                    h = hi[:, k, off:off + n].bitcast(F32)
                    s = shift_of(k, t)
                    if s is None:
                        ins = eng.tensor_tensor(lo[:, k, off:off + n], u[:, i % 4, 0:n], h, ALU.subtract)
                    else:
                        ins = eng.scalar_tensor_tensor(lo[:, k, off:off + n], u[:, i % 4, 0:n], s, h,
                                                       ALU.add, ALU.subtract)
                    ins.then_inc(lo_done, 1)

                for k in range(KD):
                    i = t * KD + k
                    if out is not None:
                        eng.scalar_tensor_tensor(out[:, k, off:off + n], x_of(k, off, n), gain_of(k, t),
                                                 rstd[:, t, 0:n], ALU.mult, ALU.mult).then_inc(u_ready, 1)
                        continue
                    if i >= 4:
                        eng.wait_ge(lo_done, i - 3)
                    eng.scalar_tensor_tensor(u[:, i % 4, 0:n], x_of(k, off, n), gain_of(k, t),
                                             rstd[:, t, 0:n], ALU.mult, ALU.mult).then_inc(u_ready, 1)
                    if k >= 1:
                        split(k - 1)
                if out is None:
                    split(KD - 1)
                if wts and t == 1:
                    wts.first_lo(eng)

        if out is not None:
            @block.sync
            def _(eng):
                for t, (off, n) in enumerate(tiles):
                    eng.wait_ge(u_ready, KD * (t + 1))
                    eng.dma_start(out_dram[:, :, off:off + n], out[:, :, off:off + n]).then_inc(E.y_stored, 16)
                eng.wait_ge(E.y_stored, 16 * NTL)


class JobArgs:
    def __init__(self, func=None, out=None, gain=None, f=None, gate_of=None, first=False, last=False, gates=None,
                 hi=None, lo=None, slot=None, reuse=None, needs=None, merged=False):
        self.func, self.out, self.gain, self.f, self.gate_of = func, out, gain, f, gate_of
        self.first, self.last, self.gates, self.hi, self.lo = first, last, gates, hi, lo
        self.slot, self.reuse, self.needs, self.merged = slot, reuse, needs, merged


class Job:
    def __init__(self, w, k0, k1, rhs, tiles, kind, **kw):
        self.w, self.k0, self.k1, self.rhs, self.tiles, self.kind = w, k0, k1, rhs, tiles, kind
        self.a = JobArgs(**kw)


class Weights:
    def __init__(self, nc, ctx, dram, ring=3):
        tag = nc_tag(nc)
        self.dram, self.ring = dram, ring
        self.stage = ctx.enter_context(nc.sbuf_tensor(f"w_stage_{tag}", [P, ring, KD * P], F32))
        self.hi, self.lo = (ctx.enter_context(nc.sbuf_tensor(f"w_{n}_{tag}", [P, 2, KD * P], F32R)) for n in ("hi", "lo"))

    def sems(self, sem):
        self.loaded, self.rounded = sem("first_w_loaded"), sem("first_w_hi")

    def first_loads(self, eng):
        for w in range(2):
            eng.dma_start(self.stage[:, w, :], self.dram[w]).then_inc(self.loaded, 16)

    def first_hi(self, eng):
        eng.wait_ge(self.loaded, 32)
        eng.activation(self.hi[:], self.stage[:, 0:2, :], ACT.Copy).then_inc(self.rounded, 1)

    def first_lo(self, eng):
        eng.wait_ge(self.rounded, 1)
        eng.tensor_tensor(self.lo[:], self.stage[:, 0:2, :], self.hi[:].bitcast(F32), ALU.subtract)


def gemm_phase(nc, E, wts, jobs, comb=None, adaln=None, decay_rows=None):
    with ExitStack() as ctx:
        sb, ps, sem = phase(nc, ctx)
        NJ = len(jobs)
        NW = max(j.w for j in jobs) + 1
        last_job = {j.w: i for i, j in enumerate(jobs)}
        kinds = {j.kind for j in jobs}
        NTmax = 1280 if "rope" in kinds or any(j.tiles[-1][0] + j.tiles[-1][1] > L2 for j in jobs) else L2
        wdram, NSTG, stage, whi, wlo = wts.dram, wts.ring, wts.stage, wts.hi, wts.lo
        acc = [ps(f"acc{i}", [P, 3, 512]) for i in range(2)]
        w_in = [sem(f"w_loaded{i}") for i in range(NSTG)]
        w_hi, w_lo, mm = sem("w_hi_ready"), sem("w_lo_ready"), sem("products")
        free = [sem(f"acc_free{i}") for i in range(2)]
        steps = sem("dve_steps")
        out_stored = [sem(f"out_stored{i}") for i in range(2)]
        tiles_before = [sum(len(j.tiles) for j in jobs[:i]) for i in range(NJ + 1)]
        free_before = {}
        cnt = [0, 0]
        for i, j in enumerate(jobs):
            free_before[i] = cnt[i % 2]
            cnt[i % 2] += len(j.tiles)
        storing = [i for i, j in enumerate(jobs) if j.kind in ("store", "rope")]
        turn = {i: n for n, i in enumerate(storing)}
        if storing:
            outb = sb("out_stage", [P, 2, NTmax])
        if "rope" in kinds:
            xg = sb("rope_x", [P, 1280])
            sq = sb("rope_sq", [P, 1280])
            tab = sb("rope_tab", [P, 2, T])
            t1 = sb("rope_t1", [P, 512])
            t2 = sb("rope_t2", [P, 512])
            rs = sb("rope_rs", [P, 512])
            aux = [ps("rope_ss", [P, 512]), ps("rope_rot", [P, 512])]
            tab_in, xg_ready, aux_done, rope_done, ms_ready, rs_ready = (
                sem(n) for n in ("tab_loaded", "xg_ready", "aux_done", "rope_done", "mean_square_ready", "rstd_ready"))
        ropes = [i for i, j in enumerate(jobs) if j.kind == "rope"]
        ropes_tiles = {i: sum(len(jobs[q].tiles) for q in ropes if q < i) for i in ropes}
        if "gate" in kinds:
            gt = sb("gates", [P, 3, 352])
            gtmp = sb("gated", [P, 352])
            gate_in = [sem(f"gp_gate_loaded{i}") for i in range(3)]
            gated, m_hi, m_lo = sem("gated"), sem("merged_hi"), sem("merged_lo")

            def halves(x):
                return x.rearrange("p (a b) -> p a b", a=2)

            def merged(t, n):
                return E.X[:, 2 * t:2 * t + 2, C0:C0 + n // 2]
        if "up" in kinds:
            s1 = sb("silu_up", [P, L2])
            h2 = sb("hidden", [P, 3, 352])
            cb = sb("comb", [P, 2, L2])
            hhi, hlo = comb["hhi"], comb["hlo"]
            cb_in = [sem(f"gp_comb_loaded{i}") for i in range(2)]
            he_ready, he_hi, he_lo = sem("he_ready"), sem("he_hi"), sem("he_lo")
        if "rope" in kinds:
            load_exp_ln(nc)
        if adaln is not None:
            ring, cond, junk = sb("adaln_w", [P, 2, D]), sb("silu_rows", [P, 2, D]), sb("mod_product", [P, D], BF16)
            ring_in, ring_used = [sem(f"gp_adaln_loaded{i}") for i in range(2)], sem("adaln_used")
            cond_in, cond_exp, cond_ready = sem("gp_cond_loaded"), sem("cond_exp"), sem("cond_ready")
        if "decay" in kinds:
            FH = 8
            fz, fa, fo = (sb(n, [FH, L2]) for n in ("forget", "forget_exp", "ones_row"))
            frows = sb("decay_rows", [FH, 6, L2], F32R)
            f_act, f_done, f_stored = sem("forget_act"), sem("decay_done"), sem("gp_decay_stored")
            load_exp_ln(nc)
        block = ctx.enter_context(nc.Block())
        order = {}
        for kd in ("up", "he", "down", "gate"):
            n = 0
            for i, j in enumerate(jobs):
                if j.kind == kd:
                    for t in range(len(j.tiles)):
                        order[i, t] = n
                        n += 1

        @block.sync
        def _(eng):
            if "rope" in kinds:
                eng.dma_start(tab[:], E.tables).then_inc(tab_in, 16)
            for w in range(2, NW):
                if w >= NSTG + 2:
                    eng.wait_ge(w_lo, w - NSTG - 1)
                eng.dma_start(stage[:, w % NSTG, :], wdram[w]).then_inc(w_in[w % NSTG], 16)

        @block.gpsimd
        def _(eng):
            if "decay" in kinds:
                eng.wait_ge(f_done, 1)
                eng.dma_start(decay_rows, frows[:]).then_inc(f_stored, 16)
                eng.wait_ge(f_stored, 16)
            if adaln is not None:
                eng.dma_start(cond[:], adaln["cond"].unsqueeze(0).to_broadcast([P, 2, D])).then_inc(cond_in, 16)
                eng.wait_ge(cond_ready, 1)
                for f in range(3 * KD):
                    if f >= 2:
                        eng.wait_ge(ring_used, 2 * (f - 1))
                    eng.dma_start(ring[:, f % 2, :], adaln["w"][f]).then_inc(ring_in[f % 2], 16)
            if "gate" in kinds:
                for i, j in enumerate(jobs):
                    if j.kind == "gate":
                        for t, (off, w) in enumerate(j.tiles):
                            if i >= 1:
                                eng.wait_ge(free[(i - 1) % 2], free_before[i - 1] + t + 1)
                            eng.dma_start(gt[:, t, 0:w], j.a.gates[:, off:off + w]).then_inc(gate_in[t], 16)
            if "up" in kinds:
                for e in range(NE):
                    if e >= 2:
                        eng.wait_ge(he_ready, 6 * (e - 1))
                    eng.dma_start(cb[:, e % 2, :], comb["dram"][e:e + 1, :].to_broadcast([P, L2])).then_inc(cb_in[e % 2], 16)

        @block.scalar
        def _(eng):
            def round_w(w):
                eng.wait_ge(w_in[w % NSTG], 16 * (w // NSTG + (w % NSTG >= 2)))
                eng.activation(whi[:, w % 2, :], stage[:, w % NSTG, :], ACT.Copy).then_inc(w_hi, 1)
            def store(i):
                n, j = turn[i], jobs[i]
                width = j.tiles[-1][0] + j.tiles[-1][1]
                if j.kind == "store":
                    eng.wait_ge(free[i % 2], free_before[i] + len(j.tiles))
                else:
                    eng.wait_ge(rope_done, ropes_tiles[i] + len(j.tiles))
                eng.dma_start(j.a.out[:, 0:width], outb[:, n % 2, 0:width]).then_inc(out_stored[n % 2], 16)

            def roots(i):
                for t, (off, n) in enumerate(jobs[i].tiles):
                    r = ropes_tiles[i] + t
                    eng.wait_ge(aux_done, r + 1)
                    if r >= 1:
                        eng.wait_ge(rope_done, r)
                    eng.activation(rs[:, 0:n], aux[0][:, 0:n], ACT.Ln, scale=1.0 / HD, bias=E.eps[:]).then_inc(ms_ready, 1)
                    eng.wait_ge(ms_ready, r + 1)
                    eng.activation(rs[:, 0:n], rs[:, 0:n], ACT.Exp, scale=-0.5).then_inc(rs_ready, 1)

            for i, j in enumerate(jobs):
                if adaln is not None and i == 1:
                    eng.wait_ge(cond_in, 16)
                    eng.activation(ring[:], cond[:], ACT.Exp, scale=-1.0).then_inc(cond_exp, 1)
                if i >= 1 and jobs[i - 1].kind == "rope":
                    roots(i - 1)
                    store(i - 1)
                if last_job[j.w] == i and j.w + 2 < NW:
                    eng.wait_ge(mm, tiles_before[i + 1])
                    round_w(j.w + 2)
                a = acc[i % 2]
                for t, (off, n) in enumerate(j.tiles):
                    src = a[:, t, 0:n]
                    if j.kind == "store":
                        if t == 0 and turn[i] >= 2:
                            eng.wait_ge(out_stored[turn[i] % 2], 16 * (turn[i] // 2))
                        eng.wait_ge(mm, tiles_before[i] + t + 1)
                        eng.activation(outb[:, turn[i] % 2, off:off + n], src, j.a.func).then_inc(free[i % 2], 1)
                    elif j.kind == "rope":
                        if t == 0 and i != ropes[0]:
                            eng.wait_ge(rope_done, ropes_tiles[i])
                        eng.wait_ge(mm, tiles_before[i] + t + 1)
                        eng.activation(sq[:, off:off + n], src, ACT.Square).then_inc(xg_ready, 1)
                        eng.activation(xg[:, off:off + n], src, ACT.Copy, scale=j.a.gain).then_inc(free[i % 2], 1)
                    elif j.kind == "decay":
                        eng.wait_ge(mm, tiles_before[i] + t + 1)
                        eng.activation(fz[:, off:off + n], src[0:FH, :], ACT.Identity,
                                       bias=col(E.par, PARAM_AT, "bforget")[0:FH, :]).then_inc(free[i % 2], 1)
                    elif j.kind == "up":
                        q = order[i, t]
                        if q >= 3:
                            eng.wait_ge(he_ready, q - 2)
                        eng.wait_ge(mm, tiles_before[i] + t + 1)
                        eng.activation(s1[:, off:off + n], src, ACT.Silu).then_inc(free[i % 2], 1)
                    elif j.kind == "he":
                        q = order[i, t]
                        if j.a.reuse is not None:
                            eng.wait_ge(mm, tiles_before[j.a.reuse + 1])
                        eng.wait_ge(he_ready, q + 1)
                        eng.activation(hhi[:, j.a.slot, off:off + n], h2[:, t, 0:n], ACT.Copy).then_inc(he_hi, 1)
                    elif j.kind == "gate" and j.a.last:
                        eng.wait_ge(gated, 6 * j.a.f + 3 + t + 1)
                        eng.activation(halves(j.a.hi[:, j.a.f, off:off + n]), merged(t, n), ACT.Copy).then_inc(m_hi, 1)
                if j.kind == "store":
                    store(i)
                if j.kind == "decay":
                    eng.wait_ge(free[i % 2], len(j.tiles))
                    eng.activation(fa[:], fz[:], ACT.Abs).then_inc(f_act, 1)
                    eng.wait_ge(f_act, 1)
                    eng.activation(fa[:], fa[:], ACT.Exp, scale=-1.0).then_inc(f_act, 1)
                    eng.wait_ge(f_act, 2)
                    eng.activation(fa[:], fa[:], ACT.Ln, bias=1.0).then_inc(f_act, 1)
            if jobs[-1].kind == "rope":
                roots(NJ - 1)
                store(NJ - 1)
            for b in range(2):
                if len(storing) > b:
                    eng.wait_ge(out_stored[b], 16 * ((len(storing) - b + 1) // 2))

        @block.vector
        def _(eng):
            chain = Chain(eng, steps)

            def split_w(w):
                eng.wait_ge(w_hi, w - 1)
                eng.tensor_tensor(wlo[:, w % 2, :], stage[:, w % NSTG, :], whi[:, w % 2, :].bitcast(F32),
                                  ALU.subtract).then_inc(w_lo, 1)

            def hidden(i, j):
                e = order[i, 0] // 6
                for t, (off, n) in enumerate(j.tiles):
                    eng.wait_ge(mm, tiles_before[i] + t + 1)
                    eng.wait_ge(free[1 - i % 2], free_before[i - 1] + t + 1)
                    if order[i, t] >= 3:
                        eng.wait_ge(he_lo, order[i, t] - 2)
                    eng.tensor_tensor(h2[:, t, 0:n], acc[i % 2][:, t, 0:n], s1[:, off:off + n],
                                      ALU.mult).then_inc(free[i % 2], 1)
                if order[i, 0] % 6 == 0:
                    eng.wait_ge(cb_in[e % 2], 16 * (e // 2 + 1))
                for t, (off, n) in enumerate(j.tiles):
                    eng.wait_ge(free[i % 2], free_before[i] + t + 1)
                    eng.tensor_tensor(h2[:, t, 0:n], h2[:, t, 0:n], cb[:, e % 2, off:off + n], ALU.mult).then_inc(he_ready, 1)
                for t, (off, n) in enumerate(j.tiles):
                    eng.wait_ge(he_hi, order[i, t] + 1)
                    eng.tensor_tensor(hlo[:, j.a.slot, off:off + n], h2[:, t, 0:n],
                                      hhi[:, j.a.slot, off:off + n].bitcast(F32), ALU.subtract).then_inc(he_lo, 1)

            def log_sigmoid():
                eng.wait_ge(f_act, 3)
                chain(eng.memset(fo[:], 1.0))
                chain(eng.scalar_tensor_tensor(fz[:], fz[:], 0.0, fa[:], ALU.min, ALU.subtract))
                chain(eng.tensor_scalar(fz[:], fz[:], 1.0 / SCALE, None, ALU.mult))

            def decay_sums():
                chain(eng.tensor_tensor_scan(fa[:], fo[:], fz[:], 0.0, ALU.mult, ALU.add))

            def decay_split():
                chain(eng.tensor_copy(frows[:, 0, :], fa[:]))
                chain(eng.tensor_tensor(frows[:, 1, :], fa[:], frows[:, 0, :].bitcast(F32), ALU.subtract))

            def decay_row(j):
                chain(eng.tensor_copy(frows[:, 2 + j, :], fo[:]))
                chain(eng.tensor_scalar(frows[:, 4 + j, :], frows[:, j, :].bitcast(F32), -1.0, None, ALU.mult))
                if j:
                    eng.engine_nop().then_inc(f_done, 1)

            decay_steps = [log_sigmoid, decay_sums, decay_split, lambda: decay_row(0), lambda: decay_row(1)]

            def silu_rows(step):
                if step == 0:
                    eng.wait_ge(cond_exp, 1)
                    chain(eng.tensor_scalar(ring[:], ring[:], 1.0, None, ALU.add))
                elif step == 1:
                    chain(eng.reciprocal(ring[:], ring[:]))
                else:
                    eng.tensor_tensor(cond[:], cond[:], ring[:], ALU.mult).then_inc(cond_ready, 1)

            def modulate(f):
                eng.wait_ge(ring_in[f % 2], 16 * (f // 2 + 1))
                for c in range(2):
                    if 2 * f + c:
                        eng.wait_ge(ring_used, 2 * f + c)
                    else:
                        eng.wait_ge(cond_ready, 1)
                    eng.scalar_tensor_tensor(junk[:], ring[:, f % 2, :], 1.0, cond[:, c, :], ALU.mult, ALU.mult,
                                             accum_out=E.mod[:, 1, 2 * f + c:2 * f + c + 1]).then_inc(ring_used, 1)

            if "rope" in kinds:
                eng.wait_ge(tab_in, 16)
            n_hi, n_gated = [0], [0]
            for i, j in enumerate(jobs):
                if last_job[j.w] == i and j.w + 2 < NW:
                    split_w(j.w + 2)
                a = acc[i % 2]
                if j.kind == "he":
                    hidden(i, j)
                    continue
                for t, (off, n) in enumerate(j.tiles):
                    src = a[:, t, 0:n]
                    if j.kind == "resid":
                        eng.wait_ge(mm, tiles_before[i] + t + 1)
                        xs = E.X[:, j.a.f, X0 + off:X0 + off + n]
                        eng.scalar_tensor_tensor(xs, src, j.a.gate_of(t), xs, ALU.mult, ALU.add).then_inc(free[i % 2], 1)
                    elif j.kind in ("add", "down"):
                        eng.wait_ge(mm, tiles_before[i] + t + 1)
                        xs = E.X[:, j.a.f, off:off + n]
                        q = order.get((i, t), 0)
                        eng.tensor_tensor(xs, src, xs, ALU.add).then_inc(free[i % 2], 1)
                    elif j.kind == "rope":
                        r = ropes_tiles[i] + t
                        if t == 0 and turn[i] >= 2:
                            eng.wait_ge(out_stored[turn[i] % 2], 16 * (turn[i] // 2))
                        eng.wait_ge(aux_done, r + 1)
                        out = outb[:, turn[i] % 2, off:off + n]
                        if off < T:
                            eng.tensor_tensor(t2[:, 0:n], aux[1][:, 0:n], tab[:, 1, off:off + n], ALU.mult)
                            chain(eng.tensor_tensor(t1[:, 0:n], xg[:, off:off + n], tab[:, 0, off:off + n], ALU.mult))
                            chain(eng.tensor_tensor(t1[:, 0:n], t1[:, 0:n], t2[:, 0:n], ALU.add))
                        eng.wait_ge(rs_ready, r + 1)
                        if off < T:
                            ins = eng.tensor_tensor(out, t1[:, 0:n], rs[:, 0:n], ALU.mult)
                        else:
                            ins = eng.tensor_tensor(out, xg[:, off:off + n], rs[:, 0:n], ALU.mult)
                        ins.then_inc(rope_done, 1)
                    elif j.kind == "gate":
                        q = order[i, t]
                        g = q // 3
                        eng.wait_ge(mm, tiles_before[i] + t + 1)
                        eng.wait_ge(gate_in[t], 16 * (g + 1))
                        m, gate, x = merged(t, n), halves(gt[:, t, 0:n]), halves(src)
                        if j.a.first:
                            if q >= 9:
                                eng.wait_ge(m_lo, q // 9 * 3 - 3 + t + 1)
                            eng.tensor_tensor(m, x, gate, ALU.mult).then_inc(free[i % 2], 1)
                            eng.wait_ge(free[i % 2], free_before[i] + t + 1)
                        else:
                            if n_gated[0]:
                                eng.wait_ge(gated, n_gated[0])
                            n_gated[0] += 1
                            eng.tensor_tensor(halves(gtmp[:, 0:n]), x, gate, ALU.mult).then_inc(free[i % 2], 1)
                            eng.wait_ge(free[i % 2], free_before[i] + t + 1)
                            eng.tensor_tensor(m, m, halves(gtmp[:, 0:n]), ALU.add).then_inc(gated, 1)
                        if j.a.last:
                            n_hi[0] += 1
                            eng.wait_ge(m_hi, n_hi[0])
                            eng.tensor_tensor(halves(j.a.lo[:, j.a.f, off:off + n]), m,
                                              halves(j.a.hi[:, j.a.f, off:off + n]).bitcast(F32),
                                              ALU.subtract).then_inc(m_lo, 1)
                if "decay" in kinds and 1 <= i <= len(decay_steps):
                    decay_steps[i - 1]()
                if adaln is not None and 1 <= i < 4:
                    silu_rows(i - 1)
                if adaln is not None and i >= 5:
                    modulate(i - 5)

            if adaln is not None:
                for f in range(NJ - 5, 3 * KD):
                    modulate(f)
                eng.wait_ge(ring_used, 6 * KD)
                modulation(eng, chain, E, 1, E.mod[:, 1, :])

        @block.tensor
        def _(eng):
            pending = []

            def rope_aux(i, t):
                j = jobs[i]
                off, n = j.tiles[t]
                r = ropes_tiles[i] + t
                eng.wait_ge(free[i % 2], free_before[i] + t + 1)
                if r >= 1:
                    eng.wait_ge(rope_done, r)
                if off < T:
                    eng.matmul(aux[1][:, 0:n], col(E.con, CONST_AT, "rot"), xg[:, off:off + n],
                               start=True, stop=True)
                eng.matmul(aux[0][:, 0:n], col(E.con, CONST_AT, "headones"), sq[:, off:off + n],
                           start=True, stop=True).then_inc(aux_done, 1)

            for i, j in enumerate(jobs):
                a = acc[i % 2]
                if j.w >= 2:
                    eng.wait_ge(w_lo, j.w - 1)
                if i >= 2:
                    eng.wait_ge(free[i % 2], free_before[i])
                if j.a.merged:
                    eng.wait_ge(m_lo, 3 * KD)
                if j.kind == "down":
                    eng.wait_ge(he_lo, j.a.needs)
                hi, lo, c0 = j.rhs
                nk = j.k1 - j.k0
                for k in range(nk):
                    kb = (j.k0 + k) * P
                    for lhs, rhs in ((whi, hi), (whi, lo), (wlo, hi)):
                        first, last = k == 0 and lhs is whi and rhs is hi, k == nk - 1 and lhs is wlo
                        for t, (off, n) in enumerate(j.tiles):
                            mmi = eng.matmul(a[:, t, 0:n], lhs[:, j.w % 2, kb:kb + P],
                                             rhs[:, c0 + k, off:off + n], start=first, stop=last)
                            if last:
                                mmi.then_inc(mm, 1)
                    if k % 2 == 1 and pending:
                        rope_aux(*pending.pop(0))
                while pending:
                    rope_aux(*pending.pop(0))
                if j.kind == "rope":
                    pending = [(i, t) for t in range(len(j.tiles))]
            while pending:
                rope_aux(*pending.pop(0))


def split_phase(nc, src_dram, n_chunks, width, hi, lo, wts, ring=6):
    half = width // 2
    pieces = [(c, off) for c in range(n_chunks) for off in (0, half)]
    with ExitStack() as ctx:
        sb, ps, sem = phase(nc, ctx)
        stage = sb("stage", [P, ring, half])
        loaded = [sem(f"loaded{i}") for i in range(ring)]
        rounded, split = sem("rounded"), sem("split")
        wts.sems(sem)
        block = ctx.enter_context(nc.Block())

        @block.sync
        def _(eng):
            for i, (c, off) in enumerate(pieces):
                if i >= ring:
                    eng.wait_ge(split, i - ring + 1)
                eng.dma_start(stage[:, i % ring, :], src_dram(c)[:, off:off + half]).then_inc(loaded[i % ring], 16)
                if i == ring - 1:
                    wts.first_loads(eng)

        @block.scalar
        def _(eng):
            for i, (c, off) in enumerate(pieces):
                eng.wait_ge(loaded[i % ring], 16 * (i // ring + 1))
                eng.activation(hi[:, c, off:off + half], stage[:, i % ring, :], ACT.Copy).then_inc(rounded, 1)
            wts.first_hi(eng)

        @block.vector
        def _(eng):
            for i, (c, off) in enumerate(pieces):
                eng.wait_ge(rounded, i + 1)
                eng.tensor_tensor(lo[:, c, off:off + half], stage[:, i % ring, :],
                                  hi[:, c, off:off + half].bitcast(F32), ALU.subtract).then_inc(split, 1)
            wts.first_lo(eng)


class Unit:
    def __init__(self, side, q0, blocks, masks=()):
        self.side, self.q0, self.blocks, self.masks = side, q0, blocks, dict(masks)
        self.at, n = [], 0
        for _, w in blocks:
            self.at.append(n)
            n += w
        self.width = n
        self.segs = []
        for at, (tok, w) in zip(self.at, blocks):
            last = self.segs[-1] if self.segs else None
            if last and last[1] + last[2] == tok and last[0] // 512 == (at + w - 1) // 512:
                self.segs[-1] = (last[0], last[1], last[2] + w)
            else:
                self.segs.append((at, tok, w))


class Chunk:
    def __init__(self, q, k, v, gate, out, units, sinks=None, frow=None, vcols=None, kv_same=False):
        self.q, self.k, self.v, self.gate, self.out, self.units = q, k, v, gate, out, units
        self.sinks, self.frow, self.vcols, self.kv_same = sinks, frow, vcols, kv_same


def attention_phase(nc, E, NT, chunks, mode, conv=None):
    diff, fox, sink = mode == "diff", mode == "fox", mode == "sink"
    with ExitStack() as ctx:
        sb, ps, sem = phase(nc, ctx)
        WMAX = max(u.width for c in chunks for u in c.units)
        NB = -(-NT // P)
        NC = len(chunks)
        qraw, kraw, vraw = sb("q_raw", [P, 2, NT]), sb("k_raw", [P, 2, NT]), sb("v_raw", [P, NT])
        qs, kh, kl = (sb(n, [P, 2, 2, NT], F32R) for n in ("q_stack", "k_hi", "k_lo"))
        if fox:
            q2 = sb("q_rows", [P, 2, 2, NT], F32R)
        LR = 68 if fox else 64
        v = sb("v", [P, NB, P])
        if not fox:
            gate = sb("gate", [P, 2, NT])
        oT = sb("o_t", [P, 2, NT])
        pr = sb("probs", [P, 4, WMAX])
        if diff:
            wd = sb("diff_w", [P, 2, WMAX])
        pT = sb("probs_t", [P, 2, WMAX if WMAX % P == 0 else (WMAX // P + 1) * P])
        on = sb("o_n", [P, 4, P])
        osq = sb("o_sq", [P, P])
        st = sb("stats", [P, 4, 4])
        un = sb("unit_stats", [P, 4, 4])
        SBK = -(-WMAX // 512)
        SB1 = SBK if diff else 2
        NTB = 2 if SBK + SB1 < 6 else 1
        NOB = 8 - SBK - SB1 - NTB
        S = [ps("scores0", [P, SBK * 512]), ps("scores1", [P, SB1 * 512])]
        TB = [ps(f"transposed{i}", [P, 512]) for i in range(NTB)]
        OB = [ps(f"outputs{i}", [P, 512]) for i in range(NOB)]
        (raw_in, v_in, hi_ready, lo_ready, scored, maxed, exped, sinked, w_ready, t_done, pv_done,
         on_ready, out_ready, rows_in, steps) = (
            sem(n) for n in ("qk_loaded", "v_loaded", "hi_ready", "lo_ready", "scored", "max_ready", "exp_ready",
                             "sink_ready", "diff_ready", "transposed", "pv_done", "o_n_ready",
                             "out_ready", "gp_rows_loaded", "dve_steps"))
        o_read = sem("o_read")
        copied = [sem(f"transposed_copied{i}") for i in range(NTB)]
        ss_ready, ms_ready, root_ready = sem("o_square_ready"), sem("o_mean_ready"), sem("o_root_ready")
        gate_in = [sem(f"gate_loaded{i}") for i in range(2)]
        stored = [sem(f"gp_stored{i}") for i in range(2)]
        k_in = sem("gp_k_loaded")
        if conv:
            cv, cg, cy = sb("conv_v", [P, L2]), sb("conv_g", [P, L2]), sb("conv_y", [P, 2, L2])
            glu = sb("glu", [P, CONV_K - 1 + L2])
            conv_in, conv_out, conv_step = sem("gp_conv_loaded"), sem("gp_conv_stored"), sem("conv_step")

        load_exp_ln(nc)
        block = ctx.enter_context(nc.Block())

        units = [(c, u) for c, ch in enumerate(chunks) for u in ch.units]
        NU = len(units)
        s_of, s_last = [], []
        for q in range(NU * (2 if diff else 1)):
            wide = units[q // 2 if diff else q][1].width > SB1 * 512
            s_of.append(0 if wide or q == 0 else 1 - s_of[-1])
            same = [p for p in range(q) if s_of[p] == s_of[q]]
            s_last.append(same[-1] if same else None)
        per = 2 if diff else 1
        per_out = 1 if diff else 2
        dv = P if diff else HD
        first_unit = [sum(len(ch.units) for ch in chunks[:c]) for c in range(NC + 1)]
        outs_before = [n // per_out for n in first_unit]
        NO = NU // per_out
        next_chunk = {first_unit[c] + 3 + 2 * a: (c + 1, a) for c in range(NC - 1) for a in range(2)}
        LAG = 2

        def outputs_after(i):
            if (i + 1) % per_out:
                return []
            m = (i + 1) // per_out - 1
            return ([m - LAG] if m >= LAG else []) + (list(range(NO - LAG, NO)) if m == NO - 1 else [])

        NG = -(-NB // 4)
        groups = [[list(range(g, min(g + 4, len(u.blocks)))) for g in range(0, len(u.blocks), 4)] for _, u in units]
        group_no, v_group_no, o_group_no, n = {}, {}, {}, 0
        for i, (c, u) in enumerate(units):
            if i == first_unit[c]:
                v_group_no[c] = n
                n += NG
            for g in range(len(groups[i])):
                group_no[i, g] = n
                n += 1
            for m in outputs_after(i):
                o_group_no[m] = n
                n += 1

        def by_vector(g):
            return not diff and g % 2 == 1

        @block.sync
        def _(eng):
            for c, ch in enumerate(chunks):
                if c >= 1:
                    eng.wait_ge(lo_ready, 4 * c)
                for a in range(2):
                    for half in range(2):
                        eng.dma_start(qraw[64 * half:64 * half + 64, a, :], ch.q[a]).then_inc(raw_in, 16)
                if c >= 1:
                    eng.wait_ge(t_done, v_group_no[c - 1] + NG)
                eng.dma_start(vraw[:], ch.v).then_inc(v_in, 16)
                if not fox:
                    if c >= 2:
                        eng.wait_ge(out_ready, outs_before[c - 1])
                    eng.dma_start(gate[:, c % 2, :], ch.gate).then_inc(gate_in[c % 2], 16)
                eng.wait_ge(raw_in, 64 * (c + 2))
                eng.wait_ge(v_in, 16 * (c + 1))

        @block.gpsimd
        def _(eng):
            def keys(c):
                eng.wait_ge(lo_ready, 4 * c)
                for a in range(2):
                    for half in range(2):
                        eng.dma_start(kraw[64 * half:64 * half + 64, a, :], chunks[c].k[a]).then_inc(k_in, 16)
                eng.wait_ge(k_in, 64 * c)

            def store(c):
                eng.wait_ge(out_ready, outs_before[c + 1])
                eng.dma_start(chunks[c].out, oT[:, c % 2, :]).then_inc(stored[c % 2], 16)

            def conv_loads(j):
                if j:
                    eng.wait_ge(conv_step, CONV_K + 2)
                eng.dma_start(cv[:], conv["p"][2 + j]).then_inc(conv_in, 16)
                eng.dma_start(cg[:], conv["p"][4 + j]).then_inc(conv_in, 16)

            def conv_store(j):
                eng.wait_ge(conv_step, 1 + (CONV_K + 1) * (j + 1))
                eng.dma_start(conv["out"][j], cy[:, j, :]).then_inc(conv_out, 16)

            def rows(c):
                if c >= 2:
                    eng.wait_ge(scored, first_unit[c - 1])
                for a in range(2):
                    f, one, nf = chunks[c].frow[a]
                    eng.dma_start(q2[64:66, c % 2, a, :], f).then_inc(rows_in, 16)
                    eng.dma_start(q2[66:68, c % 2, a, :], one).then_inc(rows_in, 16)
                    eng.dma_start(kl[64:66, c % 2, a, :], one).then_inc(rows_in, 16)
                    eng.dma_start(kl[66:68, c % 2, a, :], nf).then_inc(rows_in, 16)
                eng.wait_ge(rows_in, 128 * (c + 1))
            if fox:
                rows(0)
                conv_loads(0)
            keys(1)
            if fox:
                rows(1)
            for c in range(NC):
                if c + 2 < NC:
                    keys(c + 2)
                if fox and c == 1:
                    conv_loads(1)
                store(c)
                if fox and c + 2 < NC:
                    rows(c + 2)
                if fox and c >= NC - 2:
                    conv_store(c - (NC - 2))
            if fox:
                eng.wait_ge(conv_out, 32)
            for b in range(2):
                if NC > b:
                    eng.wait_ge(stored[b], 16 * ((NC - b + 1) // 2))

        def softmaxes(i):
            return [(2 * i + a, a) for a in range(2)] if diff else [(i, units[i][1].side)]

        def copy_group(eng, copy, i, g):
            u = units[i][1]
            eng.wait_ge(t_done, group_no[i, g] + 1)
            full = [b for b in groups[i][g] if u.blocks[b][1] == P]
            b0 = groups[i][g][0]
            T1 = TB[group_no[i, g] % NTB]
            ins = None
            if full:
                ins = copy(pT[:, i % 2, b0 * P:(b0 + len(full)) * P], T1[:, 0:len(full) * P])
            for b in groups[i][g][len(full):]:
                w, at = u.blocks[b][1], (b - b0) * P
                ins = copy(pT[0:w, i % 2, b * P:b * P + P], T1[0:w, at:at + P])
            ins.then_inc(copied[group_no[i, g] % NTB], 1)

        @block.scalar
        def _(eng):
            def copy(out, in_):
                return eng.activation(out, in_, ACT.Copy)

            def round_qk(c, a):
                eng.wait_ge(raw_in, 64 * (c + 2))
                if c >= 1:
                    eng.wait_ge(k_in, 64 * c)
                if c >= 2:
                    eng.wait_ge(scored, per * first_unit[c - 1])
                if fox:
                    copy(q2[0:64, c % 2, a, :], qraw[0:64, a, :])
                copy(qs[:, c % 2, a, :], qraw[:, a, :]).then_inc(hi_ready, 1)
                copy(kh[:, c % 2, a, :], kraw[:, a, :]).then_inc(hi_ready, 1)

            def exps(i, n):
                c, u = units[i]
                for q, a in softmaxes(i)[n:n + 1]:
                    eng.wait_ge(maxed, q + 1)
                    if diff and i >= 2:
                        eng.wait_ge(w_ready, i - 1)
                    if not diff and i >= 4:
                        eng.wait_ge(t_done, group_no[i - 4, len(groups[i - 4]) - 1] + 1)
                    eng.activation(pr[:, q % 4, 0:u.width], S[s_of[q]][:, 0:u.width], ACT.Exp,
                                   bias=st[:, q % 4, 1:2], scale=SCALE,
                                   accum_out=st[:, q % 4, 2:3]).then_inc(exped, 1)
                    if sink:
                        eng.activation(st[:, q % 4, 3:4], col(E.par, PARAM_AT, "sink", chunks[c].sinks[a]),
                                       ACT.Exp, bias=st[:, q % 4, 1:2]).then_inc(sinked, 1)

            def root(i):
                r = un[:, i % 4, 3:4]
                eng.wait_ge(ss_ready, i + 1)
                eng.activation(r, r, ACT.Ln, scale=1.0 / P, bias=E.eps[:]).then_inc(ms_ready, 1)
                eng.wait_ge(ms_ready, i + 1)
                eng.activation(r, r, ACT.Exp, scale=-0.5).then_inc(root_ready, 1)

            for a in range(2):
                for half in range(2):
                    eng.dma_start(kraw[64 * half:64 * half + 64, a, :], chunks[0].k[a]).then_inc(raw_in, 16)
            for a in range(2):
                round_qk(0, a)
            for n in range(per):
                exps(0, n)
            for i in range(NU + 1):
                j = i - 1
                if i in next_chunk:
                    round_qk(*next_chunk[i])
                if j >= 0:
                    for g in range(len(groups[j])):
                        if not by_vector(g):
                            copy_group(eng, copy, j, g)
                if i + 1 < NU:
                    exps(i + 1, 0)
                if diff and j >= 1:
                    root(j - 1)
                if diff and i + 1 < NU:
                    exps(i + 1, 1)
            if diff:
                root(NU - 1)

        @block.vector
        def _(eng):
            chain = Chain(eng, steps)

            def split_qk(c, a):
                eng.wait_ge(hi_ready, 4 * c + 2 * a + 1)
                up = qs[64:128, c % 2, a, :]
                eng.tensor_tensor(up, qraw[64:128, a, :], up.bitcast(F32), ALU.subtract).then_inc(lo_ready, 1)
                eng.wait_ge(hi_ready, 4 * c + 2 * a + 2)
                eng.tensor_tensor(kl[0:64, c % 2, a, :], kraw[0:64, a, :],
                                  kh[0:64, c % 2, a, :].bitcast(F32), ALU.subtract).then_inc(lo_ready, 1)

            def maxes(i, n):
                u = units[i][1]
                for q, a in softmaxes(i)[n:n + 1]:
                    eng.wait_ge(scored, q + 1)
                    if q >= 4:
                        eng.wait_ge(exped, q - 3)
                        if sink:
                            eng.wait_ge(sinked, q - 3)
                    chain(eng.tensor_reduce(st[:, q % 4, 0:1], S[s_of[q]][:, 0:u.width], AX, ALU.max))
                    if sink:
                        h = chunks[units[i][0]].sinks[a]
                        ins = eng.tensor_scalar(st[:, q % 4, 1:2], st[:, q % 4, 0:1], -SCALE,
                                                E.nsink[:, h:h + 1], ALU.mult, ALU.min)
                    else:
                        ins = eng.tensor_scalar(st[:, q % 4, 1:2], st[:, q % 4, 0:1], -SCALE, None, ALU.mult)
                    ins.then_inc(maxed, 1)

            def weights(i):
                u, r = units[i][1], un[:, i % 4, :]
                eng.wait_ge(exped, per * (i + 1))
                if diff:
                    q0, q1 = 2 * i % 4, (2 * i + 1) % 4
                    chain(eng.reciprocal(r[:, 0:1], st[:, q1, 2:3]))
                    chain(eng.scalar_tensor_tensor(r[:, 1:2], st[:, q0, 2:3], E.neglam[:], r[:, 0:1], ALU.mult, ALU.mult))
                    if i >= 2:
                        eng.wait_ge(t_done, group_no[i - 2, len(groups[i - 2]) - 1] + 1)
                    chain(eng.reciprocal(r[:, 2:3], st[:, q0, 2:3]))
                    eng.scalar_tensor_tensor(wd[:, i % 2, 0:u.width], pr[:, q1, 0:u.width], r[:, 1:2], pr[:, q0, 0:u.width],
                                             ALU.mult, ALU.add).then_inc(w_ready, 1)
                elif sink:
                    eng.wait_ge(sinked, i + 1)
                    chain(eng.tensor_tensor(r[:, 1:2], st[:, i % 4, 2:3], st[:, i % 4, 3:4], ALU.add))
                    chain(eng.reciprocal(r[:, 2:3], r[:, 1:2]))
                else:
                    chain(eng.reciprocal(r[:, 2:3], st[:, i % 4, 2:3]))

            def output(m):
                i = per_out * m
                eng.wait_ge(pv_done, i + per_out)
                if m >= 4:
                    eng.wait_ge(t_done, o_group_no[m - 4] + 1)
                for n in range(per_out):
                    at = HD * units[i + n][1].side
                    dst = on[:, m % 4, at:at + dv]
                    ins = eng.tensor_scalar(dst, OB[m % NOB][:, at:at + dv], un[:, (i + n) % 4, 2:3], None, ALU.mult)
                ins.then_inc(o_read, 1)
                if not diff:
                    return
                eng.wait_ge(o_read, m + 1)
                eng.scalar_tensor_tensor(osq[:], dst, 1.0, dst, ALU.mult, ALU.mult,
                                         accum_out=un[:, i % 4, 3:4]).then_inc(ss_ready, 1)

            def normalise(i):
                eng.wait_ge(root_ready, i + 1)
                dst = on[:, i % 4, :]
                eng.tensor_scalar(dst, dst, un[:, i % 4, 3:4], None, ALU.mult).then_inc(on_ready, 1)

            def finish(m):
                c, u = units[m * per_out]
                g = o_group_no[m]
                eng.wait_ge(t_done, g + 1)
                if m == outs_before[c]:
                    if c >= 2:
                        eng.wait_ge(stored[c % 2], 16 * (c // 2))
                    if not fox:
                        eng.wait_ge(gate_in[c % 2], 16 * (c // 2 + 1))
                src = TB[g % NTB][:, 0:P]
                dst = oT[:, c % 2, u.q0:u.q0 + P]
                if fox:
                    ins = eng.tensor_copy(dst, src)
                elif sink:
                    ins = eng.tensor_tensor(dst, src, gate[:, c % 2, u.q0:u.q0 + P], ALU.mult)
                else:
                    ins = eng.scalar_tensor_tensor(dst, src, E.subln[:], gate[:, c % 2, u.q0:u.q0 + P],
                                                   ALU.mult, ALU.mult)
                ins.then_inc(copied[g % NTB], 1)
                eng.wait_ge(copied[g % NTB], g // NTB + 1)
                eng.engine_nop().then_inc(out_ready, 1)

            def values(c):
                for g in range(NG):
                    eng.wait_ge(t_done, v_group_no[c] + g + 1)
                    T1 = TB[(v_group_no[c] + g) % NTB]
                    nb = min(4, NB - 4 * g)
                    rest = NT - 4 * g * P
                    full = min(nb, rest // P)
                    ins = None
                    if full:
                        ins = eng.tensor_copy(v[:, 4 * g:4 * g + full, :],
                                              T1[:, 0:full * P].rearrange("p (b f) -> p b f", f=P))
                    if full < nb:
                        w = rest - full * P
                        ins = eng.tensor_copy(v[0:w, 4 * g + full, :], T1[0:w, full * P:(full + 1) * P])
                    ins.then_inc(copied[(v_group_no[c] + g) % NTB], 1)

            if diff:
                chain(eng.tensor_scalar(E.subln[:], col(E.par, PARAM_AT, "subln"), 1.0 - LAMBDA_INIT, None, ALU.mult))
            def tap(n):
                j, i = divmod(n, CONV_K + 1)
                if i == 0:
                    eng.wait_ge(conv_in, 32 * (j + 1))
                eng.wait_ge(conv_step, n + 1)
                w = col(E.par, PARAM_AT, "conv_w", CONV_K * j + max(i - 1, 0))
                y, x = cy[:, j, :], glu[:, max(i - 1, 0):max(i - 1, 0) + L2]
                if i == 0:
                    ins = eng.tensor_tensor(glu[:, CONV_K - 1:], cv[:], cg[:], ALU.mult)
                elif i == 1:
                    ins = eng.tensor_scalar(y, x, w, col(E.par, PARAM_AT, "conv_b", j), ALU.mult, ALU.add)
                else:
                    ins = eng.scalar_tensor_tensor(y, x, w, y, ALU.mult, ALU.add)
                ins.then_inc(conv_step, 1)

            if conv:
                eng.memset(glu[:, 0:CONV_K - 1], 0.0).then_inc(conv_step, 1)
            for a in range(2):
                split_qk(0, a)
            for n in range(per):
                maxes(0, n)
            for i in range(NU + 1):
                j = i - 1
                if j >= 0 and j == first_unit[units[j][0]]:
                    values(units[j][0])
                if i + 1 < NU:
                    maxes(i + 1, 0)
                if i < NU:
                    weights(i)
                    if i in next_chunk:
                        split_qk(*next_chunk[i])
                if diff and i + 1 < NU:
                    maxes(i + 1, 1)
                if j < 0:
                    continue
                for g in range(len(groups[j])):
                    if by_vector(g):
                        copy_group(eng, eng.tensor_copy, j, g)
                if j < NU - 1:
                    for m in outputs_after(j):
                        finish(m)
                if (j + 1) % per_out == 0:
                    output(j // per_out)
                if diff and j >= 1:
                    normalise(j - 1)
                if conv and j < 2 * (CONV_K + 1):
                    tap(j)
            if diff:
                normalise(NU - 1)
            for m in outputs_after(NU - 1):
                finish(m)

        @block.tensor
        def _(eng):
            def scores(i, n):
                c, u = units[i]
                if softmaxes(i)[n][0] - per * first_unit[c] in (0, 1):
                    ready = 4 * c + 2 * (softmaxes(i)[n][1] + 1)
                    eng.wait_ge(lo_ready, ready)
                    eng.wait_ge(hi_ready, ready)
                if fox and i == first_unit[c]:
                    eng.wait_ge(rows_in, 128 * (c + 1))
                for q, a in softmaxes(i)[n:n + 1]:
                    if s_last[q] is not None:
                        eng.wait_ge(exped, s_last[q] + 1)
                    s, sl = S[s_of[q]], c % 2
                    second = q2 if fox else qs
                    qcols = slice(u.q0, u.q0 + P)
                    masks = {u.at[b]: m for b, m in u.masks.items()}
                    for at, tok, w in u.segs:
                        inside = [(p0, m) for p0, m in masks.items() if at <= p0 < at + w]
                        eng.matmul(s[:, at:at + w], qs[:, sl, a, qcols], kh[:, sl, a, tok:tok + w],
                                   start=True, stop=False)
                        for p0, (m0, mw) in inside:
                            eng.matmul(s[:, p0:p0 + mw], E.mask[:, 0:P], E.mask[:, m0:m0 + mw], start=False,
                                       stop=False, skip_group_check=True)
                        mmi = eng.matmul(s[:, at:at + w], second[0:LR, sl, a, qcols], kl[0:LR, sl, a, tok:tok + w],
                                         start=False, stop=True)
                    mmi.then_inc(scored, 1)

            def transpose_group(number, parts):
                if number >= NTB:
                    eng.wait_ge(copied[number % NTB], number // NTB)
                for dst, src in parts:
                    ins = eng.transpose(dst, src, col(E.con, CONST_AT, "ident"))
                ins.then_inc(t_done, 1)

            def values(c):
                eng.wait_ge(v_in, 16 * (c + 1))
                for g in range(NG):
                    parts = []
                    T1 = TB[(v_group_no[c] + g) % NTB]
                    for b in range(4 * g, min(4 * g + 4, NB)):
                        w = min(P, NT - b * P)
                        parts.append((T1[0:w, (b - 4 * g) * P:(b - 4 * g + 1) * P], vraw[:, b * P:b * P + w]))
                    transpose_group(v_group_no[c] + g, parts)

            def weights_t(i, g):
                u = units[i][1]
                src = wd[:, i % 2, :] if diff else pr[:, i % 4, :]
                if g == 0:
                    if diff:
                        eng.wait_ge(w_ready, i + 1)
                    else:
                        eng.wait_ge(exped, i + 1)
                b0 = groups[i][g][0]
                T1 = TB[group_no[i, g] % NTB]
                transpose_group(group_no[i, g], [
                    (T1[0:u.blocks[b][1], (b - b0) * P:(b - b0 + 1) * P], src[:, u.at[b]:u.at[b] + u.blocks[b][1]])
                    for b in groups[i][g]])

            def pv(i, g):
                c, u = units[i]
                m = i // per_out
                o0 = HD * u.side
                n = group_no[i, g]
                vc = 0 if diff else chunks[c].vcols[u.side]
                if g == 0 and i == first_unit[c]:
                    for vg in range(v_group_no[c], v_group_no[c] + NG):
                        eng.wait_ge(copied[vg % NTB], vg // NTB + 1)
                eng.wait_ge(copied[n % NTB], n // NTB + 1)
                if g == 0 and m >= NOB:
                    eng.wait_ge(o_read, m - NOB + 1)
                nb = len(u.blocks)
                for b in groups[i][g]:
                    tok, w = u.blocks[b]
                    ins = eng.matmul(OB[m % NOB][:, o0:o0 + dv], pT[0:w, i % 2, b * P:(b + 1) * P],
                                     v[0:w, tok // P, vc:vc + dv], start=b == 0, stop=b == nb - 1)
                if g == len(groups[i]) - 1:
                    ins.then_inc(pv_done, 1)

            def output_t(m):
                eng.wait_ge(on_ready if diff else o_read, m + 1)
                transpose_group(o_group_no[m], [(TB[o_group_no[m] % NTB][:, 0:P], on[:, m % 4, :])])

            for n in range(per):
                scores(0, n)
            for i in range(NU + 1):
                j = i - 1
                G = len(groups[j]) if j >= 0 else 0
                if j >= 0:
                    if j == first_unit[units[j][0]]:
                        values(units[j][0])
                    weights_t(j, 0)
                if i + 1 < NU:
                    scores(i + 1, 0)
                if G > 1:
                    weights_t(j, 1)
                if G:
                    pv(j, 0)
                if G > 2:
                    weights_t(j, 2)
                if diff and i + 1 < NU:
                    scores(i + 1, 1)
                if 0 <= j < NU - 1:
                    for m in outputs_after(j):
                        output_t(m)
                for g in range(1, G):
                    pv(j, g)
            for m in outputs_after(NU - 1):
                output_t(m)


def gla_phase(nc, E, dram):
    with ExitStack() as ctx:
        sb, ps, sem = phase(nc, ctx)
        NP_, NCH, NXC, NCC = T // P, NT1 // GC, T // GC, CTX // GC
        NBK = NT1 // P
        NS = NCH - 1
        ISC = 1.0 / 16.0
        reset = sb("reset", [P, NT1])
        r = sb("rank", [48, NT1])
        wa = sb("wa", [48, GH * GDK])
        q, k, vraw, gate = sb("q", [P, T]), sb("k", [P, NT1]), sb("v_raw", [P, 2, NT1]), sb("gate", [P, 2, T])
        v = sb("v", [P, NBK, GDV])
        M2, A2, CUM2 = sb("log_decay", [P, 2, NT1]), sb("expo", [P, 2, NT1]), sb("cum", [P, 2, NT1])
        bl, dec = sb("chunk_total", [P, 4, NCH]), sb("chunk_decay", [P, 4, NCH])
        QD, KD = sb("q_decayed", [P, 2, T]), sb("k_decayed", [P, 2, T])
        K2, K2T = sb("k_to_end", [P, NT1]), sb("k_to_end_t", [P, 2, NBK, GDK])
        ST = sb("states", [P, 2, NXC, GDV])
        RUN = sb("ctx_state", [P, 2, 2, GDV])
        AT = sb("att", [P, 2, 2, P])
        ATS = sb("att_sum", [P, 2, P])
        OX = sb("o", [P, 2, T])
        sq = K2T[:, :, 0:4, :].rearrange("p e b f -> p e (b f)")
        rs = K2T[:, :, 4:8, :].rearrange("p e b f -> p e (b f)")
        Z = ps("z", [P, 3, 512])
        TR = ps("tr", [P, 512])
        AB, OPB = [ps(f"state_att{i}", [P, 512]) for i in range(2)], [ps(f"o_p{i}", [P, 512]) for i in range(2)]
        (base_in, qk_in, v_in, gate_in, z_done, z_copied, ln_done, cum_done, e_done, kq_done, t_done,
         t_copied, ds_done, state_done, att_done, att_ready, o_done, o_copied, sq_done, ss_done, rs_done,
         out_done, stored, steps, asteps, ms_ready) = (sem(n) for n in (
             "base_loaded", "qk_loaded", "v_loaded", "gate_loaded", "z_done", "z_copied", "ln_done",
             "cum_done", "exps_done", "kq_done", "t_done", "t_copied", "ds_done", "state_done", "att_done",
             "att_ready", "o_done", "o_copied", "sq_done", "ss_done", "rs_done", "out_done", "gp_stored", "dve_steps",
             "act_steps", "mean_square_ready"))
        k2_done = sem("k_to_end_ready")
        load_exp_ln(nc)
        block = ctx.enter_context(nc.Block())
        NVG, NKG = 5, 3
        TG = NVG + 2 * NKG

        @block.sync
        def _(eng):
            eng.dma_start(reset[:], dram["reset"]).then_inc(base_in, 16)
            eng.dma_start(r[0:16, :], dram["rank"][0:16, :]).then_inc(base_in, 16)
            eng.dma_start(r[32:48, :], dram["rank"][16:32, :]).then_inc(base_in, 16)
            eng.dma_start(wa[0:16, :], dram["wa_f"]).then_inc(base_in, 16)
            eng.dma_start(wa[32:48, :], dram["wa_b"]).then_inc(base_in, 16)
            for h in range(GH):
                if h >= 1:
                    eng.wait_ge(kq_done, 2 * h)
                eng.dma_start(q[:], dram["q"](h)).then_inc(qk_in, 16)
                eng.dma_start(k[:], dram["k"](h)).then_inc(qk_in, 16)
                if h >= 1:
                    eng.wait_ge(t_done, TG * (h - 1) + NVG)
                eng.dma_start(vraw[:], dram["v"](h)).then_inc(v_in, 16)
                if h >= 1:
                    eng.wait_ge(out_done, 4 * h)
                eng.dma_start(gate[:], dram["gate"](h)).then_inc(gate_in, 16)
                eng.wait_ge(qk_in, 32 * (h + 1))

        @block.gpsimd
        def _(eng):
            for h in range(GH):
                eng.wait_ge(out_done, 4 * (h + 1))
                eng.dma_start(dram["out"](h), OX[:]).then_inc(stored, 16)
            eng.wait_ge(stored, 16 * GH)

        @block.scalar
        def _(eng):
            chain = Chain(eng, asteps)

            def log1p(g):
                h, d = divmod(g, 2)
                M, A = M2[:, d, :], A2[:, d, :]
                eng.wait_ge(z_done, g + 1)
                if g >= 2:
                    eng.wait_ge(kq_done, g - 1)
                eng.activation(M[:], Z[:].rearrange("p b n -> p (b n)")[:, 0:NT1], ACT.Identity,
                               bias=col(E.par, PARAM_AT, "ba", 4 * d + h)).then_inc(z_copied, 1)
                eng.wait_ge(z_copied, g + 1)
                chain(eng.activation(A[:], M[:], ACT.Abs))
                chain(eng.activation(A[:], A[:], ACT.Exp, scale=-1.0))
                eng.activation(A[:], A[:], ACT.Ln, bias=1.0).then_inc(ln_done, 1)

            def exps(g):
                h, d = divmod(g, 2)
                M, A, CUM = M2[:, d, :], A2[:, d, :], CUM2[:, d, :]
                eng.wait_ge(cum_done, g + 1)
                eng.activation(A[:, 0:T], CUM[:, 0:T], ACT.Exp, scale=ISC)
                chain(eng.activation(M[:], M[:], ACT.Exp, scale=ISC))
                if h >= 2:
                    eng.wait_ge(state_done, 2 * NS * (h - 1))
                eng.activation(dec[:, g % 4, :], bl[:, g % 4, :], ACT.Exp, scale=ISC)
                eng.activation(CUM[:, 0:T], CUM[:, 0:T], ACT.Exp, scale=-ISC).then_inc(e_done, 1)

            def outs(h):
                for p in range(NP_):
                    n = h * NP_ + p
                    eng.wait_ge(o_done, n + 1)
                    if p == 0 and h >= 1:
                        eng.wait_ge(stored, 16 * h)
                    eng.activation(OX[:, :, p * P:(p + 1) * P],
                                   OPB[n % 2][:, 0:256].rearrange("p (e c) -> p e c", e=2),
                                   ACT.Copy).then_inc(o_copied, 1)
                for t in range(2):
                    for e in range(2):
                        n = 4 * h + 2 * t + e
                        if n >= 2:
                            eng.wait_ge(ss_done, n - 1)
                        eng.wait_ge(o_copied, NP_ * (h + 1))
                        eng.activation(sq[:, e, :], OX[:, e, 512 * t:512 * t + 512], ACT.Square).then_inc(sq_done, 1)
                for t in range(2):
                    n = 2 * h + t
                    eng.wait_ge(ss_done, 4 * h + 2 * t + 2)
                    eng.activation(rs[:, t, :], OPB[t][:], ACT.Ln, scale=1.0 / GDV, bias=E.eps[:]).then_inc(ms_ready, 1)
                    eng.wait_ge(ms_ready, n + 1)
                    eng.activation(rs[:, t, :], rs[:, t, :], ACT.Exp, scale=-0.5).then_inc(rs_done, 1)

            eng.wait_ge(base_in, 80)
            for g in range(2):
                log1p(g)
            for g in range(2):
                exps(g)
            for h in range(GH):
                if h + 1 < GH:
                    for g in (2 * h + 2, 2 * h + 3):
                        log1p(g)
                        exps(g)
                outs(h)

        @block.vector
        def _(eng):
            chain = Chain(eng, steps)
            chain(eng.memset(AT[:], 0.0))
            eng.wait_ge(base_in, 80)

            def decays(g):
                h, d = divmod(g, 2)
                M, A, CUM = M2[:, d, :], A2[:, d, :], CUM2[:, d, :]
                eng.wait_ge(ln_done, g + 1)
                chain(eng.scalar_tensor_tensor(M[:], M[:], 0.0, A[:], ALU.min, ALU.subtract))
                if d == 0:
                    chain(eng.tensor_tensor_scan(CUM[:], reset[:], M[:], 0.0, ALU.mult, ALU.add))
                    tot = CUM[:, GC - 1:NT1:GC]
                else:
                    chain(eng.tensor_tensor_scan(CUM[:, ::-1], reset[:], M[:, ::-1], 0.0, ALU.mult, ALU.add))
                    tot = CUM[:, 0:NT1:GC]
                chain(eng.tensor_copy(bl[:, g % 4, :], tot))
                eng.tensor_tensor(M[:].rearrange("p (c t) -> p c t", t=GC),
                                  bl[:, g % 4, :].unsqueeze(2).to_broadcast([P, NCH, GC]),
                                  CUM[:].rearrange("p (c t) -> p c t", t=GC), ALU.subtract).then_inc(cum_done, 1)

            def products(g):
                h, d = divmod(g, 2)
                M, A, CUM = M2[:, d, :], A2[:, d, :], CUM2[:, d, :]
                eng.wait_ge(e_done, g + 1)
                if d == 0:
                    eng.wait_ge(qk_in, 32 * (h + 1))
                    if h >= 1:
                        eng.wait_ge(o_done, NP_ * h)
                if g >= 1:
                    eng.wait_ge(t_done, TG * ((g - 1) // 2) + NVG + NKG * ((g - 1) % 2 + 1))
                eng.tensor_tensor(K2[:], k[:], M[:], ALU.mult).then_inc(k2_done, 1)
                eng.scalar_tensor_tensor(QD[:, d, :], q[:], GDK ** -0.5, A[:, 0:T], ALU.mult, ALU.mult)
                eng.tensor_tensor(KD[:, d, :], k[:, 0:T], CUM[:, 0:T], ALU.mult).then_inc(kq_done, 1)

            def copies(h, g0, n, dst):
                for g in range(n):
                    eng.wait_ge(t_done, TG * h + g0 + g + 1)
                    dst(g).then_inc(t_copied, 1)

            def values(h):
                def dst(g):
                    return eng.tensor_copy(v[:, 2 * g:2 * g + 2, :].rearrange("p b f -> p (b f)"), TR[:])
                copies(h, 0, NVG, dst)

            def keys(h, d):
                def dst(g):
                    nb = min(4, NBK - 4 * g)
                    return eng.tensor_copy(K2T[:, d, 4 * g:4 * g + nb, :].rearrange("p b f -> p (b f)"), TR[:, 0:nb * P])
                copies(h, NVG + NKG * d, NKG, dst)

            def states(h, n0, n1):
                for n in range(n0, n1):
                    for d in range(2):
                        c = chunk_order(d, NXC, NCC)[n]
                        i = 2 * (NS * h + n) + d
                        eng.wait_ge(ds_done, i + 1)
                        dsp = AB[i % 2][:, 0:256]
                        if n < NCC:
                            dst = RUN[:, d, n % 2, :] if n < NCC - 1 else ST[:, d, 0, :]
                            src = RUN[:, d, (n - 1) % 2, :]
                        else:
                            dst, src = ST[:, d, n - NCC + 1, :], ST[:, d, n - NCC, :]
                        if n == 0:
                            ins = eng.tensor_copy(dst, dsp)
                        else:
                            eng.wait_ge(state_done, i - 1)
                            ins = eng.scalar_tensor_tensor(dst, src, dec[:, 2 * (h % 2) + d, c:c + 1], dsp,
                                                           ALU.mult, ALU.add)
                        ins.then_inc(state_done, 1)

            def attend(h):
                for p in range(NP_):
                    n = h * NP_ + p
                    for d, m in enumerate(("causal", "anti")):
                        eng.wait_ge(att_done, 2 * n + 2)
                        at = AB[n % 2][:, 128 * d:128 * d + 128]
                        ins = eng.copy_predicated(AT[:, n % 2, d, :], col(E.con, CONST_AT, m).bitcast(mybir.dt.int32), at)
                        chain(ins)
                    if n >= 2:
                        eng.wait_ge(o_done, n - 1)
                    eng.tensor_tensor(ATS[:, n % 2, :], AT[:, n % 2, 0, :], AT[:, n % 2, 1, :], ALU.add).then_inc(att_ready, 1)

            def finish(h):
                for t in range(2):
                    eng.wait_ge(ss_done, 4 * h + 2 * t + 2)
                    eng.wait_ge(rs_done, 2 * h + t + 1)
                    if t == 0:
                        eng.wait_ge(gate_in, 16 * (h + 1))
                        eng.wait_ge(sq_done, 4 * (h + 1))
                    for e in range(2):
                        o = OX[:, e, 512 * t:512 * t + 512]
                        chain(eng.scalar_tensor_tensor(o, o, col(E.par, PARAM_AT, "out_norm", e), rs[:, t, :], ALU.mult, ALU.mult))
                        eng.tensor_tensor(o, o, gate[:, e, 512 * t:512 * t + 512], ALU.mult).then_inc(out_done, 1)

            decays(0)
            decays(1)
            for h in range(GH):
                values(h)
                products(2 * h)
                if h >= 1:
                    finish(h - 1)
                keys(h, 0)
                products(2 * h + 1)
                keys(h, 1)
                cuts = [0, NS // 3, 2 * NS // 3, NS] if h + 1 < GH else [0, NS]
                for n, (n0, n1) in enumerate(zip(cuts, cuts[1:])):
                    if n:
                        decays(2 * h + 1 + n)
                    states(h, n0, n1)
                attend(h)
            finish(GH - 1)

        @block.tensor
        def _(eng):
            ident = col(E.con, CONST_AT, "ident")

            def group(number, parts):
                if number >= 1:
                    eng.wait_ge(t_copied, number)
                for dst, src in parts:
                    ins = eng.transpose(dst, src, ident)
                ins.then_inc(t_done, 1)

            def z(g):
                h, d = divmod(g, 2)
                if g >= 1:
                    eng.wait_ge(z_copied, g)
                for t, (off, n) in enumerate(TILES1):
                    ins = eng.matmul(Z[:, t, 0:n], wa[32 * d:32 * d + 16, h * P:(h + 1) * P],
                                     r[32 * d:32 * d + 16, off:off + n], start=True, stop=True)
                ins.then_inc(z_done, 1)

            eng.wait_ge(base_in, 80)
            z(0)
            z(1)
            for h in range(GH):
                eng.wait_ge(v_in, 16 * (h + 1))
                for g in range(NVG):
                    group(TG * h + g, [(TR[:, (2 * b + e) * P:(2 * b + e + 1) * P],
                                        vraw[:, e, (2 * g + b) * P:(2 * g + b + 1) * P])
                                       for b in range(2) for e in range(2)])
                for d in range(2):
                    eng.wait_ge(k2_done, 2 * h + d + 1)
                    for g in range(NKG):
                        group(TG * h + NVG + NKG * d + g,
                              [(TR[:, (b - 4 * g) * P:(b - 4 * g + 1) * P], K2[:, b * P:(b + 1) * P])
                               for b in range(4 * g, min(4 * g + 4, NBK))])
                eng.wait_ge(t_copied, TG * (h + 1))
                for n in range(NS):
                    if h + 1 < GH and n in (0, NS // 3):
                        z(2 * h + 2 + (n > 0))
                    for d in range(2):
                        c = chunk_order(d, NXC, NCC)[n]
                        i = 2 * (NS * h + n) + d
                        if i >= 2:
                            eng.wait_ge(state_done, i - 1)
                        rows = slice(GC * (c % 2), GC * (c % 2) + GC)
                        eng.matmul(AB[i % 2][:, 0:256], K2T[rows, d, c // 2, :],
                                   v[rows, c // 2, :], start=True, stop=True).then_inc(ds_done, 1)

                def att(p):
                    n = h * NP_ + p
                    if n >= 2:
                        eng.wait_ge(att_ready, n - 1)
                    for d in range(2):
                        eng.matmul(AB[n % 2][:, 128 * d:128 * d + 128], KD[:, d, p * P:(p + 1) * P], QD[:, d, p * P:(p + 1) * P],
                                   start=True, stop=True).then_inc(att_done, 1)
                eng.wait_ge(state_done, NS * 2 * (h + 1))
                eng.wait_ge(kq_done, 2 * (h + 1))
                att(0)
                for p in range(NP_):
                    n = h * NP_ + p
                    if p + 1 < NP_:
                        att(p + 1)
                    eng.wait_ge(att_ready, n + 1)
                    if n >= 2:
                        eng.wait_ge(o_copied, n - 1)
                    if h >= 1 and p < 2:
                        eng.wait_ge(ms_ready, 2 * h)
                    for e in range(2):
                        o = OPB[n % 2][:, P * e:P * e + P]
                        es = slice(P * e, P * e + P)
                        eng.matmul(o, v[:, p, es], ATS[:, n % 2, :], start=True, stop=False, skip_group_check=True)
                        for j in range(2):
                            c = 2 * p + j
                            for d in range(2):
                                pos = c if d == 0 else NXC - 1 - c
                                ins = eng.matmul(o[:, GC * j:GC * j + GC], ST[:, d, pos, es],
                                                 QD[:, d, GC * c:GC * c + GC], start=False, stop=(j == 1 and d == 1),
                                                 skip_group_check=True)
                    ins.then_inc(o_done, 1)
                for t in range(2):
                    for e in range(2):
                        n = 4 * h + 2 * t + e
                        eng.wait_ge(sq_done, n + 1)
                        eng.matmul(OPB[t][:], col(E.con, CONST_AT, "ones"), sq[:, e, :], start=(e == 0),
                                   stop=(e == 1)).then_inc(ss_done, 1)


def chunk_order(d, nx, nctx):
    if d == 0:
        return [nx + c for c in range(nctx)] + list(range(nx))
    return [nx + c for c in reversed(range(nctx))] + list(reversed(range(nx)))


def branch_phase(nc, E, dram, hi, lo):
    with ExitStack() as ctx:
        sb, ps, sem = phase(nc, ctx)
        a = sb("pool_in", [P, META + L2])
        win = sb("pool_sums", [P, 4, META + L2])
        diff = sb("pool_diff", [P, L2])
        pw = sb("pool_w", [P, 2, P])
        y = sb("conv_y", [P, 2, L2])
        u = sb("branch", [P, L2])
        stat, t0 = sb("ln_mean", [P, L2]), sb("ln_sq", [P, 2, L2])
        acc = ps("pool_acc", [P, 3, 512])
        acc2 = ps("ln_acc", [P, 3, 512])
        (pin, cin, win_ready, pe_done, u_ready, hi_done, a_used, sq_ready, mean_done,
         var_done, steps, silu_done) = (sem(n) for n in (
             "pool_loaded", "conv_loaded", "diff_ready", "pool_done", "branch_ready", "branch_hi", "pool_used",
             "sq_ready", "mean_done", "var_done", "dve_steps", "silu_done"))
        ms_ready, root_ready = sem("mean_square_ready"), sem("root_ready")
        load_exp_ln(nc)
        block = ctx.enter_context(nc.Block())

        @block.sync
        def _(eng):
            eng.dma_start(pw[:], dram["pool_w"]).then_inc(pin, 16)
            eng.dma_start(a[:, META:], dram["p2"][0]).then_inc(pin, 16)
            for j in range(2):
                eng.dma_start(y[:, j, :], dram["conv"][j]).then_inc(cin, 16)
            eng.wait_ge(win_ready, 1)
            eng.dma_start(a[:, META:], dram["p2"][1]).then_inc(a_used, 16)

        @block.scalar
        def _(eng):
            for j in range(2):
                eng.wait_ge(u_ready, j + 1)
                eng.activation(hi[:, j, :], u[:], ACT.Copy).then_inc(hi_done, 1)
            eng.wait_ge(var_done, 1)
            for t, (off, n) in enumerate(TILES2):
                ln = eng.activation(stat[:, off:off + n], acc2[:, t, 0:n], ACT.Ln, scale=1.0 / 256, bias=E.eps[:])
            ln.then_inc(ms_ready, 1)
            eng.wait_ge(ms_ready, 1)
            eng.activation(stat[:], stat[:], ACT.Exp, scale=-0.5).then_inc(root_ready, 1)
            for j in range(2):
                eng.wait_ge(u_ready, j + 3)
                eng.activation(u[:], t0[:, j, :], ACT.Silu).then_inc(silu_done, 1)
                eng.wait_ge(silu_done, j + 1)
                eng.activation(hi[:, 2 + j, :], u[:], ACT.Copy).then_inc(hi_done, 1)

        @block.tensor
        def _(eng):
            eng.wait_ge(pin, 32)
            for j in range(2):
                eng.wait_ge(win_ready, j + 1)
                if j:
                    eng.wait_ge(u_ready, 1)
                for t, (off, n) in enumerate(TILES2):
                    mm = eng.matmul(acc[:, t, 0:n], pw[:, j, :], diff[:, off:off + n], start=True, stop=True)
                mm.then_inc(pe_done, 1)
            ones = col(E.con, CONST_AT, "ones")
            eng.wait_ge(cin, 32)
            for t, (off, n) in enumerate(TILES2):
                for j in range(2):
                    mm = eng.matmul(acc2[:, t, 0:n], ones, y[:, j, off:off + n], start=(j == 0), stop=(j == 1))
            mm.then_inc(mean_done, 1)
            eng.wait_ge(sq_ready, 1)
            for t, (off, n) in enumerate(TILES2):
                for j in range(2):
                    mm = eng.matmul(acc2[:, t, 0:n], ones, t0[:, j, off:off + n], start=(j == 0), stop=(j == 1))
            mm.then_inc(var_done, 1)

        @block.vector
        def _(eng):
            chain = Chain(eng, steps)
            eng.memset(a[:, 0:META], 0.0)
            chain(eng.memset(win[:, :, 0:META], 0.0))
            inv = col(E.con, CONST_AT, "invcnt")
            for j in range(2):
                if j == 0:
                    eng.wait_ge(pin, 32)
                else:
                    eng.wait_ge(a_used, 16)
                prev = a[:, :]
                for g in range(2 * j + 2):
                    sh = 1 << g
                    chain(eng.tensor_tensor(win[:, g, META:], prev[:, META:], prev[:, META - sh:META + L2 - sh], ALU.add))
                    prev = win[:, g, :]
                if j:
                    eng.wait_ge(pe_done, 1)
                for half in range(2):
                    g = 2 * j + half
                    rows = slice(64 * half, 64 * half + 64)
                    chain(eng.scalar_tensor_tensor(diff[rows, :], win[rows, g, META:], 1.0 / 2 ** (g + 1),
                                                   a[rows, META:], ALU.mult, ALU.subtract))
                    chain(eng.tensor_tensor(diff[rows, 0:META], win[rows, g, META:2 * META],
                                            inv[rows, META * j:META * j + META], ALU.mult))
                    chain(eng.tensor_tensor(diff[rows, 0:META], diff[rows, 0:META], a[rows, META:2 * META], ALU.subtract))
                eng.engine_nop().then_inc(win_ready, 1)
                eng.wait_ge(pe_done, j + 1)
                for t, (off, n) in enumerate(TILES2):
                    chain(eng.tensor_scalar(u[:, off:off + n], acc[:, t, 0:n], col(E.par, PARAM_AT, "pool_b", j),
                                            col(E.par, PARAM_AT, "pool_scale", j), ALU.add, ALU.mult))
                eng.engine_nop().then_inc(u_ready, 1)
                eng.wait_ge(hi_done, j + 1)
                chain(eng.tensor_tensor(lo[:, j, :], u[:], hi[:, j, :].bitcast(F32), ALU.subtract))
            eng.wait_ge(mean_done, 1)
            for t, (off, n) in enumerate(TILES2):
                chain(eng.tensor_scalar(stat[:, off:off + n], acc2[:, t, 0:n], 1.0 / 256, None, ALU.mult))
            for j in range(2):
                chain(eng.tensor_tensor(y[:, j, :], y[:, j, :], stat[:], ALU.subtract))
                chain(eng.tensor_tensor(t0[:, j, :], y[:, j, :], y[:, j, :], ALU.mult))
            eng.engine_nop().then_inc(sq_ready, 1)
            eng.wait_ge(root_ready, 1)
            for j in range(2):
                chain(eng.scalar_tensor_tensor(t0[:, j, :], y[:, j, :], col(E.par, PARAM_AT, "conv_g", j), stat[:],
                                               ALU.mult, ALU.mult))
                chain(eng.tensor_scalar(t0[:, j, :], t0[:, j, :], col(E.par, PARAM_AT, "conv_lb", j), None, ALU.add))
                eng.engine_nop().then_inc(u_ready, 1)
                eng.wait_ge(hi_done, 3 + j)
                chain(eng.tensor_tensor(lo[:, 2 + j, :], u[:], hi[:, 2 + j, :].bitcast(F32), ALU.subtract))


def router_phase(nc, E, dram, hi, lo, wts):
    NG = 4
    starts = [P * i for i in range(L2 // P)] + [L2 - P]
    NTL = len(starts)
    with ExitStack() as ctx:
        sb, ps, sem = phase(nc, ctx)
        NL = 20
        w = sb("router_w", [P, KD * P])
        wh, wl = sb("router_hi", [P, KD * P], F32R), sb("router_lo", [P, KD * P], F32R)
        zt = sb("logits_t", [NL, L2])
        lg = sb("logits", [P, NTL, 20])
        s1, s2, t4, ex = (sb(n, [P, NTL, 4]) for n in ("sel1", "sel2", "tmp4", "ex"))
        gs = sb("gsel", [P, NTL, 4])
        m, rem, sm, gw, v1, v2 = (sb(n, [P, NTL]) for n in ("m", "rem", "sm", "gw", "v1", "v2"))
        cm = sb("comb", [P, NTL, 16])
        ct = sb("comb_t", [16, L2])
        pz = ps("logits_t_p", [P, 3, 512])
        pl = ps("logits_p", [P, NTL, 20])
        pt = ps("comb_p", [16, 3, 512])
        loaded, wlo_d, mm, step, x_in, x_out, comb_d, t_d, ct_d, out_d = (sem(n) for n in (
            "loaded", "w_lo", "logits_done", "dve_steps", "exp_in", "exp_out", "comb_ready", "t_done",
            "ct_ready", "stored"))
        z_done, z_copied = sem("logits_t_done"), sem("logits_t_copied")
        wts.sems(sem)
        block = ctx.enter_context(nc.Block())

        @block.sync
        def _(eng):
            eng.dma_start(w[:], dram["router_w"]).then_inc(loaded, 16)
            wts.first_loads(eng)
            eng.wait_ge(ct_d, 1)
            eng.dma_start(dram["comb"], ct[:]).then_inc(out_d, 16)
            eng.wait_ge(out_d, 16)

        @block.tensor
        def _(eng):
            eng.wait_ge(wlo_d, 1)
            for k in range(KD):
                for x, y in ((wh, hi), (wh, lo), (wl, hi)):
                    for t, (off, n) in enumerate(TILES2):
                        ins = eng.matmul(pz[:, t, 0:n], x[:, k * P:(k + 1) * P], y[:, k, off:off + n],
                                         start=(k == 0 and x is wh and y is hi), stop=(k == KD - 1 and x is wl))
            ins.then_inc(z_done, 1)
            eng.wait_ge(z_copied, 1)
            for t, off in enumerate(starts):
                ins = eng.transpose(pl[:, t, :], zt[:, off:off + P], col(E.con, CONST_AT, "ident")[0:NL, 0:NL])
            ins.then_inc(mm, 1)
            eng.wait_ge(comb_d, 1)
            for t in range(NTL):
                ins = eng.transpose(pt[:, t // 4, (t % 4) * P:(t % 4 + 1) * P], cm[:, t, :], col(E.con, CONST_AT, "ident"))
            ins.then_inc(t_d, 1)

        @block.scalar
        def _(eng):
            wts.first_hi(eng)
            eng.wait_ge(z_done, 1)
            for t, (off, n) in enumerate(TILES2):
                ins = eng.activation(zt[:, off:off + n], pz[0:NL, t, 0:n], ACT.Copy)
            ins.then_inc(z_copied, 1)
            eng.wait_ge(x_in, 1)
            eng.activation(ex[:], t4[:], ACT.Exp).then_inc(x_out, 1)
            eng.wait_ge(x_in, 2)
            eng.activation(ex[:], t4[:], ACT.Exp).then_inc(x_out, 1)

        @block.vector
        def _(eng):
            chain = Chain(eng, step)

            def b4(x):
                return x[:].unsqueeze(2).to_broadcast([P, NTL, 4])

            def first_max(sel, val, src):
                chain(eng.tensor_reduce(val[:], src, AX, ALU.max))
                chain(eng.tensor_tensor(sel[:], src, b4(val), ALU.is_ge))
                chain(eng.memset(rem[:], 1.0))
                for j in range(4):
                    chain(eng.tensor_tensor(sel[:, :, j], sel[:, :, j], rem[:], ALU.mult))
                    chain(eng.tensor_tensor(rem[:], rem[:], sel[:, :, j], ALU.subtract))

            eng.wait_ge(loaded, 16)
            chain(eng.tensor_copy(wh[:], w[:]))
            eng.tensor_tensor(wl[:], w[:], wh[:].bitcast(F32), ALU.subtract).then_inc(wlo_d, 1)
            wts.first_lo(eng)
            eng.wait_ge(mm, 1)
            bias = col(E.par, PARAM_AT, "rbias").unsqueeze(1).to_broadcast([P, NTL, 20])
            chain(eng.tensor_tensor(lg[:], pl[:], bias, ALU.add))
            g = lg[:, :, 0:4]
            first_max(gs, m, g)
            chain(eng.tensor_tensor(t4[:], g, b4(m), ALU.subtract))
            eng.engine_nop().then_inc(x_in, 1)
            eng.wait_ge(x_out, 1)
            chain(eng.tensor_reduce(gw[:], ex[:], AX, ALU.add))
            chain(eng.reciprocal(gw[:], gw[:]))
            for j in range(NG):
                e = lg[:, :, 4 + 4 * j:8 + 4 * j]
                one = gs[:, :, j].unsqueeze(2).to_broadcast([P, NTL, 4])
                if j == 0:
                    chain(eng.tensor_tensor(s2[:], e, one, ALU.mult))
                else:
                    chain(eng.tensor_tensor(t4[:], e, one, ALU.mult))
                    chain(eng.tensor_tensor(s2[:], s2[:], t4[:], ALU.add))
            chain(eng.tensor_reduce(m[:], s2[:], AX, ALU.max))
            chain(eng.tensor_tensor(t4[:], s2[:], b4(m), ALU.subtract))
            eng.engine_nop().then_inc(x_in, 1)
            eng.wait_ge(x_out, 2)
            chain(eng.tensor_reduce(sm[:], ex[:], AX, ALU.add))
            chain(eng.reciprocal(sm[:], sm[:]))
            chain(eng.tensor_tensor(ex[:], ex[:], b4(sm), ALU.mult))
            first_max(s1, v1, ex[:])
            chain(eng.scalar_tensor_tensor(t4[:], s1[:], -2.0, ex[:], ALU.mult, ALU.add))
            first_max(s2, v2, t4[:])
            chain(eng.tensor_tensor(sm[:], v1[:], v2[:], ALU.add))
            chain(eng.reciprocal(sm[:], sm[:]))
            chain(eng.tensor_tensor(sm[:], sm[:], gw[:], ALU.mult))
            chain(eng.tensor_tensor(s1[:], s1[:], b4(v1), ALU.mult))
            chain(eng.tensor_tensor(s2[:], s2[:], b4(v2), ALU.mult))
            chain(eng.tensor_tensor(s1[:], s1[:], s2[:], ALU.add))
            chain(eng.tensor_tensor(s1[:], s1[:], b4(sm), ALU.mult))
            for j in range(NG):
                one = gs[:, :, j].unsqueeze(2).to_broadcast([P, NTL, 4])
                chain(eng.tensor_tensor(cm[:, :, 4 * j:4 * j + 4], s1[:], one, ALU.mult))
            eng.engine_nop().then_inc(comb_d, 1)
            eng.wait_ge(t_d, 1)
            chain(eng.tensor_copy(ct[:, 0:1024], pt[:, 0:2, :].rearrange("p b n -> p (b n)")))
            tail = L2 - 1024
            chain(eng.tensor_copy(ct[:, 1024:L2], pt[:, 2, P - tail:P]))
            eng.engine_nop().then_inc(ct_d, 1)


def build(nc, d):
    TAGS.update(n=0, used=[])
    with ExitStack() as ctx:
        def sb(name, shape, dt=F32):
            return ctx.enter_context(nc.sbuf_tensor(name, shape, dt))

        E = Shared(nc, sb, d["tables"])
        with ExitStack() as c2:
            E.mask32 = c2.enter_context(nc.sbuf_tensor("mask32", [P, 5 * P], F32))
            setup_phase(nc, E, d)

        def split_tiles(c, width):
            return [c.enter_context(nc.sbuf_tensor(f"act_{n}_{nc_tag(nc)}", [P, KD, width], F32R)) for n in ("hi", "lo")]

        def scratch(name, shape, dt=F32):
            return nc.dram_tensor(name, shape, dt, kind="Internal").ap()

        XT = TILES1[:2]
        P1 = scratch("proj1", (26, P, NT1))
        O1 = scratch("mixed1", (8, P, NT1))
        P2 = scratch("proj2", (25, P, NT1))
        O2 = scratch("mixed2", (8, P, T))
        P3 = scratch("proj3", (18, P, L2))
        G3 = scratch("gates3", (24, P, L2))
        O3 = scratch("fox3", (4, P, L2))
        FR = scratch("decay_rows", (8, 6, L2), F32R)
        CB = scratch("comb", (16, L2))
        CY = scratch("conv3", (2, P, L2))

        def modulated(layer, hi, lo, wts):
            norm_phase(nc, E, lambda k, off, n: E.X[:, k, X0 + off:X0 + off + n], TILES1,
                       lambda k, t: E.gain[:, layer, 2 * k + (t == 2):2 * k + (t == 2) + 1],
                       lambda k, t: E.mod[:, layer, 2 * k + (t == 2):2 * k + (t == 2) + 1], hi, lo, wts=wts)

        def out_proj(layer, o, tiles):
            with ExitStack() as c:
                hi, lo = split_tiles(c, NT1)
                width = tiles[-1][0] + tiles[-1][1]
                wts = Weights(nc, c, d["w_out"][layer])
                split_phase(nc, lambda ch: o[ch], KD, width, hi, lo, wts)
                gemm_phase(nc, E, wts, [
                    Job(f, 0, KD, (hi, lo, 0), tiles, "resid", f=f,
                        gate_of=lambda t, f=f: E.mod[:, layer, 32 + 2 * f + (t == 2):32 + 2 * f + (t == 2) + 1])
                    for f in range(KD)])

        par = lambda name, j=None: col(E.par, PARAM_AT, name, j)
        with ExitStack() as c:
            hi, lo = split_tiles(c, NT1)
            order = [*range(5), *range(10, 18), 5, *range(18, 22), *range(6, 10), *range(22, 26)]
            wts = Weights(nc, c, [d["ab_w_in"][f] for f in order])
            modulated(0, hi, lo, wts)
            kind = {}
            for f in range(26):
                if f < 4: kind[f] = ("rope", dict(gain=par("a_qn")))
                elif f == 4: kind[f] = ("rope", dict(gain=par("a_kn")))
                elif 10 <= f < 14: kind[f] = ("rope", dict(gain=par("b_qn")))
                elif 14 <= f < 18: kind[f] = ("rope", dict(gain=par("b_kn")))
                elif f == 5 or 18 <= f < 22: kind[f] = ("store", dict(func=ACT.Copy))
                else: kind[f] = ("store", dict(func=ACT.Silu))
            gemm_phase(nc, E, wts,
                       [Job(n, 0, KD, (hi, lo, 0), TILES1, kind[f][0], out=P1[f], **kind[f][1])
                        for n, f in enumerate(order)], adaln=dict(w=d["adaln_w1"], cond=d["cond"]))

        def qblocks(i, band):
            ctxb = [(T, P), (T + P, P)]
            if i >= 8:
                return ctxb, {}
            if not band:
                return [(P * b, P) for b in range(10)], {}
            bl = [b for b in (i - 1, i, i + 1) if 0 <= b < 8]
            masks = {n: ((P, P) if b < i else (3 * P, P)) for n, b in enumerate(bl) if b != i}
            return [(P * b, P) for b in bl] + ctxb, masks

        chunks = []
        for c in range(4):
            g = c // 2
            chunks.append(Chunk([P1[c][64 * a:64 * a + 64] for a in range(2)], [P1[4][64 * g:64 * g + 64]] * 2, P1[5],
                                P1[6 + c], O1[c], [Unit(a, P * i, *qblocks(i, True)) for i in range(10) for a in range(2)],
                                sinks=[2 * c, 2 * c + 1], vcols=[64 * g] * 2))
        attention_phase(nc, E, NT1, chunks, "sink")
        chunks = [Chunk([P1[10 + c][64 * a:64 * a + 64] for a in range(2)], [P1[14 + c][64 * a:64 * a + 64] for a in range(2)],
                        P1[18 + c], P1[22 + c], O1[4 + c], [Unit(0, P * i, *qblocks(i, False)) for i in range(10)])
                  for c in range(4)]
        attention_phase(nc, E, NT1, chunks, "diff")
        out_proj(0, O1, TILES1)

        with ExitStack() as c:
            hi, lo = split_tiles(c, NT1)
            wts = Weights(nc, c, d["gla_w_in"])
            modulated(1, hi, lo, wts)
            jobs = []
            for f in range(25):
                jobs.append(Job(f, 0, KD, (hi, lo, 0), XT if f < 4 or 16 <= f < 24 else TILES1, "store",
                                func=ACT.Silu if 16 <= f < 24 else ACT.Copy, out=P2[f]))
            gemm_phase(nc, E, wts, jobs)
        gla_phase(nc, E, dict(
            reset=d["reset"], rank=P2[24], wa_f=d["wa_f"], wa_b=d["wa_b"], q=lambda h: P2[h][:, 0:T], k=lambda h: P2[4 + h],
            v=lambda h: P2[8 + 2 * h:10 + 2 * h].rearrange("e p n -> p e n"),
            gate=lambda h: P2[16 + 2 * h:18 + 2 * h, :, 0:T].rearrange("e p n -> p e n"),
            out=lambda h: O2[2 * h:2 * h + 2].rearrange("e p n -> p e n")))
        out_proj(1, O2, XT)

        with ExitStack() as c:
            hi, lo = split_tiles(c, L2)
            order = [18, 0, 1, 2, 3, *range(6, 18), 4, 5, *range(19, 43)]
            wts = Weights(nc, c, [d["w_in"][f] for f in order])
            norm_phase(nc, E, lambda k, off, n: E.X[:, k, off:off + n], TILES2, lambda k, t: par("norm1", k),
                       lambda k, t: None, hi, lo, wts=wts)
            jobs = []
            for n, f in enumerate(order):
                if f == 18:
                    jobs.append(Job(n, 0, KD, (hi, lo, 0), TILES2, "decay"))
                    continue
                out = P3[f] if f < 19 else G3[f - 19]
                func = ACT.Sigmoid if f in (4, 5) or f >= 19 else ACT.Copy
                jobs.append(Job(n, 0, KD, (hi, lo, 0), TILES2, "store", func=func, out=out))
            gemm_phase(nc, E, wts, jobs, decay_rows=FR)
        units = []
        for i in range(9):
            q0 = P * i if i < 8 else L2 - P
            blocks = [(P * b, P) for b in range(min(i + 1, 8))] + ([(T, META)] if i == 8 else [])
            masks = {i: (3 * P, P)} if i < 8 else {7: (3 * P - 16, P), 8: (3 * P + 112, META)}
            units += [Unit(a, q0, blocks, masks) for a in range(2)]
        chunks = [Chunk([P3[6 + c][64 * a:64 * a + 64] for a in range(2)], [P3[10 + c][64 * a:64 * a + 64] for a in range(2)],
                        P3[14 + c], None, O3[c], units, vcols=[0, 64],
                        frow=[[FR[2 * c + a, 2 * j:2 * j + 2] for j in range(3)] for a in range(2)]) for c in range(4)]
        attention_phase(nc, E, L2, chunks, "fox", conv=dict(p=P3, out=CY))
        with ExitStack() as c:
            hi, lo = split_tiles(c, L2)
            branch_phase(nc, E, dict(pool_w=d["pool_w"], p2=P3, conv=CY), hi, lo)
            mhi, mlo = split_tiles(c, L2)
            wts = Weights(nc, c, [d["w_abc"][f] for f in range(KD)] + [d["w_o"][f] for f in range(KD)], ring=2)
            split_phase(nc, lambda ch: O3[ch], 4, L2, hi[:, 4:8, :], lo[:, 4:8, :], wts, ring=3)
            jobs = []
            for f in range(KD):
                for b, (k0, k1) in enumerate(((0, 2), (2, 4), (4, 8))):
                    jobs.append(Job(f, k0, k1, (hi, lo, k0), TILES2, "gate", f=f, first=b == 0, last=b == 2,
                                    gates=G3[8 * b + f], hi=mhi, lo=mlo))
            jobs += [Job(KD + f, 0, KD, (mhi, mlo, 0), TILES2, "add", f=f, merged=f == 0) for f in range(KD)]
            gemm_phase(nc, E, wts, jobs)
        with ExitStack() as c:
            hi, lo = split_tiles(c, L2)
            norm_phase(nc, E, lambda k, off, n: E.X[:, k, off:off + n], TILES2, lambda k, t: par("norm2", k),
                       lambda k, t: None, hi, lo)
            hhi, hlo = (c.enter_context(nc.sbuf_tensor(f"hidden_{n}", [P, 4, L2], F32R)) for n in ("hi", "lo"))
            jobs, last_down = [], {}

            def up(e, ch):
                slot = 2 * (e % 2) + ch
                jobs.append(Job(4 * e + 2 * ch, 0, KD, (hi, lo, 0), TILES2, "up"))
                jobs.append(Job(4 * e + 2 * ch + 1, 0, KD, (hi, lo, 0), TILES2, "he", slot=slot, reuse=last_down.get(e - 2)))

            def down(e):
                for f in range(KD):
                    jobs.append(Job(("down", e, f // 4), 2 * (f % 4), 2 * (f % 4) + 2, (hhi, hlo, 2 * (e % 2)), TILES2,
                                    "down", f=f, needs=6 * (e + 1)))
                last_down[e] = len(jobs) - 1

            for e in range(NE + 1):
                if e < NE:
                    up(e, 0)
                    up(e, 1)
                if e >= 1:
                    down(e - 1)
            tiles, number = [], {}
            for j in jobs:
                if j.w not in number:
                    number[j.w] = len(tiles)
                    tiles.append(d["exp_down"][j.w[1], j.w[2]] if isinstance(j.w, tuple) else d["exp_up"][j.w])
                j.w = number[j.w]
            wts = Weights(nc, c, tiles)
            router_phase(nc, E, dict(router_w=d["router_w"], comb=CB), hi, lo, wts)
            gemm_phase(nc, E, wts, jobs, comb=dict(hhi=hhi, hlo=hlo, dram=CB))
        with ExitStack() as c:
            out = c.enter_context(nc.sbuf_tensor("y", [P, KD, T], F32))
            norm_phase(nc, E, lambda k, off, n: E.X[:, k, META + off:META + off + n], TILES1[:2],
                       lambda k, t: par("final_g", k), lambda k, t: None, None, None, out=out, out_dram=d["y"])


def tiles_of(w):
    k, n = w.shape
    pad = -n % P
    if pad:
        w = np.concatenate([w, np.zeros((k, pad), w.dtype)], 1)
    return np.ascontiguousarray(w.reshape(k // P, P, (n + pad) // P, P).transpose(2, 1, 0, 3)).reshape(-1, P, k)


def by_chunk(vec):
    return vec.reshape(-1, P).T


def rows_of(vec):
    return np.broadcast_to(vec.reshape(1, -1), (P, vec.size))


def layout(i):
    f = {k: np.asarray(v) for k, v in i.items()}
    par = {
        "cond": np.stack([by_chunk(f["c"][0]), by_chunk(f["c_ctx"])], 2).reshape(P, 16),
        "adaln_b": np.concatenate([by_chunk(f["adaln_b"][l]) for l in range(2)], 1),
        "norm_g": np.concatenate([by_chunk(f["norm_g"][l]) for l in range(2)], 1),
        "a_qn": np.tile(f["a_q_norm"][0], 2)[:, None], "a_kn": np.tile(f["a_k_norm"][0], 2)[:, None],
        "sink": rows_of(f["a_sink"][0]),
        "b_qn": np.tile(f["b_q_norm"][0], 2)[:, None], "b_kn": np.tile(f["b_k_norm"][0], 2)[:, None],
        "lq1": rows_of(f["b_lambda_q1"][0]), "lk1": rows_of(f["b_lambda_k1"][0]),
        "lq2": rows_of(f["b_lambda_q2"][0]), "lk2": rows_of(f["b_lambda_k2"][0]),
        "subln": f["b_subln"][0][:, None],
        "ba": np.concatenate([by_chunk(f["gla_ba_f"][0]), by_chunk(f["gla_ba_b"][0])], 1),
        "out_norm": by_chunk(f["gla_out_norm"][0]),
        "norm1": by_chunk(f["norm1_g_2"][0]),
        "bforget": np.concatenate([f["b_forget_2"][0], np.zeros(P - 8, np.float32)])[:, None],
        "pool_b": by_chunk(f["pool_b_2"][0].reshape(-1)), "pool_scale": by_chunk(f["pool_scale_2"][0]),
        "conv_w": f["conv_w_2"][0].T.reshape(2, P, 31).transpose(1, 0, 2).reshape(P, 62),
        "conv_b": by_chunk(f["conv_b_2"][0]), "conv_g": by_chunk(f["conv_ln_g_2"][0]),
        "conv_lb": by_chunk(f["conv_ln_b_2"][0]),
        "norm2": by_chunk(f["norm2_g_2"][0]),
        "rbias": rows_of(np.concatenate([f["router_g_b_2"][0], f["router_e_b_2"][0]])),
        "final_g": by_chunk(f["final_g_2"]),
    }
    con = shape_constants()
    pw = np.zeros((P, 2, P), np.float32)
    for g in range(4):
        r = slice(64 * (g % 2), 64 * (g % 2) + 64)
        pw[r, g // 2, r] = f["pool_w_2"][0, g]
    w_in = f["w_in_2"][0]
    c0 = 3 * 256 + 3 * 512
    x = np.concatenate([f["x"][0], f["ctx"][0]], 0).T.reshape(KD, P, NT1).transpose(1, 0, 2)
    down = f["exp_w2_2"][0].reshape(NE, 2, P, 2, 4, P)
    arrays = dict(
        params=np.concatenate([par[n] for n, _ in PARAM_WIDTHS], 1),
        consts=np.concatenate([con[n] for n, _ in CONST_WIDTHS], 1).astype(np.float32),
        masks=mask_constants().astype(np.float32),
        tables=np.stack([con["cos"], con["sin"]], 1).astype(np.float32),
        reset=con["reset"].astype(np.float32),
        x0=x, meta=f["meta_2"].T.reshape(KD, P, META).transpose(1, 0, 2),
        adaln_w0=f["adaln_w"][0].reshape(KD, P, 3 * D), adaln_w1=f["adaln_w"][1].T.reshape(3 * KD, P, D),
        cond=np.stack([f["c"][0], f["c_ctx"]]),
        ab_w_in=tiles_of(f["ab_w_in"][0]),
        w_out=np.stack([tiles_of(f["w_out"][l]) for l in range(2)]),
        gla_w_in=tiles_of(f["gla_w_in"][0]),
        wa_f=f["gla_wa_f"][0], wa_b=f["gla_wa_b"][0],
        w_in=np.concatenate([tiles_of(w_in[:, :c0 + 8]), tiles_of(w_in[:, c0 + 8:])], 0),
        pool_w=pw,
        w_abc=tiles_of(np.concatenate([f["w_out_a_2"][0], f["w_out_b_2"][0], f["w_out_c_2"][0]], 0)),
        w_o=tiles_of(f["w_o_2"][0]),
        router_w=tiles_of(np.concatenate([f["router_g_2"][0], f["router_e_2"][0]], 1))[0],
        exp_up=np.stack([tiles_of(f["exp_w1_2"][0, e]) if j == 0 else tiles_of(f["exp_w3_2"][0, e])
                         for e in range(NE) for j in range(2)], 0).reshape(NE, 2, 2, P, D)
                 .transpose(0, 2, 1, 3, 4).reshape(4 * NE, P, D),
        exp_down=down.transpose(0, 3, 2, 4, 1, 5).reshape(NE, 2, P, 8 * P),
    )
    return {k: np.ascontiguousarray(v) for k, v in arrays.items()}


def kernel(**inputs):
    import numpy as _np
    import concourse.bacc as _bacc
    from concourse import mybir as _mybir
    from concourse.bass_utils import run_bass_kernel_spmd as _run

    arrays = layout(inputs)
    nc = _bacc.Bacc("TRN2", target_bir_lowering=False, num_devices=1)
    d = {n: nc.dram_tensor(f"in_{n}", a.shape, F32, kind="ExternalInput").ap() for n, a in arrays.items()}
    d["y"] = nc.dram_tensor("y_dram", (P, KD, T), F32, kind="ExternalOutput").ap()
    build(nc, d)
    r = _run(nc, [{f"in_{n}": a for n, a in arrays.items()}], core_ids=[0])
    y = r.results[0]["y_dram"]
    return _np.ascontiguousarray(y.transpose(2, 1, 0)).reshape(1, T, D)
```
